# Optimizing a Trainium2 kernel written in Bass

```python
import jax, jax.numpy as jnp
from jax import lax
import numpy as np
import math

D_MODEL = 1024
BATCH = 1
SEQ = 512
DEPTH = 1

MIX_W = D_MODEL
HEAD_DIM = 64
ATTN_W = MIX_W // 2
N_ATTN_HEADS = ATTN_W // HEAD_DIM
N_KV_HEADS = 2
KV_W = N_KV_HEADS * HEAD_DIM
WINDOW = 128
BLOCK = 128
RET_W = MIX_W - ATTN_W
N_RET_HEADS = 4
RET_HEAD_DIM = RET_W // N_RET_HEADS
RET_CHUNK = 128
IN_W = ATTN_W + 2 * KV_W + 4 * RET_W
D_FF = 2816
CONV_WIDTH = 3
RMS_EPS = 1e-6
GN_EPS = 1e-6
MASK_VALUE = -1e30


def rms_norm(x, w):
    xf = x.astype(jnp.float32)
    y = xf * lax.rsqrt(jnp.mean(xf * xf, axis=-1, keepdims=True) + RMS_EPS)
    return (y * w.astype(jnp.float32)).astype(x.dtype)

def sliding_window_sink_attention(q, k, v, sinks):
    b, s, _ = q.shape
    nb = s // BLOCK
    g = N_ATTN_HEADS // N_KV_HEADS
    qb = q.reshape(b, nb, BLOCK, N_KV_HEADS, g, HEAD_DIM)
    kb = k.reshape(b, nb, BLOCK, N_KV_HEADS, HEAD_DIM)
    vb = v.reshape(b, nb, BLOCK, N_KV_HEADS, HEAD_DIM)
    pad = ((0, 0), (1, 0), (0, 0), (0, 0), (0, 0))
    kk = jnp.concatenate([jnp.pad(kb, pad)[:, :-1], kb], axis=2)
    vv = jnp.concatenate([jnp.pad(vb, pad)[:, :-1], vb], axis=2)
    scores = jnp.einsum('bnqhgd,bnkhd->bnhgqk', qb, kk).astype(jnp.float32) * (HEAD_DIM ** -0.5)
    qpos = jnp.arange(BLOCK)[:, None] + BLOCK
    kpos = jnp.arange(2 * BLOCK)[None, :]
    rel = qpos - kpos
    band = (rel >= 0) & (rel < WINDOW)
    not_pad = (jnp.arange(nb)[:, None, None] > 0) | (kpos >= BLOCK)[None]
    valid = band[None] & not_pad
    scores = jnp.where(valid[None, :, None, None], scores, MASK_VALUE)
    sink = jnp.broadcast_to(
        sinks.astype(jnp.float32).reshape(N_KV_HEADS, g)[None, None, :, :, None, None],
        scores.shape[:-1] + (1,))
    probs = jax.nn.softmax(jnp.concatenate([scores, sink], axis=-1), axis=-1)[..., :-1]
    out = jnp.einsum('bnhgqk,bnkhd->bnqhgd', probs.astype(vv.dtype), vv)
    return out.reshape(b, s, ATTN_W)

def rotate_every_two(x):
    x1 = x[..., ::2]
    x2 = x[..., 1::2]
    return jnp.stack([-x2, x1], axis=-1).reshape(x.shape)

def retention_chunkwise(q, k, v):
    b, s, h, dk = q.shape
    dv = v.shape[-1]
    nc = s // RET_CHUNK
    c = RET_CHUNK
    log_gamma = jnp.log(1.0 - jnp.power(2.0, -5.0 - jnp.arange(h, dtype=jnp.float32)))
    idx = jnp.arange(c, dtype=jnp.float32)
    rel = idx[:, None] - idx[None, :]
    d_intra = jnp.where(rel[None] >= 0,
                        jnp.exp(log_gamma[:, None, None] * jnp.maximum(rel, 0.0)[None]), 0.0)
    xi = jnp.exp(log_gamma[None, :] * (idx[:, None] + 1.0))
    zeta = jnp.exp(log_gamma[None, :] * (c - 1.0 - idx[:, None]))
    chunk_decay = jnp.exp(log_gamma * c)
    qc = q.reshape(b, nc, c, h, dk)
    kc = k.reshape(b, nc, c, h, dk)
    vc = v.reshape(b, nc, c, h, dv)
    inner = jnp.einsum('bnqhd,bnkhd->bnhqk', qc, kc) * d_intra[None, None]
    o_inner = jnp.einsum('bnhqk,bnkhe->bnqhe', inner, vc)
    kv_chunk = jnp.einsum('bnkhd,kh,bnkhe->bnhde', kc, zeta, vc)

    def step(state, kv):
        return chunk_decay[None, :, None, None] * state + kv, state

    _, prev = lax.scan(step, jnp.zeros((b, h, dk, dv), jnp.float32), jnp.moveaxis(kv_chunk, 1, 0))
    prev = jnp.moveaxis(prev, 0, 1)
    o_cross = jnp.einsum('bnqhd,bnhde->bnqhe', qc, prev) * xi[None, None, :, :, None]
    return (o_inner + o_cross).reshape(b, s, h, dv)

def retention_group(q, k, v, gate):
    b, s, _ = q.shape
    dtype = q.dtype
    pos = jnp.arange(s, dtype=jnp.float32)
    angle = 1.0 / jnp.power(10000.0, jnp.linspace(0.0, 1.0, RET_HEAD_DIM // 2, dtype=jnp.float32))
    angle = jnp.repeat(angle, 2)
    sin = jnp.sin(pos[:, None] * angle[None])[None, :, None, :]
    cos = jnp.cos(pos[:, None] * angle[None])[None, :, None, :]
    qf = q.astype(jnp.float32).reshape(b, s, N_RET_HEADS, RET_HEAD_DIM)
    kf = k.astype(jnp.float32).reshape(b, s, N_RET_HEADS, RET_HEAD_DIM) * (RET_HEAD_DIM ** -0.5)
    vf = v.astype(jnp.float32).reshape(b, s, N_RET_HEADS, RET_HEAD_DIM)
    qf = qf * cos + rotate_every_two(qf) * sin
    kf = kf * cos + rotate_every_two(kf) * sin
    o = retention_chunkwise(qf, kf, vf)
    mu = jnp.mean(o, axis=-1, keepdims=True)
    var = jnp.mean(jnp.square(o - mu), axis=-1, keepdims=True)
    o = ((o - mu) * lax.rsqrt(var + GN_EPS)).reshape(b, s, RET_W)
    return (jax.nn.silu(gate.astype(jnp.float32)) * o).astype(dtype)

def causal_depthwise_conv(u, w, bias):
    ch = u.shape[-1]
    y = lax.conv_general_dilated(u, w[:, None, :].astype(u.dtype), window_strides=(1,),
                                 padding=[(CONV_WIDTH - 1, 0)],
                                 dimension_numbers=('NWC', 'WIO', 'NWC'),
                                 feature_group_count=ch)
    return y + bias.astype(u.dtype)

def first_inputs(seed: int = 0) -> dict:
    key = jax.random.key(seed)
    ks = jax.random.split(key, 13)
    f32 = jnp.float32

    def gain(k):
        return 1.0 + 0.02 * jax.random.normal(k, (DEPTH, D_MODEL), f32)

    return {
        "x": jax.random.normal(ks[0], (BATCH, SEQ, D_MODEL), f32),
        "mix_pre_norm": gain(ks[1]),
        "w_in": jax.random.normal(ks[2], (DEPTH, D_MODEL, IN_W), f32) * D_MODEL ** -0.5,
        "attn_sinks": jax.random.normal(ks[3], (DEPTH, N_ATTN_HEADS), f32),
        "w_out": jax.random.normal(ks[4], (DEPTH, MIX_W, D_MODEL), f32) * MIX_W ** -0.5,
        "mix_post_norm": gain(ks[5]),
        "ffn_pre_norm": gain(ks[6]),
        "w_up": jax.random.normal(ks[7], (DEPTH, D_MODEL, 2 * D_FF), f32) * D_MODEL ** -0.5,
        "conv_w": jax.random.normal(ks[8], (DEPTH, CONV_WIDTH, 2 * D_FF), f32) * CONV_WIDTH ** -0.5,
        "conv_b": 0.01 * jax.random.normal(ks[9], (DEPTH, 2 * D_FF), f32),
        "w_down": jax.random.normal(ks[10], (DEPTH, D_FF, D_MODEL), f32) * D_FF ** -0.5,
        "ffn_post_norm": gain(ks[11]),
    }

def first_block(x, mix_pre_norm, w_in, attn_sinks, w_out, mix_post_norm,
              ffn_pre_norm, w_up, conv_w, conv_b, w_down, ffn_post_norm):
    splits = np.cumsum([ATTN_W, KV_W, KV_W, RET_W, RET_W, RET_W]).tolist()
    for l in range(DEPTH):
        h = rms_norm(x, mix_pre_norm[l])
        proj = jnp.einsum('bsd,de->bse', h, w_in[l])
        q_a, k_a, v_a, q_r, k_r, v_r, g_r = jnp.split(proj, splits, axis=-1)
        attn_out = sliding_window_sink_attention(q_a, k_a, v_a, attn_sinks[l])
        ret_out = retention_group(q_r, k_r, v_r, g_r)
        mixed = jnp.einsum('bse,ed->bsd', jnp.concatenate([attn_out, ret_out], axis=-1), w_out[l])
        x = x + rms_norm(mixed, mix_post_norm[l])
        h = rms_norm(x, ffn_pre_norm[l])
        u = causal_depthwise_conv(jnp.einsum('bsd,df->bsf', h, w_up[l]), conv_w[l], conv_b[l])
        u_gate, u_val = jnp.split(u, 2, axis=-1)
        y = jax.nn.gelu(u_gate, approximate=True) * u_val
        y = jnp.einsum('bsf,fd->bsd', y, w_down[l])
        x = x + rms_norm(y, ffn_post_norm[l])
    return x


DA_HEADS = 8
DA_V_DIM = 2 * HEAD_DIM
NSA_HEADS = 16
NSA_GROUPS = 2
NSA_HPG = NSA_HEADS // NSA_GROUPS
CMP_BLOCK = 32
CMP_STRIDE = 16
CMP_HIDDEN = 256
SLC_BLOCK = 64
SLC_TOPN = 16
WIN = 512
Q_BLOCK = 128
SLC_Q_BLOCK = 64
ROPE_THETA = 10000.0
EPS = 1e-6
NEG_INF = -1e30
FORCE_SCORE = 1e9

DA_QK_W = DA_HEADS * 2 * HEAD_DIM
DA_V_W = DA_HEADS * DA_V_DIM
NSA_Q_W = NSA_HEADS * HEAD_DIM
NSA_KV_W = NSA_GROUPS * HEAD_DIM
NSA_GATE_W = 3 * NSA_HEADS
IN_WIDTHS = (DA_QK_W, DA_QK_W, DA_V_W, NSA_Q_W) + (NSA_KV_W,) * 6 + (NSA_GATE_W, D_MODEL, D_MODEL)
D_IN = sum(IN_WIDTHS)


def rmsnorm(x, g):
    xf = x.astype(jnp.float32)
    y = xf * lax.rsqrt(jnp.mean(xf * xf, axis=-1, keepdims=True) + EPS)
    return (y * g.astype(jnp.float32)).astype(x.dtype)

def swiglu(h, w1, w3, w2):
    return (jax.nn.silu(h @ w1) * (h @ w3)) @ w2

def rope_tables(T, dim):
    pos = jnp.arange(T, dtype=jnp.float32)
    inv = 1.0 / (ROPE_THETA ** (jnp.arange(0, dim, 2, dtype=jnp.float32) / dim))
    ang = pos[:, None] * inv[None, :]
    return jnp.cos(ang), jnp.sin(ang)

def apply_rope(x, cos, sin):
    half = x.shape[-1] // 2
    shape = (1, x.shape[1]) + (1,) * (x.ndim - 3) + (half,)
    c = cos.reshape(shape).astype(x.dtype)
    s = sin.reshape(shape).astype(x.dtype)
    x1, x2 = x[..., :half], x[..., half:]
    return jnp.concatenate([x1 * c - x2 * s, x2 * c + x1 * s], axis=-1)

def _sweep(block_fn, n_blocks):
    out = lax.map(block_fn, jnp.arange(n_blocks))
    out = jnp.moveaxis(out, 0, 1)
    return out.reshape((out.shape[0], n_blocks * out.shape[2]) + out.shape[3:])

def diff_attention(q, k, v, cos, sin, lam_params, head_gain, lam_init):
    B, T = q.shape[0], q.shape[1]
    q = apply_rope(q, cos, sin)
    k = apply_rope(k, cos, sin)
    lp = lam_params.astype(jnp.float32)
    lam = jnp.exp(jnp.sum(lp[0] * lp[1])) - jnp.exp(jnp.sum(lp[2] * lp[3])) + lam_init
    kpos = jnp.arange(T)
    scale = HEAD_DIM ** -0.5

    def block(i):
        qb = lax.dynamic_slice_in_dim(q, i * Q_BLOCK, Q_BLOCK, axis=1)
        qpos = i * Q_BLOCK + jnp.arange(Q_BLOCK)
        s = jnp.einsum('bqhcd,bkhcd->bhcqk', qb, k).astype(jnp.float32) * scale
        s = jnp.where(kpos[None, :] <= qpos[:, None], s, NEG_INF)
        p = jax.nn.softmax(s, axis=-1)
        a = p[:, :, 0] - lam * p[:, :, 1]
        return jnp.einsum('bhqk,bkhe->bqhe', a.astype(v.dtype), v)

    o = _sweep(block, T // Q_BLOCK)
    o = rmsnorm(o, head_gain) * (1.0 - lam_init)
    return o.reshape(B, T, DA_V_W)

def compress(x_raw, pos, w1, w2):
    B, T = x_raw.shape[0], x_raw.shape[1]
    n_cmp = (T - CMP_BLOCK) // CMP_STRIDE + 1
    idx = np.arange(n_cmp)[:, None] * CMP_STRIDE + np.arange(CMP_BLOCK)[None, :]
    blocks = x_raw[:, idx] + pos[:, None, :]
    blocks = jnp.swapaxes(blocks, 2, 3).reshape(B, n_cmp, NSA_GROUPS, CMP_BLOCK * HEAD_DIM)
    return jax.nn.gelu(blocks @ w1) @ w2

def _overlap_matrix(n_cmp, n_slc):
    start = np.arange(n_cmp) * CMP_STRIDE
    sb = np.arange(n_slc) * SLC_BLOCK
    ov = (start[:, None] < sb[None, :] + SLC_BLOCK) & (start[:, None] + CMP_BLOCK > sb[None, :])
    return ov.astype(np.float32)

def nsa(q, k_cmp, v_cmp, k_slc, v_slc, k_win, v_win, gate_logits, cos, sin, cmp_pos, cmp_w1, cmp_w2):
    B, T = q.shape[0], q.shape[1]
    dt = q.dtype
    scale = HEAD_DIM ** -0.5
    t = jnp.arange(T)

    kc = compress(k_cmp, cmp_pos[0], cmp_w1[0], cmp_w2[0])
    vc = compress(v_cmp, cmp_pos[1], cmp_w1[1], cmp_w2[1])
    n_cmp = kc.shape[1]
    s = jnp.einsum('btgjd,bngd->btgjn', q, kc).astype(jnp.float32) * scale
    c_valid = ((jnp.arange(n_cmp) * CMP_STRIDE + CMP_BLOCK - 1)[None, :] <= t[:, None])[None, :, None, None, :]
    p_cmp = jnp.where(c_valid, jax.nn.softmax(jnp.where(c_valid, s, NEG_INF), axis=-1), 0.0)
    o_cmp = jnp.einsum('btgjn,bngd->btgjd', p_cmp.astype(dt), vc)

    n_slc = T // SLC_BLOCK
    overlap = jnp.asarray(_overlap_matrix(n_cmp, n_slc))
    imp = jnp.einsum('btgjn,ns->btgs', p_cmp, overlap)
    blk_t = t // SLC_BLOCK
    sblk = jnp.arange(n_slc)
    causal = sblk[None, :] <= blk_t[:, None]
    forced = (sblk[None, :] == 0) | (sblk[None, :] == blk_t[:, None]) | (sblk[None, :] == blk_t[:, None] - 1)
    score = jnp.where(forced[None, :, None, :], FORCE_SCORE,
                      jnp.where(causal[None, :, None, :], imp, -1.0))
    _, sel = lax.top_k(score, min(SLC_TOPN, n_slc))
    sel_valid = sel <= blk_t[None, :, None, None]

    qr = apply_rope(q, cos, sin)
    ks = apply_rope(k_slc, cos, sin)
    kw = apply_rope(k_win, cos, sin)

    ks_blk = ks.reshape(B, n_slc, SLC_BLOCK, NSA_GROUPS, HEAD_DIM).transpose(0, 3, 1, 2, 4)
    vs_blk = v_slc.reshape(B, n_slc, SLC_BLOCK, NSA_GROUPS, HEAD_DIM).transpose(0, 3, 1, 2, 4)
    bidx = jnp.arange(B)[:, None, None, None]
    gidx = jnp.arange(NSA_GROUPS)[None, None, :, None]

    def slc_block(i):
        qb = lax.dynamic_slice_in_dim(qr, i * SLC_Q_BLOCK, SLC_Q_BLOCK, axis=1)
        selb = lax.dynamic_slice_in_dim(sel, i * SLC_Q_BLOCK, SLC_Q_BLOCK, axis=1)
        validb = lax.dynamic_slice_in_dim(sel_valid, i * SLC_Q_BLOCK, SLC_Q_BLOCK, axis=1)
        qpos = i * SLC_Q_BLOCK + jnp.arange(SLC_Q_BLOCK)
        kg = ks_blk[bidx, gidx, selb]
        vg = vs_blk[bidx, gidx, selb]
        kpos = selb[..., None] * SLC_BLOCK + jnp.arange(SLC_BLOCK)
        mask = validb[..., None] & (kpos <= qpos[None, :, None, None, None])
        s = jnp.einsum('bqgjd,bqgnld->bqgjnl', qb, kg).astype(jnp.float32) * scale
        s = jnp.where(mask[:, :, :, None], s, NEG_INF)
        sh = s.shape
        p = jax.nn.softmax(s.reshape(sh[:4] + (-1,)), axis=-1).reshape(sh)
        return jnp.einsum('bqgjnl,bqgnld->bqgjd', p.astype(dt), vg)

    o_slc = _sweep(slc_block, T // SLC_Q_BLOCK)

    kw_pad = jnp.pad(kw, ((0, 0), (WIN, 0), (0, 0), (0, 0)))
    vw_pad = jnp.pad(v_win, ((0, 0), (WIN, 0), (0, 0), (0, 0)))

    def win_block(i):
        qb = lax.dynamic_slice_in_dim(qr, i * Q_BLOCK, Q_BLOCK, axis=1)
        qpos = i * Q_BLOCK + jnp.arange(Q_BLOCK)
        kb = lax.dynamic_slice_in_dim(kw_pad, i * Q_BLOCK, WIN + Q_BLOCK, axis=1)
        vb = lax.dynamic_slice_in_dim(vw_pad, i * Q_BLOCK, WIN + Q_BLOCK, axis=1)
        kpos = i * Q_BLOCK - WIN + jnp.arange(WIN + Q_BLOCK)
        mask = (kpos[None, :] >= 0) & (kpos[None, :] <= qpos[:, None]) & (kpos[None, :] > qpos[:, None] - WIN)
        s = jnp.einsum('bqgjd,bkgd->bqgjk', qb, kb).astype(jnp.float32) * scale
        s = jnp.where(mask[None, :, None, None, :], s, NEG_INF)
        p = jax.nn.softmax(s, axis=-1)
        return jnp.einsum('bqgjk,bkgd->bqgjd', p.astype(dt), vb)

    o_win = _sweep(win_block, T // Q_BLOCK)

    g = jax.nn.sigmoid(gate_logits.astype(jnp.float32)).astype(dt).reshape(B, T, NSA_GROUPS, NSA_HPG, 3)
    o = g[..., 0:1] * o_cmp + g[..., 1:2] * o_slc + g[..., 2:3] * o_win
    return o.reshape(B, T, NSA_Q_W)

def token_mix(h, w_in, da_lambda, da_head_norm, cmp_pos, cmp_w1, cmp_w2, w_proj_da, w_proj_nsa, w_out, lam_init):
    B, T = h.shape[0], h.shape[1]
    proj = h @ w_in
    offs = []
    acc = 0
    for w in IN_WIDTHS[:-1]:
        acc += w
        offs.append(acc)
    (q_da, k_da, v_da, q_ns, kc_raw, vc_raw, ks_raw, vs_raw, kw_raw, vw_raw,
     g_ns, g_a, g_b) = jnp.split(proj, offs, axis=-1)
    cos, sin = rope_tables(T, HEAD_DIM)
    y_da = diff_attention(q_da.reshape(B, T, DA_HEADS, 2, HEAD_DIM),
                          k_da.reshape(B, T, DA_HEADS, 2, HEAD_DIM),
                          v_da.reshape(B, T, DA_HEADS, DA_V_DIM),
                          cos, sin, da_lambda, da_head_norm, lam_init)
    kv = lambda a: a.reshape(B, T, NSA_GROUPS, HEAD_DIM)
    y_ns = nsa(q_ns.reshape(B, T, NSA_GROUPS, NSA_HPG, HEAD_DIM),
               kv(kc_raw), kv(vc_raw), kv(ks_raw), kv(vs_raw), kv(kw_raw), kv(vw_raw),
               g_ns, cos, sin, cmp_pos, cmp_w1, cmp_w2)
    merged = jax.nn.sigmoid(g_a) * (y_da @ w_proj_da) + jax.nn.sigmoid(g_b) * (y_ns @ w_proj_nsa)
    return merged @ w_out

def second_inputs(seed: int = 0) -> dict:
    key = jax.random.key(seed)
    ks = jax.random.split(key, 24)
    f32 = jnp.float32

    def w(k, shape, fan_in):
        return jax.random.normal(k, shape, f32) * fan_in ** -0.5

    def gain(k, shape):
        return 1.0 + 0.05 * jax.random.normal(k, shape, f32)

    return {
        'x': jax.random.normal(ks[0], (BATCH, SEQ, D_MODEL), f32),
        'ffn1_norm': gain(ks[1], (DEPTH, D_MODEL)),
        'ffn1_w1': w(ks[2], (DEPTH, D_MODEL, D_FF), D_MODEL),
        'ffn1_w3': w(ks[3], (DEPTH, D_MODEL, D_FF), D_MODEL),
        'ffn1_w2': w(ks[4], (DEPTH, D_FF, D_MODEL), D_FF),
        'mix_norm': gain(ks[5], (DEPTH, D_MODEL)),
        'w_in': w(ks[6], (DEPTH, D_MODEL, D_IN), D_MODEL),
        'da_lambda': 0.1 * jax.random.normal(ks[7], (DEPTH, 4, HEAD_DIM), f32),
        'da_head_norm': gain(ks[8], (DEPTH, DA_HEADS, DA_V_DIM)),
        'cmp_pos': 0.1 * jax.random.normal(ks[9], (DEPTH, 2, CMP_BLOCK, HEAD_DIM), f32),
        'cmp_w1': w(ks[10], (DEPTH, 2, CMP_BLOCK * HEAD_DIM, CMP_HIDDEN), CMP_BLOCK * HEAD_DIM),
        'cmp_w2': w(ks[11], (DEPTH, 2, CMP_HIDDEN, HEAD_DIM), CMP_HIDDEN),
        'w_proj_da': w(ks[12], (DEPTH, DA_V_W, D_MODEL), DA_V_W),
        'w_proj_nsa': w(ks[13], (DEPTH, NSA_Q_W, D_MODEL), NSA_Q_W),
        'w_out': w(ks[14], (DEPTH, D_MODEL, D_MODEL), D_MODEL),
        'ffn2_norm': gain(ks[15], (DEPTH, D_MODEL)),
        'ffn2_w1': w(ks[16], (DEPTH, D_MODEL, D_FF), D_MODEL),
        'ffn2_w3': w(ks[17], (DEPTH, D_MODEL, D_FF), D_MODEL),
        'ffn2_w2': w(ks[18], (DEPTH, D_FF, D_MODEL), D_FF),
        'final_norm': gain(ks[19], (D_MODEL,)),
    }

def second_block(x, ffn1_norm, ffn1_w1, ffn1_w3, ffn1_w2, mix_norm, w_in, da_lambda, da_head_norm,
              cmp_pos, cmp_w1, cmp_w2, w_proj_da, w_proj_nsa, w_out,
              ffn2_norm, ffn2_w1, ffn2_w3, ffn2_w2, final_norm):
    for l in range(DEPTH):
        lam_init = 0.8 - 0.6 * math.exp(-0.3 * l)
        h = rmsnorm(x, ffn1_norm[l])
        x = x + 0.5 * swiglu(h, ffn1_w1[l], ffn1_w3[l], ffn1_w2[l])
        h = rmsnorm(x, mix_norm[l])
        x = x + token_mix(h, w_in[l], da_lambda[l], da_head_norm[l], cmp_pos[l], cmp_w1[l], cmp_w2[l],
                          w_proj_da[l], w_proj_nsa[l], w_out[l], lam_init)
        h = rmsnorm(x, ffn2_norm[l])
        x = x + 0.5 * swiglu(h, ffn2_w1[l], ffn2_w3[l], ffn2_w2[l])
    return rmsnorm(x, final_norm)


def setup_inputs(seed=0):
    out = dict(first_inputs(seed))
    for name, value in second_inputs(seed + 1).items():
        if name != "x":
            out[name + "_2"] = value
    return out


def reference(
    x, mix_pre_norm, w_in, attn_sinks, w_out, mix_post_norm, ffn_pre_norm, w_up, conv_w, conv_b,
    w_down, ffn_post_norm, ffn1_norm_2, ffn1_w1_2, ffn1_w3_2, ffn1_w2_2, mix_norm_2, w_in_2,
    da_lambda_2, da_head_norm_2, cmp_pos_2, cmp_w1_2, cmp_w2_2, w_proj_da_2, w_proj_nsa_2,
    w_out_2, ffn2_norm_2, ffn2_w1_2, ffn2_w3_2, ffn2_w2_2, final_norm_2,
):
    x = first_block(
        x, mix_pre_norm, w_in, attn_sinks, w_out, mix_post_norm, ffn_pre_norm, w_up, conv_w,
        conv_b, w_down, ffn_post_norm,
    )
    return second_block(
        x, ffn1_norm_2, ffn1_w1_2, ffn1_w3_2, ffn1_w2_2, mix_norm_2, w_in_2, da_lambda_2,
        da_head_norm_2, cmp_pos_2, cmp_w1_2, cmp_w2_2, w_proj_da_2, w_proj_nsa_2, w_out_2,
        ffn2_norm_2, ffn2_w1_2, ffn2_w3_2, ffn2_w2_2, final_norm_2,
    )


_drawn_inputs = setup_inputs


def setup_inputs(seed=0):
    import zlib

    import numpy as np

    out = dict(_drawn_inputs(seed))
    spreads = {}
    factors = {'mix_post_norm': 3.039,
     'ffn_pre_norm': 3.095,
     'conv_b': 5.607,
     'ffn_post_norm': 4.585,
     'ffn1_norm_2': 4.334,
     'mix_norm_2': 2.907,
     'da_head_norm_2': 16.144,
     'cmp_pos_2': 7.091,
     'ffn2_norm_2': 4.927}
    for name, (base, spread) in spreads.items():
        noise = np.random.default_rng([zlib.crc32(name.encode()), seed]).standard_normal(out[name].shape)
        drawn = base * np.exp(spread * noise) if base else spread * noise
        out[name] = __import__('jax').numpy.asarray(drawn.astype(out[name].dtype))
    for name, factor in factors.items():
        out[name] = (out[name] * factor).astype(out[name].dtype)
    return out
```

```python
from contextlib import ExitStack

import numpy as np

import concourse.bass as bass
from concourse import mybir

F32 = mybir.dt.float32
F32R = mybir.dt.float32r
BF16 = mybir.dt.bfloat16
ACT = mybir.ActivationFunctionType
ALU = mybir.AluOpType
AX = mybir.AxisListType

P = 128
SEQ = 512
D = 1024
TT = SEQ // P
KT = D // P
D_FF = 2816
FT = D_FF // P
CHUNK = 1024
SLOTS = 4
LEAD = 3
EPS = 1e-6
NEG = -1e30
HD = 64
N_CMP = 31
NSA_HEADS = 16
LAM_INIT = 0.2

STAGES = [
    ("norm0", 0, [0] * 8, [1] * 8),
    ("qa", 4, [1, 1, 1, 1, 0, 0, 0, 0], [0] * 8),
    ("kva", 2, [1, 1, 0, 0, 0, 0, 0, 0], [0] * 8),
    ("rope_r", 8, [2, 2, 2, 2, 0, 0, 0, 0], [0, 0, 0, 0, 4, 4, 0, 0]),
    ("vg", 8, [1] * 8, [0] * 8),
    ("ret", 0, [0] * 8, [4, 4, 4, 4, 2, 2, 0, 0]),
    ("local", 0, [0] * 8, [8, 8, 8, 8, 16, 16, 8, 8]),
    ("cat", 0, [0] * 8, [1] * 8),
    ("out1", 8, [1] * 8, [0] * 8),
    ("norm1", 0, [0] * 8, [1] * 8),
    ("up1", 2 * FT, [FT // 2] * 4 + [0] * 4, [0] * 8),
    ("down1", FT, [1] * 8, [0] * 8),
    ("norm2", 0, [0] * 8, [1] * 8),
    ("up2", 2 * FT, [FT // 2] * 4 + [0] * 4, [0] * 8),
    ("down2", FT, [1] * 8, [0] * 8),
    ("norm3", 0, [0] * 8, [1] * 8),
    ("rope_dq", 8, [2, 2, 2, 2, 0, 0, 0, 0], [0, 0, 0, 0, 4, 4, 0, 0]),
    ("rope_dk", 8, [2, 2, 2, 2, 0, 0, 0, 0], [0, 0, 0, 0, 4, 4, 0, 0]),
    ("vda", 8, [1] * 8, [0] * 8),
    ("da", 0, [0] * 8, [16, 16, 16, 16, 16, 16, 16, 16]),
    ("nsf", 4, [1, 1, 1, 1, 0, 0, 0, 0], [0, 0, 0, 0, 1, 1, 0, 0]),
    ("nst", 3, [1, 1, 1, 0, 0, 0, 0, 0], [0] * 8),
    ("cmp", 0, [0] * 8, [0, 0, 0, 0, 1, 1, 1, 1]),
    ("rope_q", 8, [2, 2, 2, 2, 0, 0, 0, 0], [0, 0, 0, 0, 4, 4, 0, 0]),
    ("cmpa", 0, [0] * 8, [4, 4, 8, 8, 4, 4, 4, 4]),
    ("nsa", 0, [0] * 8, [32, 32, 32, 32, 64, 64, 32, 32]),
    ("ydat", 0, [0] * 8, [1] * 8),
    ("ga", 8, [1] * 8, [0] * 8),
    ("gb", 8, [1] * 8, [0] * 8),
    ("ynst", 0, [0] * 8, [1] * 8),
    ("pda", 8, [1] * 8, [0] * 8),
    ("pns", 8, [1] * 8, [0] * 8),
    ("mt", 0, [0] * 8, [1] * 8),
    ("out2", 8, [1] * 8, [0] * 8),
    ("norm4", 0, [0] * 8, [1] * 8),
    ("up3", 2 * FT, [FT // 2] * 4 + [0] * 4, [0] * 8),
    ("down3", FT, [1] * 8, [0] * 8),
]
T_STAGES = ["vg", "out1", "down1", "down2", "vda", "ga", "gb", "pda", "pns", "out2", "down3"]
NORMS = ["norm0", "norm1", "norm2", "norm3", "norm4"]
HT_STAGES = ["norm0", "cat", "norm1", "norm2", "norm3", "ydat", "ynst", "mt", "norm4"]


def counts():
    chunk, freed, filled = {}, {}, {}
    c, fr, fi = 0, [0] * 8, [0] * 8
    for name, n, streamed, other in STAGES:
        chunk[name], freed[name], filled[name] = c, list(fr), list(fi)
        c += n
        fr = [a + b + d for a, b, d in zip(fr, streamed, other)]
        fi = [a + b for a, b in zip(fi, other)]
    return chunk, freed, filled, c


CHUNK0, FREED, FILLED, N_CHUNKS = counts()


def at_least(eng, sem, value):
    if isinstance(value, int) and value <= 0:
        return
    eng.wait_ge(sem, value)


def program(nc, t, out, stop=None):
    scalar, vector, tensor, pool = nc.scalar, nc.vector, nc.tensor, nc.gpsimd
    names = [s[0] for s in STAGES]
    last_stage = len(names) if stop is None else names.index(stop)

    def on(name):
        return names.index(name) < last_stage

    n_chunks = N_CHUNKS if stop is None else CHUNK0[stop]

    with ExitStack() as ctx:
        def sb(name, shape, dt=F32):
            return ctx.enter_context(nc.sbuf_tensor(name, shape, dt))

        def sem(name):
            return ctx.enter_context(nc.semaphore(name))

        X = sb("X", [P, TT, D])
        HTh = sb("HTh", [P, KT, SEQ], F32R)
        HTl = sb("HTl", [P, KT, SEQ], F32R)
        raw = sb("raw", [P, SLOTS, CHUNK])
        Wh = sb("Wh", [P, SLOTS, CHUNK], F32R)
        Wl = sb("Wl", [P, SLOTS, CHUNK], F32R)
        ident = sb("ident", [P, P])
        identb = sb("identb", [P, P], BF16)
        causal = sb("causal", [P, P], BF16)
        outside = sb("outside", [P, P], BF16)
        perm = sb("perm", [P, P])
        cos = sb("cos", [P, SEQ])
        sin = sb("sin", [P, SEQ])
        gains = sb("gains", [P, 6, KT])
        gpost = sb("gpost", [P, D])
        conv = sb("conv", [P, 2 * FT, 4])
        sinks = sb("sinks", [P, 8])
        nsinks = sb("nsinks", [P, 8])
        lam_pr = sb("lam_pr", [P, 2, HD])
        lam_s = sb("lam_s", [P, 2])
        lam_e = sb("lam_e", [P, 2])
        nlam = sb("nlam", [P, 1])
        cmask = sb("cmask", [P, TT, N_CMP])
        cvalid = sb("cvalid", [P, TT])
        eps = sb("eps", [P, 1])
        ss = sb("ss", [P, 8])
        sst = sb("sst", [P, TT])
        std = sb("std", [P, TT])
        rstd = sb("rstd", [P, TT])
        nmx = sb("nmx", [P, 2, 2])
        rs = sb("rs", [P, 2, 2])
        esk = sb("esk", [P, 2, 2])
        rr = sb("rr", [P, 2, 2])
        gg = sb("gg", [P, 2, 2])
        bn = sb("bn", [P, 16, 6])
        mv = sb("mv", [P, 16, 2])
        gsd = sb("gsd", [P, 16])
        grs = sb("grs", [P, 16])
        hss = sb("hss", [P, 32])
        hsd = sb("hsd", [P, 32])
        hrs = sb("hrs", [P, 32])

        K = 1024
        region = (nc.sbuf_base + 31) // 32 * 32
        limit = nc.sbuf_usable_end

        def at(name, kib, shape, dt=F32):
            off = region + int(kib * K)
            size = int(np.prod(shape[1:])) * 4
            assert off + size <= limit, (name, off + size, limit)
            return nc.alloc_sbuf_tensor_at(name, shape, dt, offset=off)

        XN = at("XN", 0, [P, TT, D])
        Y = at("Y", 0, [P, FT, SEQ])
        Yh = at("Yh", 44, [P, SLOTS, SEQ], F32R)
        Yl = at("Yl", 52, [P, SLOTS, SEQ], F32R)
        U = at("U", 60, [P, 4, SEQ])
        GU = at("GU", 68, [P, 2, SEQ])
        masks_f = at("masks_f", 58, [P, 3, P])
        lam_in = at("lam_in", 60, [P, 2, 2, HD])
        qaT = at("qaT", 0, [P, 4, SEQ])
        kaT = at("kaT", 8, [P, 2, SEQ])
        va = at("va", 12, [P, TT, P])
        qkr = at("qkr", 14, [P, 8, SEQ])
        vr = at("vr", 30, [P, TT, SEQ])
        sg = at("sg", 38, [P, TT, SEQ])
        CAT = at("CAT", 46, [P, TT, D])
        Pb = at("Pb", 62, [P, 2, 2, SEQ])
        AT = at("AT", 70, [P, 2, 2, SEQ])
        QS = at("QS", 78, [P, 2, SEQ])
        KS = at("KS", 82, [P, 2, SEQ])
        rtmp = at("rtmp", 86, [P, SEQ])
        decay = at("decay", 88, [P, 4, SEQ])
        STs = [at(f"STs{u}", 62 + 5 * u, [P, 1280]) for u in range(2)]
        qkd = at("qkd", 0, [P, 16, SEQ])
        vd = at("vd", 32, [P, TT, D])
        YD = at("YD", 46 + 2, [P, TT, D])
        Pb2 = at("Pb2", 64, [P, 2, 2, SEQ])
        AT2 = at("AT2", 72, [P, 2, 2, SEQ])
        QS2 = at("QS2", 80, [P, 2, SEQ])
        KS2 = at("KS2", 84, [P, 2, SEQ])
        rtmp2 = at("rtmp2", 78, [P, SEQ])
        DSQ = at("DSQ", 64, [P, TT, D])
        cw1k = at("cw1k", 0, [P, 16, 256])
        cw1v = at("cw1v", 16, [P, 16, 256])
        w2k = at("w2k", 32, [P, 2, 2, HD])
        w2v = at("w2v", 33, [P, 2, HD])
        posT = at("posT", 34, [P, 2, 32])
        YN = at("YN", 32, [P, TT, D])
        qn = at("qn", 0, [P, 8, SEQ])
        qnr = at("qnr", 16, [P, 8, SEQ])
        kcv = at("kcv", 64, [P, 2, SEQ])
        cA = at("cA", 68, [P, 2, 16, 62])
        hid = at("hid", 76, [P, 2, 2, 62])
        kraw = at("kraw", 80, [P, 2, SEQ])
        ksw = at("ksw", 84, [P, 2, 2, SEQ])
        vsw = at("vsw", 92, [P, 2, TT, P])
        gates = at("gates", 96, [P, TT, 48])
        kcT = at("kcT", 96.75, [P, 62])
        vcm = at("vcm", 97, [31, 2 * HD])
        QSn = at("QSn", 80, [P, SEQ])
        QSc = at("QSc", 80, [P, 2, SEQ])
        CS = at("CS", 64, [P, 2, 8, 32])
        CP = at("CP", 66, [P, 2, 8, 32])
        CA = at("CA", 68, [31, 2, 8, P])
        cst = at("cst", 76, [P, 2, 5, 8])
        HT2h = at("HT2h", 0, [P, KT, SEQ], F32R)
        HT2l = at("HT2l", 16, [P, KT, SEQ], F32R)
        GA = at("GA", 64, [P, TT, D])
        GB = at("GB", 80, [P, TT, D])

        ps = [ctx.enter_context(nc.psum_tensor(f"ps{b}", [P, 512], F32)) for b in range(8)]

        in_x = sem("in_x")
        in_c = sem("in_c")
        in_rope = sem("in_rope")
        in_post = sem("in_post")
        in_cw = sem("in_cw")
        w_raw = [sem(f"w_raw{s}") for s in range(SLOTS)]
        w_hi = sem("w_hi")
        w_lo = sem("w_lo")
        w_used = sem("w_used")
        t_done = sem("t_done")
        free = [sem(f"free{b}") for b in range(8)]
        full = [sem(f"full{b}") for b in range(8)]
        boot = sem("boot")
        boot2 = sem("boot2")
        boot3 = sem("boot3")
        x_ready = sem("x_ready")
        n_std = sem("n_std")
        xn_ready = sem("xn_ready")
        ht_hi = sem("ht_hi")
        roped = sem("roped")
        post_used = sem("post_used")
        r_sq = sem("r_sq")
        r_sum = sem("r_sum")
        r_std = sem("r_std")
        gn_mv = sem("gn_mv")
        gn_sd = sem("gn_sd")
        cat_ret = sem("cat_ret")
        staged = sem("staged")
        mx_done = sem("mx_done")
        a_ready = sem("a_ready")
        u_ready = sem("u_ready")
        g_ready = sem("g_ready")
        y_ready = sem("y_ready")
        y_pre_hi = sem("y_pre_hi")
        y_pre = sem("y_pre")
        da_sq = sem("da_sq")
        da_ss = sem("da_ss")
        da_sd = sem("da_sd")
        da_fin = sem("da_fin")
        cm_a = sem("cm_a")
        cm_s = sem("cm_s")
        cm_e = sem("cm_e")
        cm_p = sem("cm_p")
        cst_q = sem("cst_q")
        merged = sem("merged")
        f_out = sem("f_out")
        s_out = sem("s_out")

        lam_stage_x = {"norm1": 0, "norm2": 1, "norm3": 2, "norm4": 3}

        STEP0 = {"local": 0, "da": 16, "nsa": 48}
        STG0 = {"local": 0, "da": 8, "nsa": 24}

        def bank_t(tt, half):
            return 2 * tt + half

        block = ctx.enter_context(nc.Block())

        @block.sync
        def _(sp):
            sp.dma_start(X[:], t["x"].rearrange("(t p) d -> p t d", p=P)).then_inc(in_x, 16)
            w = t["w_all"]
            for n in range(SLOTS):
                sp.dma_start(raw[:, n, :], w[n]).then_inc(w_raw[n], 16)
            rounds = (n_chunks - SLOTS) // SLOTS
            with sp.Fori(0, rounds) as i:
                for s in range(SLOTS):
                    sp.wait_ge(w_lo, i * SLOTS + s + 1)
                    sp.dma_start(raw[:, s, :], w[bass.ds(i * SLOTS + (SLOTS + s), 1)].rearrange("a p n -> p (a n)")).then_inc(w_raw[s], 16)
            for n in range(SLOTS + rounds * SLOTS, n_chunks):
                sp.wait_ge(w_lo, n - SLOTS + 1)
                sp.dma_start(raw[:, n % SLOTS, :], w[n]).then_inc(w_raw[n % SLOTS], 16)
            if stop is None:
                for tt in range(TT):
                    sp.wait_ge(f_out, tt + 1)
                    sp.dma_start(out[tt * P:(tt + 1) * P, :], XN[:, tt, :]).then_inc(s_out, 16)
                sp.wait_ge(s_out, TT * 16)
            else:
                k = sum(4 for s in ("out1", "down1", "down2", "out2") if on(s))
                sp.wait_ge(x_ready, k)
                sp.dma_start(out.rearrange("(t p) d -> p t d", p=P), X[:]).then_inc(s_out, 16)
                sp.wait_ge(s_out, 16)

        @block.gpsimd
        def _(pl):
            def everywhere(v):
                return v.rearrange("(a n) -> a n", a=1).broadcast_to((P, v.shape[0]))

            def load(dst, src, s):
                pl.dma_start(dst, src).then_inc(s, 16)

            load(ident[:], t["c_ident"], in_c)
            load(masks_f[:], t["c_masks"], in_c)
            load(gains[:], t["gains"], in_c)
            load(perm[:], t["c_perm_r"], in_c)
            load(cos[:], t["c_cos_r"], in_c)
            load(sin[:], t["c_sin_r"], in_c)
            load(sinks[:], everywhere(t["attn_sinks"]), in_c)
            load(lam_in[:].rearrange("p a b d -> p (a b d)"), everywhere(t["da_lambda"]), in_c)
            load(decay[:], t["c_decay"], in_c)
            load(conv[:], t["conv"], in_c)
            load(cmask[:], t["c_cmask"], in_c)
            load(cvalid[:], t["c_cvalid"], in_c)
            load(gpost[:], everywhere(t["mix_post"]), in_post)

            if on("local"):
                for it in range(2):
                    for p_ in range(2):
                        at_least(pl, full[3], FILLED["local"][3] + 4 * (it - 1) + 2 * p_ + 2)
                        if it == 0 and p_ == 0:
                            pl.wait_ge(free[3], FREED["vg"][3])
                            pl.wait_ge(free[0], FREED["rope_r"][0])
                        pool.tensor_copy(QS[:, p_, :], qaT[:, 2 * it + p_, :]).then_inc(staged, 1)
                        pool.tensor_copy(KS[:, p_, :], kaT[:, it, :]).then_inc(staged, 1)
            if on("out1"):
                pl.wait_ge(post_used, 1)
                load(gpost[:], everywhere(t["ffn_post"]), in_post)
            if on("rope_r"):
                pl.wait_ge(roped, 8)
                load(perm[:], t["c_perm_n"], in_rope)
                load(cos[:], t["c_cos_n"], in_rope)
                load(sin[:], t["c_sin_n"], in_rope)
            if on("down1"):
                pl.wait_ge(post_used, 2)
                load(gpost[:], everywhere(t["final"]), in_post)
            if on("da"):
                pl.wait_ge(roped, 24)
                with pl.Fori(0, 4) as it:
                    for p_ in range(2):
                        pl.wait_ge(full[3], it * 4 + (FILLED["da"][3] - 4 + 2 * p_ + 2))
                        pool.tensor_copy(QS2[:, p_, :], qkd[:, bass.ds(it * 2 + p_, 1), :].rearrange("p a n -> p (a n)")).then_inc(staged, 1)
                        pool.tensor_copy(KS2[:, p_, :], qkd[:, bass.ds(it * 2 + (8 + p_), 1), :].rearrange("p a n -> p (a n)")).then_inc(staged, 1)
            if on("cmp"):
                pl.wait_ge(full[7], FILLED["nsf"][7])
                load(cw1k[:], t["cw1"][0].rearrange("(j p) n -> p j n", p=P), in_cw)
                load(cw1v[:], t["cw1"][1].rearrange("(j p) n -> p j n", p=P), in_cw)
                load(posT[:], t["posT"], in_cw)
                load(w2k[:], t["w2k"], in_cw)
                load(w2v[:], t["w2v"], in_cw)
            if on("cmpa"):
                pl.wait_ge(roped, 34)
                for g in range(2):
                    with pl.Fori(0, 2) as it:
                        for p_ in range(2):
                            pl.wait_ge(full[6 + p_], it + (FILLED["cmpa"][6 + p_] + 2 * g))
                            pool.tensor_copy(QSc[:, p_, :], qn[:, bass.ds(it * 2 + (4 * g + p_), 1), :].rearrange("p a n -> p (a n)")).then_inc(cst_q, 1)
            if on("nsa"):
                for g in range(2):
                    if g == 0:
                        pl.wait_ge(full[1], FILLED["nsa"][1])
                    with pl.Fori(0, 4) as it:
                        for u in range(2):
                            pl.wait_ge(full[3], it * 4 + (FILLED["nsa"][3] + 16 * g - 4 + 2 * u + 2))
                            pool.tensor_copy(QSn[64 * u:64 * u + 64, :], qnr[64 * u:64 * u + 64, bass.ds(it + 4 * g, 1), :].rearrange("p a n -> p (a n)")).then_inc(staged, 1)

        @block.tensor
        def _(pe):
            def weights(k, it=0):
                pe.wait_ge(w_lo, it * 4 + (k + 1))
                return k % SLOTS

            def three(dst, a_hi, a_lo, b_hi, b_lo, start, stop):
                tensor.matmul(dst, a_hi, b_hi, start=start, stop=False)
                tensor.matmul(dst, a_hi, b_lo, start=False, stop=False)
                return tensor.matmul(dst, a_lo, b_hi, start=False, stop=stop)

            def bank_free(stage, b, k=0):
                at_least(pe, free[b], k + FREED[stage][b])

            def ht_ready(stage):
                for b in range(KT):
                    pe.wait_ge(free[b], FREED[stage][b])

            def gemm_f(stage, c, bank, it=0, per=1, k0=0, hh=None, hl=None):
                s = weights(CHUNK0[stage] + c, it)
                bank_free(stage, bank, it * per + k0)
                for k in range(KT):
                    a = slice(k * P, (k + 1) * P)
                    last = three(ps[bank][:], Wh[:, s, a], Wl[:, s, a], HTh[:, k, :], HTl[:, k, :], k == 0, k == KT - 1)
                last.then_inc(w_used, 1)

            def gemm_n(stage, c, bank, it=0):
                s = weights(CHUNK0[stage] + c, it)
                bank_free(stage, bank)
                for tt in range(TT):
                    q = slice(tt * P, (tt + 1) * P)
                    for k in range(KT):
                        a = slice(k * P, (k + 1) * P)
                        last = three(ps[bank][:, q], HTh[:, k, q], HTl[:, k, q], Wh[:, s, a], Wl[:, s, a], k == 0, k == KT - 1)
                last.then_inc(w_used, 1)

            def chunk_t(stage, c, lh, ll, first, final, it=0):
                s = weights(CHUNK0[stage] + c, it)
                for tt in range(TT):
                    q = slice(tt * P, (tt + 1) * P)
                    for half in range(2):
                        b = bank_t(tt, half)
                        if first:
                            bank_free(stage, b)
                        n = slice(half * 512, (half + 1) * 512)
                        last = three(ps[b][:], lh[:, q], ll[:, q], Wh[:, s, n], Wl[:, s, n], first, final)
                        if final and b < 7:
                            last.then_inc(t_done, 1)
                last.then_inc(w_used, 1)

            def gemm_t(stage, hh=HTh, hl=HTl):
                for k in range(KT):
                    chunk_t(stage, k, hh[:, k, :], hl[:, k, :], k == 0, k == KT - 1)

            def to_ht(stage, src, ready=None):
                for k in range(KT):
                    bank_free(stage, k)
                    for tt in range(TT):
                        if k == 0 and ready is not None:
                            ready(tt)
                        last = tensor.transpose(ps[k][:, tt * P:(tt + 1) * P], src[:, tt, k * P:(k + 1) * P], ident[:])
                    last.then_inc(full[k], 1)

            def norm(i):
                to_ht(NORMS[i], XN, lambda tt: pe.wait_ge(xn_ready, 4 * i + tt + 1))

            def rotate(stage, c, src, it, per, dst_bank, uses):
                bank_free(stage, dst_bank, it * uses[0] + uses[1])
                tensor.matmul(ps[dst_bank][:], perm[:], src, start=True, stop=True).then_inc(full[dst_bank], 1)

            def rope(stage, rounds, src, tile0):
                with pe.Fori(0, rounds) as it:
                    for c in range(4):
                        gemm_f(stage, c, c, it, 1)
                        if c:
                            pe.wait_ge(free[c - 1], it + (FREED[stage][c - 1] + 1))
                            rotate(stage, c - 1, src[:, bass.ds(it * 4 + (tile0 + c - 1), 1), :].rearrange("p a n -> p (a n)"), it, 1,
                                   4 + (c - 1) % 2, (2, (c - 1) // 2))
                    pe.wait_ge(free[3], it + (FREED[stage][3] + 1))
                    rotate(stage, 3, src[:, bass.ds(it * 4 + (tile0 + 3), 1), :].rearrange("p a n -> p (a n)"), it, 1, 5, (2, 1))

            def up(stage, rounds=FT // 2):
                with pe.Fori(0, rounds) as it:
                    for c in range(4):
                        gemm_f(stage, c, c, it, 1)

            def down(stage):
                pe.wait_ge(y_pre, {"down1": 1, "down2": 2, "down3": 3}[stage])
                chunk_t(stage, 0, Yh[:, 0, :], Yl[:, 0, :], True, False)
                with pe.Fori(0, 4) as it:
                    for c in range(4):
                        s = (1 + c) % SLOTS
                        chunk_t(stage, 1 + c, Yh[:, s, :], Yl[:, s, :], False, False, it)
                for c in range(17, FT):
                    chunk_t(stage, c, Yh[:, c % SLOTS, :], Yl[:, c % SLOTS, :], False, c == FT - 1)

            def attend(kind, it, g=0):
                p_, at_ = (Pb, AT) if kind == "local" else (Pb2, AT2)
                qs, ks = (QS, KS) if kind == "local" else (QS2, KS2)
                steps0 = {"local": 0, "da": 0, "nsa": 32 * g}[kind]

                def uses(s, b):
                    if b < 4:
                        return it * 4 + (steps0 // 2 + s // 2)
                    if b < 6 and kind != "da":
                        return it * 8 + (steps0 + s)
                    return it * 4 + (steps0 // 2 + s // 2)

                def keys(i):
                    return (max(i - 1, 0), i + 1) if kind == "local" else (0, i + 1)

                def scores(s):
                    i = s % 4
                    k0, k1 = keys(i)
                    w = (k1 - k0) * P
                    if kind == "nsa":
                        if i == 0:
                            pe.wait_ge(staged, it * 2 + (STG0[kind] + 8 * g + s // 4 + 1))
                    elif i == 0:
                        pe.wait_ge(staged, it * 4 + (STG0[kind] + 2 * (s // 4) + 2))
                    for m in range(2):
                        b = 2 * (s % 2) + m
                        bank_free(kind, b, uses(s, b))
                        if kind == "nsa":
                            h = slice(64 * (s // 4), 64 * (s // 4) + 64)
                            lhs, rhs = QSn[h, i * P:(i + 1) * P], ksw[h, m, g, k0 * P:k1 * P]
                        else:
                            h = slice(64 * m, 64 * m + 64)
                            lhs, rhs = qs[h, s // 4, i * P:(i + 1) * P], ks[h, s // 4, k0 * P:k1 * P]
                        tensor.matmul(ps[b][:, 0:w], lhs, rhs, start=True, stop=False)
                        if kind == "local" and i > 0:
                            tensor.matmul(ps[b][:, 0:P], identb[:], outside[:], start=False, stop=False)
                        tensor.matmul(ps[b][:, w - P:w], identb[:], causal[:], start=False, stop=True).then_inc(full[b], 1)

                def turn(s):
                    k0, k1 = keys(s % 4)
                    pe.wait_ge(a_ready, it * 8 + (STEP0[kind] + steps0 + s + 1))
                    for m in range(1 if kind == "da" else 2):
                        b = 4 + s % 2 if kind == "da" else 4 + m
                        bank_free(kind, b, uses(s, b))
                        for j in range(k1 - k0):
                            last = tensor.transpose(ps[b][:, j * P:(j + 1) * P], p_[:, s % 2, m, j * P:(j + 1) * P], ident[:])
                        last.then_inc(full[b], 1)

                def values(s):
                    i = s % 4
                    k0, k1 = keys(i)
                    b = 6 + s % 2
                    bank_free(kind, b, uses(s, b))
                    n = k1 - k0
                    if kind == "da":
                        pe.wait_ge(free[4 + s % 2], uses(s, 4) + (FREED[kind][4 + s % 2] + 1))
                        for j in range(n):
                            last = tensor.matmul(ps[b][:, 0:P], at_[:, s % 2, 0, j * P:(j + 1) * P],
                                                 vd[:, j, bass.ds(it * 256 + 128 * (s // 4), P)], start=j == 0, stop=j == n - 1)
                    else:
                        for m in range(2):
                            pe.wait_ge(free[4 + m], uses(s, 4) + (FREED[kind][4 + m] + 1))
                            for j in range(n):
                                if kind == "local":
                                    last = tensor.matmul(ps[b][:, m * HD:(m + 1) * HD], at_[:, s % 2, m, j * P:(j + 1) * P],
                                                         va[:, k0 + j, it * HD:(it + 1) * HD], start=j == 0, stop=j == n - 1)
                                else:
                                    last = tensor.matmul(ps[b][:, 0:HD], at_[:, s % 2, m, j * P:(j + 1) * P],
                                                         vsw[:, m, j, g * HD:(g + 1) * HD], start=m == 0 and j == 0,
                                                         stop=m == 1 and j == n - 1)
                    last.then_inc(full[b], 1)

                scores(0)
                for s in range(8):
                    if s < 7:
                        scores(s + 1)
                    turn(s)
                    if s:
                        values(s - 1)
                values(7)

            pe.wait_ge(in_c, 16 * 12)
            pe.wait_ge(boot, 1)
            norm(0)
            ht_ready("qa")
            for c in range(4):
                gemm_f("qa", c, c)
            gemm_f("kva", 0, 0)
            gemm_n("kva", 1, 1)
            if on("rope_r"):
                rope("rope_r", 2, qkr, 0)
            if on("vg"):
                gemm_t("vg")
            if on("ret"):
                ret = "ret"
                pe.wait_ge(roped, 8)

                def ret_scores(h):
                    for c in range(4):
                        bank_free(ret, c, h)
                        tensor.matmul(ps[c][:, 0:SEQ - c * P], qkr[:, 4 + h, c * P:(c + 1) * P], qkr[:, h, c * P:],
                                      start=True, stop=True).then_inc(full[c], 1)

                def ret_values(h):
                    u = h % 2
                    bank_free(ret, 4 + u, h // 2)
                    for i in range(4):
                        for c in range(i + 1):
                            if i == c:
                                pe.wait_ge(free[c], FREED[ret][c] + h + 1)
                            o = [0, 512, 896, 1152][c]
                            last = tensor.matmul(ps[4 + u][:, i * P:(i + 1) * P], STs[u][:, o + (i - c) * P:o + (i - c + 1) * P],
                                                 vr[:, c, h * P:(h + 1) * P], start=c == 0, stop=c == i)
                    last.then_inc(full[4 + u], 1)

                for b in range(8):
                    pe.wait_ge(free[b], FREED[ret][b])
                ret_scores(0)
                for h in range(4):
                    if h < 3:
                        ret_scores(h + 1)
                    ret_values(h)
            if on("local"):
                for it in range(2):
                    attend("local", it)
            if on("cat"):
                def cat_ready(tt):
                    if tt == 0:
                        pe.wait_ge(cat_ret, 1)
                        for b in (6, 7):
                            pe.wait_ge(free[b], FREED["cat"][b])
                to_ht("cat", CAT, cat_ready)
            if on("out1"):
                ht_ready("out1")
                gemm_t("out1")
            if on("norm1"):
                norm(1)
                ht_ready("up1")
            if on("up1"):
                up("up1")
            if on("down1"):
                down("down1")
            if on("norm2"):
                norm(2)
                ht_ready("up2")
            if on("up2"):
                up("up2")
            if on("down2"):
                down("down2")
            if on("norm3"):
                norm(3)
                ht_ready("rope_dq")
            if on("rope_dq"):
                pe.wait_ge(in_rope, 48)
                rope("rope_dq", 2, qkd, 0)
                rope("rope_dk", 2, qkd, 8)
            if on("vda"):
                gemm_t("vda")
            if on("da"):
                for b in range(8):
                    pe.wait_ge(free[b], FREED["da"][b])
                pe.wait_ge(roped, 24)
                with pe.Fori(0, 4) as it:
                    attend("da", it)
            if on("nsf"):
                for c in range(4):
                    gemm_f("nsf", c, c)
                for c in (2, 3):
                    pe.wait_ge(free[c], FREED["nsf"][c] + 1)
                    rotate("nsf", c, kraw[:, c - 2, :], 0, 1, 2 + c, (0, 0))
            if on("nst"):
                for c in range(3):
                    gemm_n("nst", c, c)
            if on("cmp"):
                pe.wait_ge(in_cw, 80)
                for kv in range(2):
                    pe.wait_ge(cm_a, kv + 1)
                    bank_free("cmp", 4 + kv)
                    cw = (cw1k, cw1v)[kv]
                    for ht in range(2):
                        for j in range(16):
                            last = tensor.matmul(ps[4 + kv][:, ht * 64:ht * 64 + 62], cw[:, j, ht * P:(ht + 1) * P], cA[:, kv, j, :],
                                                 start=j == 0, stop=j == 15)
                    last.then_inc(full[4 + kv], 1)
                pe.wait_ge(free[4], FREED["cmp"][4] + 1)
                bank_free("cmp", 6)
                for ht in range(2):
                    last = tensor.matmul(ps[6][:, 0:62], w2k[:, ht, :, :].rearrange("p a d -> p (a d)"), hid[:, 0, ht, :],
                                         start=ht == 0, stop=ht == 1)
                last.then_inc(full[6], 1)
                pe.wait_ge(free[5], FREED["cmp"][5] + 1)
                bank_free("cmp", 7)
                for g in range(2):
                    for ht in range(2):
                        last = tensor.matmul(ps[7][0:31, g * HD:(g + 1) * HD], hid[:, 1, ht, g * 31:(g + 1) * 31], w2v[:, ht, :],
                                             start=ht == 0, stop=ht == 1)
                last.then_inc(full[7], 1)
            if on("rope_q"):
                rope("rope_q", 2, qn, 0)
            if on("cmpa"):
                st = "cmpa"
                for b in (6, 7):
                    pe.wait_ge(free[b], FREED[st][b])
                for g in range(2):
                    with pe.Fori(0, 2) as it:
                        for u2 in range(2):
                            def cmp_scores():
                                pe.wait_ge(cst_q, it * 2 + (4 * g + u2 + 1))
                                for u in range(2):
                                    b = (u2, 6 + u2)[u]
                                    bank_free(st, b, it + 2 * g)
                                    for i in range(4):
                                        h = slice(64 * u, 64 * u + 64)
                                        col = i * 32
                                        last = tensor.matmul(ps[b][:, col:col + N_CMP], QSc[h, u2, i * P:(i + 1) * P],
                                                             kcT[h, g * 31:(g + 1) * 31], start=True, stop=True)
                                    last.then_inc(full[b], 1)

                            def cmp_turn():
                                pe.wait_ge(cm_p, it * 2 + (4 * g + u2 + 1))
                                for u in range(2):
                                    bank_free(st, 2 + u, it * 2 + (4 * g + u2))
                                    for i in range(4):
                                        last = tensor.matmul(ps[2 + u][0:31, i * P:(i + 1) * P], CP[:, u2, 4 * u + i, 0:N_CMP], ident[:],
                                                             start=True, stop=True)
                                    last.then_inc(full[2 + u], 1)

                            def cmp_values():
                                bank_free(st, 4 + u2, it + 2 * g)
                                for u in range(2):
                                    pe.wait_ge(free[2 + u], it * 2 + (FREED[st][2 + u] + 4 * g + u2 + 1))
                                    for i in range(4):
                                        col = (4 * u + i) * HD
                                        last = tensor.matmul(ps[4 + u2][:, col:col + HD], CA[:, u2, 4 * u + i, :],
                                                             vcm[:, g * HD:(g + 1) * HD], start=True, stop=True)
                                last.then_inc(full[4 + u2], 1)

                            cmp_scores()
                            cmp_turn()
                            cmp_values()
            if on("nsa"):
                for b in range(6):
                    pe.wait_ge(free[b], FREED["nsa"][b])
                for g in range(2):
                    with pe.Fori(0, 4) as it:
                        attend("nsa", it, g)
            if on("ydat"):
                to_ht("ydat", YD, lambda tt: pe.wait_ge(da_fin, tt + 1))
            if on("ga"):
                gemm_t("ga")
            if on("gb"):
                gemm_t("gb")
            if on("ynst"):
                for b in (6, 7):
                    pe.wait_ge(free[b], FREED["ydat"][b])
                to_ht("ynst", YN)
            if on("pda"):
                gemm_t("pda", HT2h, HT2l)
            if on("pns"):
                ht_ready("pda")
                gemm_t("pns")
            if on("mt"):
                to_ht("mt", GA, lambda tt: pe.wait_ge(merged, tt + 1))
            if on("out2"):
                ht_ready("out2")
                gemm_t("out2")
            if on("norm4"):
                norm(4)
                ht_ready("up3")
            if on("up3"):
                up("up3")
            if on("down3"):
                down("down3")

        @block.scalar
        def _(ac):
            def split(k, it=0):
                if isinstance(it, int) and k + 4 * it >= n_chunks:
                    return
                s = k % SLOTS
                ac.wait_ge(w_raw[s], it * 16 + 16 * (k // SLOTS + 1))
                at_least(ac, w_used, it * 4 + (k - SLOTS + 1))
                scalar.copy(Wh[:, s, :], raw[:, s, :]).then_inc(w_hi, 1)

            def chunk_done(stage, c, it=0):
                ac.wait_ge(w_used, it * 4 + (CHUNK0[stage] + c + 1))

            def filled(stage, b, k=0):
                ac.wait_ge(full[b], k + (FILLED[stage][b] + 1))

            def bank_done(stage, tt, half, n=KT):
                b = bank_t(tt, half)
                if b < 7:
                    ac.wait_ge(t_done, 7 * T_STAGES.index(stage) + b + 1)
                else:
                    chunk_done(stage, n - 1)

            def splits_t(stage, n=KT):
                for c in range(n):
                    split(CHUNK0[stage] + c + LEAD)

            def to_ht(stage, dst, gain=None):
                for k in range(KT):
                    filled(stage, k)
                    if gain is None:
                        scalar.copy(dst[:, k, :], ps[k][:]).then_inc(ht_hi, 1)
                    else:
                        scalar.activation(dst[:, k, :], ps[k][:], ACT.Copy, scale=gain(k)).then_inc(ht_hi, 1)

            def norm(i):
                for tt in range(TT):
                    if i == 0:
                        if tt == 0:
                            ac.wait_ge(in_x, 16)
                    else:
                        ac.wait_ge(x_ready, 4 * (i - 1) + tt + 1)
                    scalar.activation(XN[:, tt, :], X[:, tt, :], ACT.Square, accum_out=sst[:, tt:tt + 1])
                scalar.drain()
                scalar.activation(std[:], sst[:], ACT.Sqrt, scale=1.0 / D, bias=eps[:]).then_inc(n_std, 1)
                to_ht(NORMS[i], HTh, lambda k: gains[:, i, k:k + 1])

            def rope(stage, rounds, dst, tile0, factor=1.0):
                with ac.Fori(0, rounds) as it:
                    for c in range(4):
                        split(CHUNK0[stage] + c + LEAD, it)
                        chunk_done(stage, c, it)
                        scalar.activation(dst[:, bass.ds(it * 4 + (tile0 + c), 1), :].rearrange("p a n -> p (a n)"), ps[c][:], ACT.Copy,
                                          scale=factor).then_inc(free[c], 1)

            def residual_squares(stage, n):
                for tt in range(TT):
                    for half in range(2):
                        bank_done(stage, tt, half, n)
                        b = bank_t(tt, half)
                        scalar.activation(XN[:, tt, half * 512:(half + 1) * 512], ps[b][:], ACT.Square,
                                          accum_out=ss[:, b:b + 1]).then_inc(r_sq, 1)
                ac.wait_ge(r_sum, {"out1": 1, "down1": 2}[stage])
                scalar.activation(std[:], sst[:], ACT.Sqrt, scale=1.0 / D, bias=eps[:]).then_inc(r_std, 1)

            def up_conv(stage):
                with ac.Fori(0, FT // 2) as it:
                    for c in range(4):
                        split(CHUNK0[stage] + c + LEAD, it)
                        tile = it * 2 + (c // 2) if c % 2 == 0 else it * 2 + (FT + c // 2)
                        if c % 2 == 0:
                            ac.wait_ge(y_ready, it * 2 + (c // 2 + 1))
                        chunk_done(stage, c, it)
                        cw = conv[:, bass.ds(tile, 1), :].rearrange("p a n -> p (a n)")
                        scalar.activation(U[:, c, :], ps[c][:], ACT.Identity, scale=cw[:, 2:3], bias=cw[:, 3:4]).then_inc(u_ready, 1)
                        if c % 2:
                            ac.wait_ge(free[c - 1], it + (FREED[stage][c - 1] + 1))
                            scalar.activation(GU[:, c // 2, :], U[:, c - 1, :], ACT.Gelu_apprx_tanh).then_inc(g_ready, 1)

            def up_swiglu(stage):
                with ac.Fori(0, FT // 2) as it:
                    for c in range(4):
                        split(CHUNK0[stage] + c + LEAD, it)
                        if c % 2 == 0:
                            at_least(ac, free[c + 1], it + FREED[stage][c + 1])
                            chunk_done(stage, c, it)
                            scalar.activation(GU[:, c // 2, :], ps[c][:], ACT.Silu).then_inc(free[c], 1)

            def down(stage, i):
                for k in range(LEAD):
                    if k == 0:
                        if stage == "down1":
                            ac.wait_ge(y_ready, FT + 2)
                        else:
                            for b in (1, 3):
                                ac.wait_ge(free[b], FREED[stage][b])
                    last = scalar.copy(Yh[:, k, :], Y[:, k, :])
                last.then_inc(y_pre_hi, 1)

                def step(c, it=0):
                    k = c + LEAD
                    if not (isinstance(it, int) and k >= FT):
                        at_least(ac, w_used, it * 4 + (CHUNK0[stage] + k - SLOTS + 1))
                        scalar.copy(Yh[:, k % SLOTS, :], Y[:, bass.ds(it * 4 + k, 1), :].rearrange("p a n -> p (a n)")
                                    if not isinstance(it, int) else Y[:, k, :])
                        if isinstance(it, int) and CHUNK0[stage] + k >= n_chunks:
                            assert False
                    split(CHUNK0[stage] + k, it)

                step(0)
                with ac.Fori(0, 4) as it:
                    for c in range(4):
                        step(1 + c, it)
                for c in range(17, FT):
                    step(c)

            def attend(kind, it, g=0):
                p_, at_ = (Pb, AT) if kind == "local" else (Pb2, AT2)
                steps0 = {"local": 0, "da": 0, "nsa": 32 * g}[kind]

                def half_uses(s):
                    return it * 4 + (steps0 // 2 + s // 2)

                def keys(i):
                    return (max(i - 1, 0), i + 1) if kind == "local" else (0, i + 1)

                def exps(s):
                    k0, k1 = keys(s % 4)
                    w = (k1 - k0) * P
                    u = s % 2
                    ac.wait_ge(mx_done, it * 8 + (STEP0[kind] + steps0 + s + 1))
                    if kind == "local":
                        for m in range(2):
                            hd = 4 * it + 2 * (s // 4) + m
                            scalar.activation(esk[:, u, m:m + 1], sinks[:, hd:hd + 1], ACT.Exp, bias=nmx[:, u, m:m + 1])
                    for m in range(2):
                        b = 2 * u + m
                        scalar.activation(p_[:, u, m, 0:w], ps[b][:, 0:w], ACT.Exp, bias=nmx[:, u, m:m + 1],
                                          accum_out=rs[:, u, m:m + 1]).then_inc(free[b], 1)

                def take_turned(s):
                    k0, k1 = keys(s % 4)
                    w = (k1 - k0) * P
                    u = s % 2
                    if kind == "da":
                        filled(kind, 4 + u, half_uses(s))
                        scalar.copy(at_[:, u, 0, 0:w], ps[4 + u][:, 0:w]).then_inc(free[4 + u], 1)
                    else:
                        filled(kind, 5, it * 8 + (steps0 + s))
                        at_least(ac, full[6 + u], it * 4 + (FILLED[kind][6 + u] + steps0 // 2 + s // 2))
                        scalar.copy(at_[:, u, 1, 0:w], ps[5][:, 0:w]).then_inc(free[5], 1)

                def take_out(s):
                    if kind == "nsa":
                        return
                    i = s % 4
                    filled(kind, 6 + s % 2, half_uses(s))
                    if kind == "da":
                        dst = YD[:, i, bass.ds(it * 256 + 128 * (s // 4), P)]
                    else:
                        tile = 2 * it + s // 4
                        dst = CAT[:, i, tile * P:(tile + 1) * P]
                    scalar.copy(dst, ps[6 + s % 2][:, 0:P]).then_inc(free[6 + s % 2], 1)

                exps(0)
                for s in range(8):
                    if s < 7:
                        exps(s + 1)
                    take_turned(s)
                    if s:
                        take_out(s - 1)
                take_out(7)

            ac.wait_ge(in_c, 16 * 12)
            ac.wait_ge(boot, 1)
            ac.wait_ge(boot2, 1)
            scalar.activation(lam_e[:], lam_s[:], ACT.Exp).then_inc(boot3, 1)
            for n in range(LEAD):
                split(n)
            norm(0)
            for c in range(4):
                split(CHUNK0["qa"] + c + LEAD)
                chunk_done("qa", c)
                scalar.mul(qaT[:, c, :], ps[c][:], HD ** -0.5).then_inc(free[c], 1)
            split(CHUNK0["kva"] + LEAD)
            chunk_done("kva", 0)
            for kv in range(2):
                for half in range(2):
                    last = scalar.copy(kaT[64 * half:64 * half + 64, kv, :], ps[0][64 * kv:64 * kv + 64, :])
            last.then_inc(free[0], 1)
            split(CHUNK0["kva"] + 1 + LEAD)
            chunk_done("kva", 1)
            scalar.copy(va[:].rearrange("p a n -> p (a n)"), ps[1][:]).then_inc(free[1], 1)
            if on("rope_r"):
                rope("rope_r", 2, qkr, 0)
            if on("vg"):
                splits_t("vg")
                for tt in range(TT):
                    bank_done("vg", tt, 1)
                    scalar.activation(sg[:, tt, :], ps[bank_t(tt, 1)][:], ACT.Silu).then_inc(free[bank_t(tt, 1)], 1)
            if on("ret"):
                for h in range(4):
                    filled("ret", 4 + h % 2, h // 2)
                    scalar.copy(CAT[:, :, 512 + h * P:512 + (h + 1) * P], ps[4 + h % 2][:].rearrange("p (i n) -> p i n", i=4)).then_inc(free[4 + h % 2], 1)
                ac.wait_ge(gn_mv, 1)
                scalar.activation(gsd[:], mv[:, :, 1], ACT.Sqrt, bias=eps[:]).then_inc(gn_sd, 1)
            if on("local"):
                for it in range(2):
                    attend("local", it)
            if on("cat"):
                to_ht("cat", HTh)
            if on("out1"):
                splits_t("out1")
                residual_squares("out1", KT)
            if on("norm1"):
                norm(1)
            if on("up1"):
                up_conv("up1")
            if on("down1"):
                down("down1", 1)
                residual_squares("down1", FT)
            if on("norm2"):
                norm(2)
            if on("up2"):
                up_swiglu("up2")
            if on("down2"):
                down("down2", 2)
            if on("norm3"):
                norm(3)
            if on("rope_dq"):
                rope("rope_dq", 2, qkd, 0, HD ** -0.5)
                rope("rope_dk", 2, qkd, 8)
            if on("vda"):
                splits_t("vda")
                for tt in range(TT):
                    bank_done("vda", tt, 1)
                    scalar.copy(vd[:, tt, 512:], ps[bank_t(tt, 1)][:]).then_inc(free[bank_t(tt, 1)], 1)
            if on("da"):
                with ac.Fori(0, 4) as it:
                    attend("da", it)
            if on("nsf"):
                scalar.drain()
                scalar.activation(DSQ[:], YD[:], ACT.Square).then_inc(da_sq, 1)
                ac.wait_ge(da_ss, 1)
                scalar.activation(hsd[:], hss[:], ACT.Sqrt, scale=1.0 / P, bias=eps[:]).then_inc(da_sd, 1)
                for c in range(4):
                    split(CHUNK0["nsf"] + c + LEAD)
                    chunk_done("nsf", c)
                    dst = kcv[:, c, :] if c < 2 else kraw[:, c - 2, :]
                    scalar.copy(dst, ps[c][:]).then_inc(free[c], 1)
            if on("nst"):
                for c in range(3):
                    split(CHUNK0["nst"] + c + LEAD)
                    chunk_done("nst", c)
                    if c < 2:
                        scalar.copy(vsw[:, c, :, :].rearrange("p a n -> p (a n)"), ps[c][:]).then_inc(free[c], 1)
                    else:
                        scalar.activation(gates[:], ps[2][:].rearrange("p (i n) -> p i n", i=4)[:, :, 0:48], ACT.Sigmoid).then_inc(free[2], 1)
            if on("cmp"):
                for kv in range(2):
                    filled("cmp", 4 + kv)
                    scalar.activation(hid[:, kv, :, :], ps[4 + kv][:, 0:128].rearrange("p (a n) -> p a n", a=2)[:, :, 0:62],
                                      ACT.Gelu_apprx_tanh).then_inc(free[4 + kv], 1)
                filled("cmp", 6)
                scalar.copy(kcT[:], ps[6][:, 0:62]).then_inc(free[6], 1)
                filled("cmp", 7)
                scalar.copy(vcm[:], ps[7][0:31, 0:2 * HD]).then_inc(free[7], 1)
            if on("rope_q"):
                rope("rope_q", 2, qn, 0, HD ** -0.5)
            if on("cmpa"):
                st = "cmpa"
                for g in range(2):
                    with ac.Fori(0, 2) as it:
                        for u2 in range(2):
                            ac.wait_ge(cm_s, it * 2 + (4 * g + u2 + 1))
                            scalar.activation(CS[:, u2, :, 0:N_CMP], CS[:, u2, :, 0:N_CMP], ACT.Exp).then_inc(cm_e, 1)
                            filled(st, 2, it * 2 + (4 * g + u2))
                            scalar.copy(CA[:, u2, 0:4, :].rearrange("p a n -> p (a n)"), ps[2][0:31, :]).then_inc(free[2], 1)
                            filled(st, 4 + u2, it + 2 * g)
                            dst = YN[:].rearrange("p i (h d) -> p h i d", d=HD)[:, bass.ds(it * 4 + (8 * g + 2 * u2), 2), :, :]
                            scalar.copy(dst, ps[4 + u2][:].rearrange("p (u i d) -> p u i d", u=2, i=4)).then_inc(free[4 + u2], 1)
            if on("nsa"):
                for g in range(2):
                    with ac.Fori(0, 4) as it:
                        attend("nsa", it, g)
            if on("ydat"):
                to_ht("ydat", HT2h, lambda k: gains[:, 5, k:k + 1])
            if on("ga"):
                splits_t("ga")
                for tt in range(TT):
                    for half in range(2):
                        bank_done("ga", tt, half)
                        scalar.activation(GA[:, tt, half * 512:(half + 1) * 512], ps[bank_t(tt, half)][:], ACT.Sigmoid).then_inc(free[bank_t(tt, half)], 1)
            if on("gb"):
                splits_t("gb")
                for tt in range(TT):
                    for half in range(2):
                        bank_done("gb", tt, half)
                        scalar.activation(GB[:, tt, half * 512:(half + 1) * 512], ps[bank_t(tt, half)][:], ACT.Sigmoid).then_inc(free[bank_t(tt, half)], 1)
            if on("ynst"):
                to_ht("ynst", HTh)
            if on("pda"):
                splits_t("pda")
            if on("pns"):
                splits_t("pns")
            if on("mt"):
                to_ht("mt", HTh)
            if on("out2"):
                splits_t("out2")
            if on("norm4"):
                norm(4)
            if on("up3"):
                up_swiglu("up3")
            if on("down3"):
                down("down3", 3)
                for tt in range(TT):
                    ac.wait_ge(x_ready, 16 + tt + 1)
                    scalar.activation(XN[:, tt, :], X[:, tt, :], ACT.Square, accum_out=sst[:, tt:tt + 1])
                scalar.drain()
                scalar.activation(std[:], sst[:], ACT.Sqrt, scale=1.0 / D, bias=eps[:]).then_inc(n_std, 1)

        @block.vector
        def _(ve):
            def split(k, it=0):
                if isinstance(it, int) and k + 4 * it >= n_chunks:
                    return
                s = k % SLOTS
                ve.wait_ge(w_hi, it * 4 + (k + 1))
                vector.tensor_tensor(Wl[:, s, :], raw[:, s, :], Wh[:, s, :], ALU.subtract).then_inc(w_lo, 1)

            def chunk_done(stage, c, it=0):
                ve.wait_ge(w_used, it * 4 + (CHUNK0[stage] + c + 1))

            def filled(stage, b, k=0):
                ve.wait_ge(full[b], k + (FILLED[stage][b] + 1))

            def bank_done(stage, tt, half, n=KT):
                b = bank_t(tt, half)
                if b < 7:
                    ve.wait_ge(t_done, 7 * T_STAGES.index(stage) + b + 1)
                else:
                    chunk_done(stage, n - 1)

            def splits_t(stage, n=KT):
                for c in range(n):
                    split(CHUNK0[stage] + c + LEAD)

            def to_ht(stage, hi, lo, gain=None):
                for k in range(KT):
                    ve.wait_ge(ht_hi, 8 * HT_STAGES.index(stage) + k + 1)
                    if gain is None:
                        vector.tensor_tensor(lo[:, k, :], ps[k][:], hi[:, k, :], ALU.subtract).then_inc(free[k], 1)
                    else:
                        vector.scalar_tensor_tensor(out=lo[:, k, :], in0=ps[k][:], scalar=gain(k), in1=hi[:, k, :],
                                                    op0=ALU.mult, op1=ALU.subtract).then_inc(free[k], 1)

            def norm(i):
                ve.wait_ge(n_std, i + 1)
                vector.reciprocal(rstd[:], std[:])
                vector.drain()
                for tt in range(TT):
                    vector.tensor_scalar(XN[:, tt, :], X[:, tt, :], rstd[:, tt:tt + 1], None, ALU.mult).then_inc(xn_ready, 1)
                to_ht(NORMS[i], HTh, HTl, lambda k: gains[:, i, k:k + 1])

            def turn_rope(stage, src, dst, bank, use, tmp):
                vector.drain()
                filled(stage, bank, use)
                vector.tensor_tensor(tmp, ps[bank][:], sin[:], ALU.mult).then_inc(free[bank], 1)
                vector.tensor_tensor(dst, src, cos[:], ALU.mult)
                vector.drain()
                vector.tensor_tensor(dst, dst, tmp, ALU.add).then_inc(roped, 1)

            def rope(stage, rounds, src, dst, tmp, tile0=0):
                with ve.Fori(0, rounds) as it:
                    for c in range(4):
                        split(CHUNK0[stage] + c + LEAD, it)
                        tile = bass.ds(it * 4 + (tile0 + c), 1)
                        turn_rope(stage, src[:, tile, :].rearrange("p a n -> p (a n)"), dst[:, tile, :].rearrange("p a n -> p (a n)"),
                                  4 + c % 2, it * 2 + c // 2, tmp[:])

            def residual(stage, i, n):
                for tt in range(TT):
                    for half in range(2):
                        b = bank_t(tt, half)
                        ve.wait_ge(r_sq, 8 * i + b + 1)
                        if b == 0:
                            ve.wait_ge(in_post, 16 * (i + 1))
                        h = slice(half * 512, (half + 1) * 512)
                        vector.tensor_tensor(XN[:, tt, h], ps[b][:], gpost[:, h], ALU.mult).then_inc(free[b], 1)
                vector.tensor_tensor(sst[:], ss[:].rearrange("p (t a) -> p t a", a=2)[:, :, 0], ss[:].rearrange("p (t a) -> p t a", a=2)[:, :, 1],
                                     ALU.add).then_inc(r_sum, 1)
                vector.drain().then_inc(post_used, 1)
                ve.wait_ge(r_std, i + 1)
                vector.reciprocal(rstd[:], std[:])
                vector.drain()
                for tt in range(TT):
                    vector.scalar_tensor_tensor(out=X[:, tt, :], in0=XN[:, tt, :], scalar=rstd[:, tt:tt + 1], in1=X[:, tt, :],
                                                op0=ALU.mult, op1=ALU.add).then_inc(x_ready, 1)

            def residual_plain(stage, factor, n):
                for tt in range(TT):
                    for half in range(2):
                        bank_done(stage, tt, half, n)
                        h = slice(half * 512, (half + 1) * 512)
                        vector.scalar_tensor_tensor(out=X[:, tt, h], in0=ps[bank_t(tt, half)][:], scalar=factor, in1=X[:, tt, h],
                                                    op0=ALU.mult, op1=ALU.add).then_inc(free[bank_t(tt, half)], 1)
                    vector.drain().then_inc(x_ready, 1)

            def up_conv(stage):
                with ve.Fori(0, FT // 2) as it:
                    for c in range(4):
                        split(CHUNK0[stage] + c + LEAD, it)
                        tile = it * 2 + (c // 2) if c % 2 == 0 else it * 2 + (FT + c // 2)
                        cw = conv[:, bass.ds(tile, 1), :].rearrange("p a n -> p (a n)")
                        ve.wait_ge(u_ready, it * 4 + (c + 1))
                        vector.scalar_tensor_tensor(out=U[:, c, 1:], in0=ps[c][:, 0:SEQ - 1], scalar=cw[:, 1:2], in1=U[:, c, 1:],
                                                    op0=ALU.mult, op1=ALU.add)
                        vector.drain()
                        vector.scalar_tensor_tensor(out=U[:, c, 2:], in0=ps[c][:, 0:SEQ - 2], scalar=cw[:, 0:1], in1=U[:, c, 2:],
                                                    op0=ALU.mult, op1=ALU.add).then_inc(free[c], 1)
                        if c % 2:
                            vector.drain()
                            ve.wait_ge(g_ready, it * 2 + (c // 2 + 1))
                            vector.tensor_tensor(Y[:, bass.ds(it * 2 + c // 2, 1), :].rearrange("p a n -> p (a n)"), GU[:, c // 2, :], U[:, c, :],
                                                 ALU.mult).then_inc(y_ready, 1)

            def up_swiglu(stage):
                with ve.Fori(0, FT // 2) as it:
                    for c in range(4):
                        split(CHUNK0[stage] + c + LEAD, it)
                        if c % 2:
                            ve.wait_ge(free[c - 1], it + (FREED[stage][c - 1] + 1))
                            chunk_done(stage, c, it)
                            vector.tensor_tensor(Y[:, bass.ds(it * 2 + c // 2, 1), :].rearrange("p a n -> p (a n)"), ps[c][:], GU[:, c // 2, :],
                                                 ALU.mult).then_inc(free[c], 1)

            def down(stage, i):
                ve.wait_ge(y_pre_hi, i)
                for k in range(LEAD):
                    last = vector.tensor_tensor(Yl[:, k, :], Y[:, k, :], Yh[:, k, :], ALU.subtract)
                last.then_inc(y_pre, 1)

                def step(c, it=0):
                    k = c + LEAD
                    if not (isinstance(it, int) and k >= FT):
                        ve.wait_ge(w_hi, it * 4 + (CHUNK0[stage] + k + 1))
                        src = Y[:, k, :] if isinstance(it, int) else Y[:, bass.ds(it * 4 + k, 1), :].rearrange("p a n -> p (a n)")
                        vector.tensor_tensor(Yl[:, k % SLOTS, :], src, Yh[:, k % SLOTS, :], ALU.subtract)
                    split(CHUNK0[stage] + k, it)

                step(0)
                with ve.Fori(0, 4) as it:
                    for c in range(4):
                        step(1 + c, it)
                for c in range(17, FT):
                    step(c)

            def attend(kind, it, g=0):
                p_, at_ = (Pb, AT) if kind == "local" else (Pb2, AT2)
                steps0 = {"local": 0, "da": 0, "nsa": 32 * g}[kind]

                def half_uses(s):
                    return it * 4 + (steps0 // 2 + s // 2)

                def keys(i):
                    return (max(i - 1, 0), i + 1) if kind == "local" else (0, i + 1)

                def maxima(s):
                    k0, k1 = keys(s % 4)
                    w = (k1 - k0) * P
                    u = s % 2
                    for m in range(2):
                        filled(kind, 2 * u + m, half_uses(s))
                        last = vector.tensor_reduce(nmx[:, u, m:m + 1], ps[2 * u + m][:, 0:w], AX.X, ALU.max, negate=True)
                    if kind == "local":
                        vector.drain()
                        hd = 4 * it + 2 * (s // 4)
                        last = vector.tensor_tensor(nmx[:, u, :], nmx[:, u, :], nsinks[:, hd:hd + 2], ALU.min)
                    last.then_inc(mx_done, 1)

                def weigh(s):
                    i = s % 4
                    k0, k1 = keys(i)
                    w = (k1 - k0) * P
                    u = s % 2
                    ve.wait_ge(free[2 * u + 1], half_uses(s) + (FREED[kind][2 * u + 1] + 1))
                    ve.wait_ge(free[2 * u], half_uses(s) + (FREED[kind][2 * u] + 1))
                    if kind == "local":
                        vector.tensor_tensor(rs[:, u, :], rs[:, u, :], esk[:, u, :], ALU.add)
                        vector.drain()
                    vector.reciprocal(rr[:, u, :], rs[:, u, :])
                    vector.drain()
                    if kind == "da":
                        vector.tensor_tensor(gg[:, u, 0:1], rr[:, u, 1:2], nlam[:], ALU.mult)
                        vector.tensor_scalar(p_[:, u, 0, 0:w], p_[:, u, 0, 0:w], rr[:, u, 0:1], None, ALU.mult)
                        vector.drain()
                        vector.scalar_tensor_tensor(out=p_[:, u, 0, 0:w], in0=p_[:, u, 1, 0:w], scalar=gg[:, u, 0:1], in1=p_[:, u, 0, 0:w],
                                                    op0=ALU.mult, op1=ALU.add).then_inc(a_ready, 1)
                        return
                    f = rr
                    if kind == "nsa":
                        gt = gates[:, i, bass.ds(it * 6 + (24 * g + 3 * (s // 4) + 1), 2)]
                        vector.tensor_tensor(gg[:, u, :], rr[:, u, :], gt, ALU.mult)
                        vector.drain()
                        f = gg
                    for m in range(2):
                        last = vector.tensor_scalar(p_[:, u, m, 0:w], p_[:, u, m, 0:w], f[:, u, m:m + 1], None, ALU.mult)
                    last.then_inc(a_ready, 1)

                def take_turned(s):
                    if kind == "da":
                        return
                    k0, k1 = keys(s % 4)
                    w = (k1 - k0) * P
                    u = s % 2
                    filled(kind, 4, it * 8 + (steps0 + s))
                    at_least(ve, full[6 + u], it * 4 + (FILLED[kind][6 + u] + steps0 // 2 + s // 2))
                    vector.tensor_copy(at_[:, u, 0, 0:w], ps[4][:, 0:w]).then_inc(free[4], 1)

                def take_out(s):
                    if kind != "nsa":
                        return
                    i = s % 4
                    filled(kind, 6 + s % 2, half_uses(s))
                    dst = YN[:, i, bass.ds(it * 128 + (512 * g + 64 * (s // 4)), HD)]
                    vector.tensor_tensor(dst, ps[6 + s % 2][:, 0:HD], dst, ALU.add).then_inc(free[6 + s % 2], 1)

                maxima(0)
                for s in range(8):
                    if s < 7:
                        maxima(s + 1)
                    weigh(s)
                    take_turned(s)
                    if s:
                        take_out(s - 1)
                take_out(7)

            vector.memset(eps[:], EPS)
            vector.drain().then_inc(y_ready, 1)
            vector.drain().then_inc(y_ready, 1)
            ve.wait_ge(in_c, 16 * 12)
            vector.tensor_copy(identb[:], masks_f[:, 2, :])
            vector.tensor_copy(causal[:], masks_f[:, 0, :])
            vector.tensor_copy(outside[:], masks_f[:, 1, :])
            vector.tensor_scalar(nsinks[:], sinks[:], -1.0, None, ALU.mult)
            vector.tensor_tensor(lam_pr[:], lam_in[:, :, 0, :], lam_in[:, :, 1, :], ALU.mult)
            vector.tensor_scalar(gains[:, 5, :], gains[:, 5, :], 1.0 - LAM_INIT, None, ALU.mult)
            vector.drain().then_inc(boot, 1)
            vector.tensor_reduce(lam_s[:], lam_pr[:], AX.X, ALU.add).then_inc(boot2, 1)
            for n in range(LEAD):
                split(n)
            norm(0)
            ve.wait_ge(boot3, 1)
            vector.tensor_tensor(nlam[:], lam_e[:, 1:2], lam_e[:, 0:1], ALU.subtract)
            vector.drain()
            vector.tensor_scalar(nlam[:], nlam[:], LAM_INIT, None, ALU.subtract)
            for c in range(4):
                split(CHUNK0["qa"] + c + LEAD)
            for c in range(2):
                split(CHUNK0["kva"] + c + LEAD)
            if on("rope_r"):
                rope("rope_r", 2, qkr, qkr, rtmp)
            if on("vg"):
                splits_t("vg")
                for tt in range(TT):
                    bank_done("vg", tt, 0)
                    vector.tensor_copy(vr[:, tt, :], ps[bank_t(tt, 0)][:]).then_inc(free[bank_t(tt, 0)], 1)
            if on("ret"):
                def decayed(h):
                    if h >= 2:
                        filled("ret", 4 + h % 2, h // 2 - 1)
                    for c in range(4):
                        filled("ret", c, h)
                        w = SEQ - c * P
                        o = [0, 512, 896, 1152][c]
                        vector.tensor_tensor(STs[h % 2][:, o:o + w], ps[c][:, 0:w], decay[:, h, 0:w], ALU.mult).then_inc(free[c], 1)

                def stats(h):
                    ve.wait_ge(free[4 + h % 2], FREED["ret"][4 + h % 2] + h // 2 + 1)
                    for i in range(4):
                        vector.bn_stats(bn[:, 4 * h + i, :], CAT[:, i, 512 + h * P:512 + (h + 1) * P])
                    vector.drain()
                    for i in range(4):
                        vector.bn_aggr(mv[:, 4 * h + i, :], bn[:, 4 * h + i, :])

                decayed(0)
                for h in range(4):
                    if h < 3:
                        decayed(h + 1)
                    stats(h)
                vector.drain().then_inc(gn_mv, 1)
                ve.wait_ge(gn_sd, 1)
                vector.reciprocal(grs[:], gsd[:])
                vector.drain()
                for h in range(4):
                    for i in range(4):
                        blk = CAT[:, i, 512 + h * P:512 + (h + 1) * P]
                        vector.tensor_scalar(blk, blk, mv[:, 4 * h + i, 0:1], grs[:, 4 * h + i:4 * h + i + 1], ALU.subtract, ALU.mult)
                vector.drain()
                for b in (1, 3, 5, 7):
                    ve.wait_ge(free[b], FREED["ret"][b])
                vector.tensor_tensor(CAT[:, :, 512:], CAT[:, :, 512:], sg[:], ALU.mult).then_inc(cat_ret, 1)
            if on("local"):
                for it in range(2):
                    attend("local", it)
            if on("cat"):
                to_ht("cat", HTh, HTl)
            if on("out1"):
                splits_t("out1")
                residual("out1", 0, KT)
            if on("norm1"):
                norm(1)
            if on("up1"):
                up_conv("up1")
            if on("down1"):
                down("down1", 1)
                residual("down1", 1, FT)
            if on("norm2"):
                norm(2)
            if on("up2"):
                up_swiglu("up2")
            if on("down2"):
                down("down2", 2)
                residual_plain("down2", 0.5, FT)
            if on("norm3"):
                norm(3)
            if on("rope_dq"):
                ve.wait_ge(in_rope, 48)
                rope("rope_dq", 2, qkd, qkd, rtmp2)
                rope("rope_dk", 2, qkd, qkd, rtmp2, 8)
            if on("vda"):
                splits_t("vda")
                for tt in range(TT):
                    bank_done("vda", tt, 0)
                    vector.tensor_copy(vd[:, tt, 0:512], ps[bank_t(tt, 0)][:]).then_inc(free[bank_t(tt, 0)], 1)
            if on("da"):
                with ve.Fori(0, 4) as it:
                    attend("da", it)
            if on("nsf"):
                ve.wait_ge(da_sq, 1)
                vector.tensor_reduce(hss[:], DSQ[:].rearrange("p i (h d) -> p (i h) d", d=P), AX.X, ALU.add).then_inc(da_ss, 1)
                ve.wait_ge(da_sd, 1)
                vector.reciprocal(hrs[:], hsd[:])
                vector.drain()
                for i in range(TT):
                    r = hrs[:, i * 8:(i + 1) * 8].rearrange("p (h a) -> p h a", a=1).broadcast_to((P, 8, P))
                    blk = YD[:, i, :].rearrange("p (h d) -> p h d", d=P)
                    vector.tensor_tensor(blk, blk, r, ALU.mult).then_inc(da_fin, 1)
                for c in range(4):
                    split(CHUNK0["nsf"] + c + LEAD)
                for kind in range(2):
                    vector.drain()
                    filled("nsf", 4 + kind)
                    vector.tensor_tensor(rtmp2[:], ps[4 + kind][:], sin[:], ALU.mult).then_inc(free[4 + kind], 1)
                    vector.tensor_tensor(kraw[:, kind, :], kraw[:, kind, :], cos[:], ALU.mult)
                    vector.drain()
                    for g in range(2):
                        for half in range(2):
                            last = vector.tensor_tensor(ksw[64 * half:64 * half + 64, kind, g, :], kraw[64 * g:64 * g + 64, kind, :],
                                                        rtmp2[64 * g:64 * g + 64, :], ALU.add)
                    last.then_inc(roped, 1)
            if on("nst"):
                for c in range(3):
                    split(CHUNK0["nst"] + c + LEAD)
            if on("cmp"):
                ve.wait_ge(in_cw, 80)
                for kv in range(2):
                    ve.wait_ge(free[kv], FREED["nst"][kv])
                    for jp in range(2):
                        for g in range(2):
                            h = slice(64 * g, 64 * g + 64)
                            src = kcv[h, kv, :].rearrange("p (n r a) -> p r n a", r=8, a=2)
                            for part in range(2):
                                x = src[:, :, part:part + N_CMP, jp]
                                pz = posT[h, kv, 16 * part:16 * part + 16].rearrange("p (j a) -> p j a", a=2)[:, :, jp:jp + 1].broadcast_to((64, 8, N_CMP))
                                last = vector.tensor_tensor(cA[64 * jp:64 * jp + 64, kv, 8 * part:8 * part + 8, g * 31:(g + 1) * 31], x, pz, ALU.add)
                    last.then_inc(cm_a, 1)
            if on("rope_q"):
                rope("rope_q", 2, qn, qnr, rtmp2)
            if on("cmpa"):
                st = "cmpa"
                for g in range(2):
                    with ve.Fori(0, 2) as it:
                        for u2 in range(2):
                            s_ = CS[:, u2, :, 0:N_CMP]
                            s4 = s_.rearrange("p (u i) n -> p u i n", u=2)
                            mx, sm, rc, ge = (cst[:, u2, j, :] for j in range(4))

                            def wide(a):
                                return a.rearrange("p (n a) -> p n a", a=1).broadcast_to((P, 8, N_CMP))

                            for u in range(2):
                                b = (u2, 6 + u2)[u]
                                filled(st, b, it + 2 * g)
                                vector.tensor_tensor(CS[:, u2, 4 * u:4 * u + 4, 0:N_CMP],
                                                     ps[b][:, 0:128].rearrange("p (i n) -> p i n", n=32)[:, :, 0:N_CMP],
                                                     cmask[:], ALU.add).then_inc(free[b], 1)
                            vector.drain()
                            vector.tensor_reduce(mx, s_, AX.X, ALU.max)
                            vector.drain()
                            vector.tensor_tensor(s_, s_, wide(mx), ALU.subtract).then_inc(cm_s, 1)
                            ve.wait_ge(cm_e, it * 2 + (4 * g + u2 + 1))
                            vector.tensor_reduce(sm, s_, AX.X, ALU.add)
                            vector.drain()
                            vector.reciprocal(rc, sm)
                            vector.drain()
                            for u in range(2):
                                gt = gates[:, :, bass.ds(it * 12 + (24 * g + 6 * u2 + 3 * u), 1)].rearrange("p i a -> p (i a)")
                                vector.tensor_tensor(ge[:, 4 * u:4 * u + 4], rc[:, 4 * u:4 * u + 4], gt, ALU.mult)
                            vector.drain()
                            for u in range(2):
                                vector.tensor_tensor(ge[:, 4 * u:4 * u + 4], ge[:, 4 * u:4 * u + 4], cvalid[:], ALU.mult)
                            vector.drain()
                            vector.tensor_tensor(CP[:, u2, :, 0:N_CMP], s_, wide(ge), ALU.mult).then_inc(cm_p, 1)
                            filled(st, 3, it * 2 + (4 * g + u2))
                            vector.tensor_copy(CA[:, u2, 4:8, :].rearrange("p a n -> p (a n)"), ps[3][0:31, :]).then_inc(free[3], 1)
            if on("nsa"):
                for g in range(2):
                    with ve.Fori(0, 4) as it:
                        attend("nsa", it, g)
            if on("ydat"):
                to_ht("ydat", HT2h, HT2l, lambda k: gains[:, 5, k:k + 1])
            if on("ga"):
                splits_t("ga")
            if on("gb"):
                splits_t("gb")
            if on("ynst"):
                to_ht("ynst", HTh, HTl)
            if on("pda"):
                splits_t("pda")
                for tt in range(TT):
                    for half in range(2):
                        bank_done("pda", tt, half)
                        h = slice(half * 512, (half + 1) * 512)
                        vector.tensor_tensor(GA[:, tt, h], ps[bank_t(tt, half)][:], GA[:, tt, h], ALU.mult).then_inc(free[bank_t(tt, half)], 1)
            if on("pns"):
                splits_t("pns")
                for tt in range(TT):
                    for half in range(2):
                        bank_done("pns", tt, half)
                        h = slice(half * 512, (half + 1) * 512)
                        vector.tensor_tensor(GB[:, tt, h], ps[bank_t(tt, half)][:], GB[:, tt, h], ALU.mult).then_inc(free[bank_t(tt, half)], 1)
                    vector.drain()
                    vector.tensor_tensor(GA[:, tt, :], GA[:, tt, :], GB[:, tt, :], ALU.add).then_inc(merged, 1)
            if on("mt"):
                to_ht("mt", HTh, HTl)
            if on("out2"):
                splits_t("out2")
                residual_plain("out2", 1.0, KT)
            if on("norm4"):
                norm(4)
            if on("up3"):
                up_swiglu("up3")
            if on("down3"):
                down("down3", 3)
                residual_plain("down3", 0.5, FT)
                ve.wait_ge(n_std, 6)
                ve.wait_ge(in_post, 48)
                vector.reciprocal(rstd[:], std[:])
                vector.drain()
                for tt in range(TT):
                    vector.scalar_tensor_tensor(out=XN[:, tt, :], in0=X[:, tt, :], scalar=rstd[:, tt:tt + 1], in1=gpost[:],
                                                op0=ALU.mult, op1=ALU.mult).then_inc(f_out, 1)


def constants():
    pos = np.arange(SEQ, dtype=np.float32)
    c = {}
    c["c_ident"] = np.eye(P, dtype=np.float32)
    q, k = np.arange(P)[:, None], np.arange(P)[None, :]
    masks = np.zeros((P, 3, P), np.float32)
    masks[:, 0] = np.where(k > q, NEG, 0)
    masks[:, 1] = np.where(k <= q, NEG, 0)
    masks[:, 2] = np.eye(P)
    c["c_masks"] = masks
    pr = np.zeros((P, P), np.float32)
    i = np.arange(0, P, 2)
    pr[i + 1, i] = -1
    pr[i, i + 1] = 1
    c["c_perm_r"] = pr
    pn = np.zeros((P, P), np.float32)
    for b in (0, 64):
        i = b + np.arange(32)
        pn[i + 32, i] = -1
        pn[i, i + 32] = 1
    c["c_perm_n"] = pn
    ang = (np.float32(1) / np.power(np.float32(10000), np.linspace(0, 1, 64, dtype=np.float32))).astype(np.float32)
    a = (pos[:, None] * np.repeat(ang, 2)[None]).astype(np.float32).astype(np.float64).T
    c["c_cos_r"], c["c_sin_r"] = np.cos(a).astype(np.float32), np.sin(a).astype(np.float32)
    inv = (np.float32(1) / np.power(np.float32(10000), np.arange(0, 64, 2, dtype=np.float32) / np.float32(64))).astype(np.float32)
    a = (pos[:, None] * np.tile(inv, 4)[None]).astype(np.float32).astype(np.float64).T
    c["c_cos_n"], c["c_sin_n"] = np.cos(a).astype(np.float32), np.sin(a).astype(np.float32)
    dec = np.zeros((P, 4, SEQ), np.float64)
    for h in range(4):
        lg = np.log(1 - 2.0 ** (-5 - h))
        rel = np.arange(SEQ)[None, :] - np.arange(P)[:, None]
        dec[:, h] = np.where(rel >= 0, np.exp(lg * np.maximum(rel, 0)), 0) * P ** -0.5
    c["c_decay"] = dec.astype(np.float32)
    tok = (np.arange(TT)[None, :, None] * P + np.arange(P)[:, None, None])
    end = np.arange(N_CMP)[None, None, :] * 16 + 31
    c["c_cmask"] = np.where(end <= tok, 0, NEG).astype(np.float32)
    c["c_cvalid"] = (tok[:, :, 0] >= 31).astype(np.float32)
    return c


def weight_order(inp):
    def f(w, c0, n):
        for j in range(n):
            part = w[:, c0 + j * P:min(c0 + (j + 1) * P, w.shape[1])]
            yield part

    chunks = []

    def add_f(w, c0, width=P):
        part = w[:, c0:c0 + width]
        if width < P:
            part = np.pad(part, ((0, 0), (0, P - width)))
        chunks.append(part.reshape(KT, P, P).transpose(1, 0, 2).reshape(P, CHUNK))

    def add_t(w, c0=0):
        for k in range(w.shape[0] // P):
            chunks.append(w[k * P:(k + 1) * P, c0:c0 + CHUNK])

    w = inp["w_in"][0]
    for c in (0, 128, 256, 384, 512, 640):
        add_f(w, c)
    for c in range(768, 1792, P):
        add_f(w, c)
    add_t(w, 1792)
    add_t(inp["w_out"][0])
    for j in range(FT):
        add_f(inp["w_up"][0], j * P)
        add_f(inp["w_up"][0], D_FF + j * P)
    add_t(inp["w_down"][0])
    for j in range(FT):
        add_f(inp["ffn1_w1_2"][0], j * P)
        add_f(inp["ffn1_w3_2"][0], j * P)
    add_t(inp["ffn1_w2_2"][0])
    w = inp["w_in_2"][0]
    for c in range(0, 2048, P):
        add_f(w, c)
    add_t(w, 2048)
    for c in (4096, 4224, 4352, 4608, 4480, 4736):
        add_f(w, c)
    add_f(w, 4864, 48)
    for c in range(3072, 4096, P):
        add_f(w, c)
    add_t(w, 4912)
    add_t(w, 5936)
    add_t(inp["w_proj_da_2"][0])
    add_t(inp["w_proj_nsa_2"][0])
    add_t(inp["w_out_2"][0])
    for j in range(FT):
        add_f(inp["ffn2_w1_2"][0], j * P)
        add_f(inp["ffn2_w3_2"][0], j * P)
    add_t(inp["ffn2_w2_2"][0])
    assert len(chunks) == N_CHUNKS
    return np.stack(chunks)


def laid_out(inp):
    a = dict(constants())
    a["x"] = inp["x"][0]
    a["w_all"] = weight_order(inp)

    def cols(v):
        return v.reshape(-1, P).T

    g = [inp["mix_pre_norm"][0], inp["ffn_pre_norm"][0], inp["ffn1_norm_2"][0], inp["mix_norm_2"][0], inp["ffn2_norm_2"][0],
         inp["da_head_norm_2"][0].reshape(-1)]
    a["gains"] = np.stack([cols(v) for v in g], axis=1)
    a["conv"] = np.stack([cols(inp["conv_w"][0][j]) for j in range(3)] + [cols(inp["conv_b"][0])], axis=2)
    a["attn_sinks"] = inp["attn_sinks"][0]
    a["da_lambda"] = inp["da_lambda_2"][0].reshape(-1)
    a["mix_post"], a["ffn_post"], a["final"] = inp["mix_post_norm"][0], inp["ffn_post_norm"][0], inp["final_norm_2"]
    pt = inp["cmp_pos_2"][0].transpose(2, 0, 1)
    a["posT"] = np.concatenate([pt, pt], axis=0)
    a["cw1"] = inp["cmp_w1_2"][0]
    w2 = inp["cmp_w2_2"][0].reshape(2, 2, P, HD).transpose(2, 0, 1, 3)
    a["w2k"] = np.repeat(w2[:, 0][:, :, None, :], 2, axis=2)
    a["w2v"] = w2[:, 1]
    return {k: np.ascontiguousarray(v) for k, v in a.items()}


STOP = None


def kernel(**inputs):
    import concourse.bacc as bacc
    from concourse.bass_utils import run_bass_kernel_spmd

    nc = bacc.Bacc("TRN2", target_bir_lowering=False, num_devices=1)
    arrays = laid_out({k: np.asarray(v) for k, v in inputs.items()})
    t = {k: nc.dram_tensor("in_" + k, v.shape, mybir.dt.from_np(v.dtype), kind="ExternalInput").ap() for k, v in arrays.items()}
    out = nc.dram_tensor("out", (SEQ, D), F32, kind="ExternalOutput").ap()
    program(nc, t, out, STOP)
    r = run_bass_kernel_spmd(nc, [{"in_" + k: v for k, v in arrays.items()}], core_ids=[0])
    return r.results[0]["out"].reshape(1, SEQ, D)
```

```python
from contextlib import ExitStack

import numpy as np

import concourse.bass as bass
from concourse import mybir

F32 = mybir.dt.float32
F32R = mybir.dt.float32r
BF16 = mybir.dt.bfloat16
ACT = mybir.ActivationFunctionType
ALU = mybir.AluOpType
AX = mybir.AxisListType

P = 128
SEQ = 512
D = 1024
TT = SEQ // P
KT = D // P
D_FF = 2816
FT = D_FF // P
CHUNK = 1024
SLOTS = 4
LEAD = 3
EPS = 1e-6
NEG = -1e30
HD = 64
N_CMP = 31
NSA_HEADS = 16
LAM_INIT = 0.2

STAGES = [
    ("norm0", 0, [0] * 8, [1] * 8),
    ("qa", 4, [1, 1, 1, 1, 0, 0, 0, 0], [0] * 8),
    ("kva", 2, [1, 1, 0, 0, 0, 0, 0, 0], [0] * 8),
    ("rope_r", 8, [2, 2, 2, 2, 0, 0, 0, 0], [0, 0, 0, 0, 4, 4, 0, 0]),
    ("vg", 8, [1] * 8, [0] * 8),
    ("ret", 0, [0] * 8, [4, 4, 4, 4, 2, 2, 0, 0]),
    ("local", 0, [0] * 8, [8, 8, 8, 8, 16, 16, 8, 8]),
    ("cat", 0, [0] * 8, [1] * 8),
    ("out1", 8, [1] * 8, [0] * 8),
    ("norm1", 0, [0] * 8, [1] * 8),
    ("up1", 2 * FT, [FT // 2] * 4 + [0] * 4, [0] * 8),
    ("down1", FT, [1] * 8, [0] * 8),
    ("norm2", 0, [0] * 8, [1] * 8),
    ("up2", 2 * FT, [FT // 2] * 4 + [0] * 4, [0] * 8),
    ("down2", FT, [1] * 8, [0] * 8),
    ("norm3", 0, [0] * 8, [1] * 8),
    ("rope_dq", 8, [2, 2, 2, 2, 0, 0, 0, 0], [0, 0, 0, 0, 4, 4, 0, 0]),
    ("rope_dk", 8, [2, 2, 2, 2, 0, 0, 0, 0], [0, 0, 0, 0, 4, 4, 0, 0]),
    ("vda", 8, [1] * 8, [0] * 8),
    ("da", 0, [0] * 8, [16, 16, 16, 16, 16, 16, 16, 16]),
    ("nsf", 4, [1, 1, 1, 1, 0, 0, 0, 0], [0, 0, 0, 0, 1, 1, 0, 0]),
    ("nst", 3, [1, 1, 1, 0, 0, 0, 0, 0], [0] * 8),
    ("cmp", 0, [0] * 8, [0, 0, 0, 0, 1, 1, 1, 1]),
    ("rope_q", 8, [2, 2, 2, 2, 0, 0, 0, 0], [0, 0, 0, 0, 4, 4, 0, 0]),
    ("cmpa", 0, [0] * 8, [4] * 8),
    ("nsa", 0, [0] * 8, [32, 32, 32, 32, 64, 64, 32, 32]),
    ("ydat", 0, [0] * 8, [1] * 8),
    ("ga", 8, [1] * 8, [0] * 8),
    ("gb", 8, [1] * 8, [0] * 8),
    ("ynst", 0, [0] * 8, [1] * 8),
    ("pda", 8, [1] * 8, [0] * 8),
    ("pns", 8, [1] * 8, [0] * 8),
    ("mt", 0, [0] * 8, [1] * 8),
    ("out2", 8, [1] * 8, [0] * 8),
    ("norm4", 0, [0] * 8, [1] * 8),
    ("up3", 2 * FT, [FT // 2] * 4 + [0] * 4, [0] * 8),
    ("down3", FT, [1] * 8, [0] * 8),
]
T_STAGES = ["vg", "out1", "down1", "down2", "vda", "ga", "gb", "pda", "pns", "out2", "down3"]
NORMS = ["norm0", "norm1", "norm2", "norm3", "norm4"]
HT_STAGES = ["norm0", "cat", "norm1", "norm2", "norm3", "ydat", "ynst", "mt", "norm4"]


def counts():
    chunk, freed, filled = {}, {}, {}
    c, fr, fi = 0, [0] * 8, [0] * 8
    for name, n, streamed, other in STAGES:
        chunk[name], freed[name], filled[name] = c, list(fr), list(fi)
        c += n
        fr = [a + b + d for a, b, d in zip(fr, streamed, other)]
        fi = [a + b for a, b in zip(fi, other)]
    return chunk, freed, filled, c


CHUNK0, FREED, FILLED, N_CHUNKS = counts()


def at_least(eng, sem, value):
    if isinstance(value, int) and value <= 0:
        return
    eng.wait_ge(sem, value)


def program(nc, t, out, stop=None):
    scalar, vector, tensor, pool = nc.scalar, nc.vector, nc.tensor, nc.gpsimd
    names = [s[0] for s in STAGES]
    last_stage = len(names) if stop is None else names.index(stop)

    def on(name):
        return names.index(name) < last_stage

    n_chunks = N_CHUNKS if stop is None else CHUNK0[stop]

    with ExitStack() as ctx:
        def sb(name, shape, dt=F32):
            return ctx.enter_context(nc.sbuf_tensor(name, shape, dt))

        def sem(name):
            return ctx.enter_context(nc.semaphore(name))

        X = sb("X", [P, TT, D])
        HTh = sb("HTh", [P, KT, SEQ], F32R)
        HTl = sb("HTl", [P, KT, SEQ], F32R)
        raw = sb("raw", [P, SLOTS, CHUNK])
        Wh = sb("Wh", [P, SLOTS, CHUNK], F32R)
        Wl = sb("Wl", [P, SLOTS, CHUNK], F32R)
        ident = sb("ident", [P, P])
        identb = sb("identb", [P, P], BF16)
        causal = sb("causal", [P, P], BF16)
        outside = sb("outside", [P, P], BF16)
        perm = sb("perm", [P, P])
        gains = sb("gains", [P, 6, KT])
        conv = sb("conv", [P, 2 * FT, 4])
        sinks = sb("sinks", [P, 8])
        nsinks = sb("nsinks", [P, 8])
        sk = sb("sk", [P, 2, 2])
        cst = sb("cst", [P, 2, 3, 8])
        lam_pr = sb("lam_pr", [P, 2, HD])
        lam_s = sb("lam_s", [P, 2])
        lam_e = sb("lam_e", [P, 2])
        nlam = sb("nlam", [P, 1])
        cmask = sb("cmask", [P, TT, N_CMP])
        cvalid = sb("cvalid", [P, TT])
        eps = sb("eps", [P, 1])
        ss = sb("ss", [P, 8])
        sst = sb("sst", [P, TT])
        std = sb("std", [P, TT])
        rstd = sb("rstd", [P, TT])
        nmx = sb("nmx", [P, 2, 2])
        rs = sb("rs", [P, 2, 2])
        esk = sb("esk", [P, 2, 2])
        rr = sb("rr", [P, 4, 2])
        gg = sb("gg", [P, 4, 2])
        bn = sb("bn", [P, 16, 6])
        mv = sb("mv", [P, 16, 2])
        gsd = sb("gsd", [P, 16])
        grs = sb("grs", [P, 16])
        hss = sb("hss", [P, 32])
        hsd = sb("hsd", [P, 32])
        hrs = sb("hrs", [P, 32])

        K = 1024
        spare = (nc.sbuf_base + 31) // 32 * 32
        region = spare + 8 * K
        limit = nc.sbuf_usable_end

        def at(name, kib, shape, dt=F32):
            off = region + int(kib * K)
            size = int(np.prod(shape[1:])) * 4
            assert off + size <= limit, (name, off + size, limit)
            return nc.alloc_sbuf_tensor_at(name, shape, dt, offset=off)

        gpost = at("gpost", -8, [P, D])
        cos = at("cos", -4, [P, SEQ])
        sin = at("sin", -2, [P, SEQ])
        kal = at("kal", -8, [P, 2, SEQ], F32R)
        Vst = at("Vst", -8, [P, 2, 2, SEQ], F32R)
        vsl = at("vsl", -8, [P, 2, TT, P], F32R)
        XN = at("XN", 0, [P, TT, D])
        Y = at("Y", 0, [P, FT, SEQ])
        Yh = at("Yh", 44, [P, SLOTS, SEQ], F32R)
        Yl = at("Yl", 52, [P, SLOTS, SEQ], F32R)
        U = at("U", 60, [P, 4, SEQ])
        GU = at("GU", 68, [P, 2, SEQ])
        masks_f = at("masks_f", 58, [P, 3, P])
        lam_in = at("lam_in", 60, [P, 2, 2, HD])
        qa = [at("qa0", 0, [P, 4, SEQ], F32R), at("qa1", 78, [P, 4, SEQ], F32R)]
        kah = at("kah", 8, [P, 2, SEQ], F32R)
        vah = at("vah", 12, [P, TT, P], F32R)
        val = at("val", 74, [P, TT, P], F32R)
        qkr = at("qkr", 14, [P, 8, SEQ])
        vr = at("vr", 30, [P, TT, SEQ])
        sg = at("sg", 38, [P, TT, SEQ])
        CAT = at("CAT", 46, [P, TT, D])
        Pb = at("Pb", 62, [P, 2, 2, 2 * P])
        ATh = at("ATh", 66, [P, 2, 2, 2 * P], F32R)
        ATl = at("ATl", 70, [P, 2, 2, 2 * P], F32R)
        rtmp = at("rtmp", 86, [P, SEQ])
        decay = at("decay", 88, [P, 4, SEQ])
        STs = [at(f"STs{u}", 62 + 5 * u, [P, 1280]) for u in range(2)]
        qkd = at("qkd", 0, [P, 16, SEQ])
        vd = at("vd", 48, [P, TT, D])
        YD = at("YD", 48, [P, TT, D])
        Pb2 = at("Pb2", 64, [P, 2, 2, SEQ])
        ATdh = at("ATdh", 72, [P, 2, 1, SEQ], F32R)
        ATdl = at("ATdl", 76, [P, 2, 1, SEQ], F32R)
        Qst = at("Qst", 32, [P, 2, 2, 2, SEQ], F32R)
        Kst = at("Kst", 80, [P, 2, 2, SEQ], F32R)
        rtmp2 = at("rtmp2", 78, [P, SEQ])
        DSQ = at("DSQ", 64, [P, TT, D])
        cw1k = at("cw1k", 0, [P, 16, 256])
        cw1v = at("cw1v", 16, [P, 16, 256])
        w2k = at("w2k", 32, [P, 2, 2, HD])
        w2v = at("w2v", 33, [P, 2, HD])
        posT = at("posT", 34, [P, 2, 32])
        YN = at("YN", 32, [P, TT, D])
        qn = at("qn", 0, [P, 8, SEQ])
        qnr = at("qnr", 16, [P, 8, SEQ])
        kcv = at("kcv", 64, [P, 2, SEQ])
        cA = at("cA", 68, [P, 2, 16, 62])
        hid = at("hid", 35, [P, 2, 2, 62])
        hid4 = at("hid4", 36, [P, 2, 2, 4, 32])
        kraw = at("kraw", 44, [P, 2, SEQ])
        ksw = at("ksw", 36, [P, 2, 2, SEQ])
        rtmp3 = at("rtmp3", 74, [P, SEQ])
        ksl = at("ksl", 76, [P, 2, 2, SEQ], F32R)
        ksh = at("ksh", 84, [P, 2, 2, SEQ], F32R)
        vsh = at("vsh", 92, [P, 2, TT, P], F32R)
        ATnh = at("ATnh", 0, [P, 2, 2, SEQ], F32R)
        ATnl = at("ATnl", 8, [P, 2, 2, SEQ], F32R)
        gates = at("gates", 96, [P, TT, 48])
        kcT = at("kcT", 96.75, [P, 62])
        QSn = at("QSn", 72, [P, 2, SEQ], F32R)
        CS = at("CS", 64, [P, 2, 8, 32])
        CP = at("CP", 66, [P, 2, 8, 32])
        CA = at("CA", 68, [P, 2, 2, P])
        vblk = at("vblk", 70, [P, 2, 4 * HD])
        HT2h = at("HT2h", 0, [P, KT, SEQ], F32R)
        HT2l = at("HT2l", 16, [P, KT, SEQ], F32R)
        GA = at("GA", 64, [P, TT, D])
        GB = at("GB", 80, [P, TT, D])

        ps = [ctx.enter_context(nc.psum_tensor(f"ps{b}", [P, 512], F32)) for b in range(8)]

        in_x = [sem(f"in_x{tt}") for tt in range(TT)]
        in_c = sem("in_c")
        in_rope = sem("in_rope")
        in_post = sem("in_post")
        in_cw = sem("in_cw")
        w_raw = [sem(f"w_raw{s}") for s in range(SLOTS)]
        w_hi = sem("w_hi")
        w_lo = sem("w_lo")
        w_used = sem("w_used")
        t_done = sem("t_done")
        free = [sem(f"free{b}") for b in range(8)]
        full = [sem(f"full{b}") for b in range(8)]
        boot = sem("boot")
        boot2 = sem("boot2")
        boot3 = sem("boot3")
        x_ready = sem("x_ready")
        n_std = sem("n_std")
        xn_ready = sem("xn_ready")
        ht_hi = sem("ht_hi")
        roped = sem("roped")
        post_used = sem("post_used")
        r_sq = sem("r_sq")
        r_sum = sem("r_sum")
        r_std = sem("r_std")
        gn_mv = sem("gn_mv")
        gn_sd = sem("gn_sd")
        gn_rs = sem("gn_rs")
        cat_ret = sem("cat_ret")
        staged = sem("staged")
        st_hi = sem("st_hi")
        st_zero = sem("st_zero")
        st_lo = sem("st_lo")
        mx_done = sem("mx_done")
        a_ready = sem("a_ready")
        at_hi = sem("at_hi")
        qk_hi = sem("qk_hi")
        ks_f = sem("ks_f")
        ks_hi = sem("ks_hi")
        vs_hi = sem("vs_hi")
        in_c2 = sem("in_c2")
        hid_v = sem("hid_v")
        vb = sem("vb")
        u_ready = sem("u_ready")
        g_ready = sem("g_ready")
        y_ready = sem("y_ready")
        y_pre_hi = sem("y_pre_hi")
        y_pre = sem("y_pre")
        da_sq = sem("da_sq")
        da_ss = sem("da_ss")
        da_sd = sem("da_sd")
        da_fin = sem("da_fin")
        cm_a = sem("cm_a")
        cm_s = sem("cm_s")
        cm_e = sem("cm_e")
        cm_p = sem("cm_p")
        merged = sem("merged")
        f_out = sem("f_out")
        s_out = sem("s_out")

        lam_stage_x = {"norm1": 0, "norm2": 1, "norm3": 2, "norm4": 3}

        MX0 = {"local": 0, "da": 32, "nsa": 96}
        AH0 = {"local": 0, "da": 32, "nsa": 64}
        PROB = {"local": Pb, "da": Pb2, "nsa": Pb2}
        TURNED = {"local": (ATh, ATl), "da": (ATdh, ATdl), "nsa": (ATnh, ATnl)}
        STEPS = 8
        TOTAL = {"local": 16, "da": 32, "nsa": 64}
        BODIES = {"local": [(0, 0), (1, 0)], "da": [(0, 0), (1, 2), (3, 0)],
                  "nsa": [(0, 0), (1, 2), (3, 0), (4, 0), (5, 2), (7, 0)]}

        def exists(kind, it, t):
            return not isinstance(it, int) or 0 <= t < TOTAL[kind]

        def keys(kind, t):
            i = t % 4
            return (max(i - 1, 0), i + 1) if kind == "local" else (0, i + 1)

        def width(kind, t):
            k0, k1 = keys(kind, t)
            return (k1 - k0) * P

        def pair_uses(it, t):
            return it * (STEPS // 2) + t // 2

        def turn_uses(kind, it, t):
            return pair_uses(it, t) if kind == "da" else it * STEPS + t

        def turn_bank(kind, t, m):
            return 4 + t % 2 if kind == "da" else 4 + m

        def attend_all(eng, kind, body):
            for c, n in BODIES[kind]:
                if n:
                    with eng.Fori(0, n) as it:
                        body(kind, it, c * STEPS)
                else:
                    body(kind, 0, c * STEPS)

        def span(it, scale, const, size):
            return slice(const, const + size) if isinstance(it, int) else bass.ds(it * scale + const, size)

        def bank_t(tt, half):
            return 2 * tt + half

        block = ctx.enter_context(nc.Block())

        @block.sync
        def _(sp):
            for tt in range(TT):
                sp.dma_start(X[:, tt, :], t["x"][tt * P:(tt + 1) * P, :]).then_inc(in_x[tt], 16)
            w = t["w_all"]
            for n in range(SLOTS):
                sp.dma_start(raw[:, n, :], w[n]).then_inc(w_raw[n], 16)
            rounds = (n_chunks - SLOTS) // SLOTS
            with sp.Fori(0, rounds) as i:
                for s in range(SLOTS):
                    sp.wait_ge(w_lo, i * SLOTS + s + 1)
                    sp.dma_start(raw[:, s, :], w[bass.ds(i * SLOTS + (SLOTS + s), 1)].rearrange("a p n -> p (a n)")).then_inc(w_raw[s], 16)
            for n in range(SLOTS + rounds * SLOTS, n_chunks):
                sp.wait_ge(w_lo, n - SLOTS + 1)
                sp.dma_start(raw[:, n % SLOTS, :], w[n]).then_inc(w_raw[n % SLOTS], 16)
            if stop is None:
                for tt in range(TT):
                    sp.wait_ge(f_out, tt + 1)
                    sp.dma_start(out[tt * P:(tt + 1) * P, :], XN[:, tt, :]).then_inc(s_out, 16)
                sp.wait_ge(s_out, TT * 16)
            else:
                k = sum(4 for s in ("out1", "down1", "down2", "out2") if on(s))
                sp.wait_ge(x_ready, k)
                sp.dma_start(out.rearrange("(t p) d -> p t d", p=P), X[:]).then_inc(s_out, 16)
                sp.wait_ge(s_out, 16)

        @block.gpsimd
        def _(pl):
            def everywhere(v):
                return v.rearrange("(a n) -> a n", a=1).broadcast_to((P, v.shape[0]))

            def load(dst, src, s):
                pl.dma_start(dst, src).then_inc(s, 16)

            load(gains[:], t["gains"], in_c)
            load(ident[:], t["c_ident"], in_c)
            load(perm[:], t["c_perm_r"], in_c2)
            load(cos[:], t["c_cos_r"], in_c2)
            load(sin[:], t["c_sin_r"], in_c2)
            load(masks_f[:], t["c_masks"], in_c2)
            load(sinks[:], everywhere(t["attn_sinks"]), in_c2)
            load(lam_in[:].rearrange("p a b d -> p (a b d)"), everywhere(t["da_lambda"]), in_c2)
            load(decay[:], t["c_decay"], in_c2)
            load(conv[:], t["conv"], in_c2)
            load(cmask[:], t["c_cmask"], in_c2)
            load(cvalid[:], t["c_cvalid"], in_c2)
            if on("ret"):
                ret_out = CAT[:, :, 512:].rearrange("p i (h d) -> p i h d", d=P)
                by_tile = lambda a: a.rearrange("p (h i a) -> p i h a", i=TT, a=1).broadcast_to((P, TT, 4, P))
                pl.wait_ge(gn_rs, 1)
                pool.tensor_tensor(ret_out, ret_out, by_tile(mv[:, :, 0]), ALU.subtract)
                pool.drain()
                pool.tensor_tensor(ret_out, ret_out, by_tile(grs[:]), ALU.mult)
                pool.drain()
                for b in (1, 3, 5, 7):
                    pl.wait_ge(free[b], FREED["ret"][b])
                pool.tensor_tensor(CAT[:, :, 512:], CAT[:, :, 512:], sg[:], ALU.mult).then_inc(cat_ret, 1)
            if on("local"):
                for b in (6, 7):
                    pl.wait_ge(full[b], FILLED["cat"][b])
                load(gpost[:], everywhere(t["mix_post"]), in_post)
            if on("out1"):
                pl.wait_ge(post_used, 1)
                load(gpost[:], everywhere(t["ffn_post"]), in_post)
            if on("rope_r"):
                pl.wait_ge(roped, 8)
                load(perm[:], t["c_perm_n"], in_rope)
                load(cos[:], t["c_cos_n"], in_rope)
                load(sin[:], t["c_sin_n"], in_rope)
            if on("da"):
                def low_parts(it, head):
                    u = head % 2
                    q = qkd[:, span(it, 2, head, 1), :].rearrange("p a n -> p (a n)")
                    for m in range(2):
                        own = slice(HD * m, HD * m + HD)
                        pool.drain()
                        pl.wait_ge(st_hi, it * 8 + (4 * head + m + 1))
                        pool.tensor_tensor(Qst[own, u, m, 1, :], q[own, :], Qst[own, u, m, 0, :], ALU.subtract).then_inc(st_lo, 1)
                    pool.drain()
                    pl.wait_ge(st_hi, it * 8 + (4 * head + 3))
                    k = qkd[:, span(it, 2, 8 + head, 1), :].rearrange("p a n -> p (a n)")
                    pool.tensor_tensor(Kst[:, u, 1, :], k, Kst[:, u, 0, :], ALU.subtract).then_inc(st_lo, 1)
                    pl.wait_ge(st_hi, it * 8 + (4 * head + 4))
                    by_tile = lambda a: a.rearrange("p (t n) -> p t n", t=TT)
                    pool.tensor_tensor(by_tile(Vst[:, u, 1, :]), vd[:, :, span(it, 2 * P, head * P, P)],
                                       by_tile(Vst[:, u, 0, :]), ALU.subtract).then_inc(st_lo, 1)

                pl.wait_ge(roped, 8 + 16)
                for m in range(2):
                    other = slice(HD * (1 - m), HD * (1 - m) + HD)
                    for u in range(2):
                        last = pool.memset(Qst[other, u, m, :, :].bitcast(F32), 0.0)
                last.then_inc(st_zero, 1)
                low_parts(0, 0)
                low_parts(0, 1)
                with pl.Fori(0, 3) as it:
                    low_parts(it, 2)
                    low_parts(it, 3)
                for b in (6, 7):
                    pl.wait_ge(full[b], FILLED["nsf"][b])
                load(cos[:], t["c_cos_n"], in_rope)
                load(sin[:], t["c_sin_n"], in_rope)
            if on("cmp"):
                pl.wait_ge(full[7], FILLED["nsf"][7])
                load(cw1k[:], t["cw1"][0].rearrange("(j p) n -> p j n", p=P), in_cw)
                load(cw1v[:], t["cw1"][1].rearrange("(j p) n -> p j n", p=P), in_cw)
                load(posT[:], t["posT"], in_cw)
                load(w2k[:], t["w2k"], in_cw)
                load(w2v[:], t["w2v"], in_cw)
            if on("nsa"):
                pl.wait_ge(roped, 34)
                def queries(u, tile):
                    own, other = slice(HD * u, HD * u + HD), slice(HD * (1 - u), HD * (1 - u) + HD)
                    x = qnr[own, tile, :].rearrange("p a n -> p (a n)")
                    pool.tensor_copy(QSn[own, u, :], x)
                    pool.drain()
                    pool.tensor_tensor(QSn[other, u, :], x, QSn[own, u, :], ALU.subtract).then_inc(staged, 1)

                for b in (6, 7):
                    pl.wait_ge(full[b], FILLED["nsa"][b])
                for u in range(2):
                    queries(u, slice(0, 1))
                with pl.Fori(0, 7) as it:
                    for u in range(2):
                        pl.wait_ge(full[3], it * 4 + (FILLED["nsa"][3] + 2 * u + 2))
                        queries(u, bass.ds(it + 1, 1))
                for b in (6, 7):
                    pl.wait_ge(full[b], FILLED["ydat"][b])
                load(gpost[:], everywhere(t["final"]), in_post)

        @block.tensor
        def _(pe):
            def weights(k, it=0):
                pe.wait_ge(w_lo, it * 4 + (k + 1))
                return k % SLOTS

            def three(dst, a_hi, a_lo, b_hi, b_lo, start, stop):
                tensor.matmul(dst, a_hi, b_hi, start=start, stop=False)
                tensor.matmul(dst, a_hi, b_lo, start=False, stop=False)
                return tensor.matmul(dst, a_lo, b_hi, start=False, stop=stop)

            def bank_free(stage, b, k=0):
                at_least(pe, free[b], k + FREED[stage][b])

            def ht_ready(stage):
                for b in range(KT):
                    pe.wait_ge(free[b], FREED[stage][b])

            def gemm_f(stage, c, bank, it=0, per=1, k0=0, hh=None, hl=None):
                s = weights(CHUNK0[stage] + c, it)
                bank_free(stage, bank, it * per + k0)
                for k in range(KT):
                    a = slice(k * P, (k + 1) * P)
                    last = three(ps[bank][:], Wh[:, s, a], Wl[:, s, a], HTh[:, k, :], HTl[:, k, :], k == 0, k == KT - 1)
                last.then_inc(w_used, 1)

            def gemm_n(stage, c, bank, it=0):
                s = weights(CHUNK0[stage] + c, it)
                bank_free(stage, bank)
                for tt in range(TT):
                    q = slice(tt * P, (tt + 1) * P)
                    for k in range(KT):
                        a = slice(k * P, (k + 1) * P)
                        last = three(ps[bank][:, q], HTh[:, k, q], HTl[:, k, q], Wh[:, s, a], Wl[:, s, a], k == 0, k == KT - 1)
                last.then_inc(w_used, 1)

            def chunk_t(stage, c, lh, ll, first, final, it=0):
                s = weights(CHUNK0[stage] + c, it)
                for tt in range(TT):
                    q = slice(tt * P, (tt + 1) * P)
                    for half in range(2):
                        b = bank_t(tt, half)
                        if first:
                            bank_free(stage, b)
                        n = slice(half * 512, (half + 1) * 512)
                        last = three(ps[b][:], lh[:, q], ll[:, q], Wh[:, s, n], Wl[:, s, n], first, final)
                        if final and b < 7:
                            last.then_inc(t_done, 1)
                last.then_inc(w_used, 1)

            def gemm_t(stage, hh=HTh, hl=HTl):
                for k in range(KT):
                    chunk_t(stage, k, hh[:, k, :], hl[:, k, :], k == 0, k == KT - 1)

            def to_ht(stage, src, ready=None):
                for k in range(KT):
                    bank_free(stage, k)
                    for tt in range(TT):
                        if k == 0 and ready is not None:
                            ready(tt)
                        last = tensor.transpose(ps[k][:, tt * P:(tt + 1) * P], src[:, tt, k * P:(k + 1) * P], ident[:])
                    last.then_inc(full[k], 1)

            def norm(i):
                to_ht(NORMS[i], XN, lambda tt: pe.wait_ge(xn_ready, 4 * i + tt + 1))

            def rotate(stage, c, src, it, per, dst_bank, uses):
                bank_free(stage, dst_bank, it * uses[0] + uses[1])
                tensor.matmul(ps[dst_bank][:], perm[:], src, start=True, stop=True).then_inc(full[dst_bank], 1)

            def rope(stage, rounds, src, tile0):
                with pe.Fori(0, rounds) as it:
                    for c in range(4):
                        gemm_f(stage, c, c, it, 1)
                        if c:
                            pe.wait_ge(free[c - 1], it + (FREED[stage][c - 1] + 1))
                            rotate(stage, c - 1, src[:, bass.ds(it * 4 + (tile0 + c - 1), 1), :].rearrange("p a n -> p (a n)"), it, 1,
                                   4 + (c - 1) % 2, (2, (c - 1) // 2))
                    pe.wait_ge(free[3], it + (FREED[stage][3] + 1))
                    rotate(stage, 3, src[:, bass.ds(it * 4 + (tile0 + 3), 1), :].rearrange("p a n -> p (a n)"), it, 1, 5, (2, 1))

            def up(stage, rounds=FT // 2):
                with pe.Fori(0, rounds) as it:
                    for c in range(4):
                        gemm_f(stage, c, c, it, 1)

            def down(stage):
                pe.wait_ge(y_pre, {"down1": 1, "down2": 2, "down3": 3}[stage])
                chunk_t(stage, 0, Yh[:, 0, :], Yl[:, 0, :], True, False)
                with pe.Fori(0, 4) as it:
                    for c in range(4):
                        s = (1 + c) % SLOTS
                        chunk_t(stage, 1 + c, Yh[:, s, :], Yl[:, s, :], False, False, it)
                for c in range(17, FT):
                    chunk_t(stage, c, Yh[:, c % SLOTS, :], Yl[:, c % SLOTS, :], False, c == FT - 1)

            def scores(kind, it, t):
                i, u, b2 = t % 4, t // 4 % 2, 2 * (t % 2)
                k0, k1 = keys(kind, t)
                w = width(kind, t)
                q, k = slice(i * P, (i + 1) * P), slice(k0 * P, k1 * P)
                if kind == "nsa" and i == 0:
                    pe.wait_ge(staged, it * 2 + (t // 4 + 1))
                if kind == "da" and i == 0:
                    pe.wait_ge(st_lo, it * 8 + (4 * (t // 4) + 3))
                for m in range(2):
                    b = b2 + m
                    bank_free(kind, b, pair_uses(it, t))
                    dst = ps[b][:, 0:w]
                    if kind == "nsa":
                        g = t // 32
                        tensor.matmul(dst, QSn[:, u, q], ksh[:, m, g, k], start=True, stop=False)
                        tensor.matmul(dst, QSn[:, u, q], ksl[:, m, g, k], start=False, stop=False)
                    elif kind == "da":
                        three(dst, Qst[:, u, m, 0, q], Qst[:, u, m, 1, q], Kst[:, u, 0, k], Kst[:, u, 1, k], True, False)
                    else:
                        tile = t // 4
                        two = qa[tile // 2][:, 2 * (tile % 2) + m, q]
                        tensor.matmul(dst, two, kah[:, tile // 2, k], start=True, stop=False)
                        tensor.matmul(dst, two, kal[:, tile // 2, k], start=False, stop=False)
                    if kind == "local" and i > 0:
                        tensor.matmul(ps[b][:, 0:P], identb[:], outside[:], start=False, stop=False)
                    tensor.matmul(ps[b][:, w - P:w], identb[:], causal[:], start=False, stop=True).then_inc(full[b], 1)

            def turn(kind, it, t):
                if kind == "da":
                    pe.wait_ge(a_ready, it * STEPS + (t + 1))
                for m in range(1 if kind == "da" else 2):
                    b = turn_bank(kind, t, m)
                    if kind != "da":
                        bank_free(kind, 2 * (t % 2) + m, pair_uses(it, t) + 1)
                    bank_free(kind, b, turn_uses(kind, it, t))
                    for j in range(width(kind, t) // P):
                        last = tensor.transpose(ps[b][:, j * P:(j + 1) * P], PROB[kind][:, t % 2, m, j * P:(j + 1) * P], ident[:])
                    last.then_inc(full[b], 1)

            def values(kind, it, t):
                hi, lo = TURNED[kind]
                k0, k1 = keys(kind, t)
                u = t % 2
                b = 6 + u
                n = k1 - k0
                bank_free(kind, b, pair_uses(it, t))
                if kind == "da" and t % 4 == 0:
                    pe.wait_ge(st_lo, it * 8 + (4 * (t // 4) + 4))
                for m in range(1 if kind == "da" else 2):
                    bank_free(kind, turn_bank(kind, t, m), turn_uses(kind, it, t) + 1)
                    for j in range(n):
                        a = slice(j * P, (j + 1) * P)
                        if kind == "da":
                            v = Vst[:, t // 4 % 2, 0, a], Vst[:, t // 4 % 2, 1, a]
                            dst = ps[b][:, 0:P]
                        elif kind == "nsa":
                            c = slice(t // 32 * HD, t // 32 * HD + HD)
                            v = vsh[:, m, j, c], vsl[:, m, j, c]
                            dst = ps[b][:, m * HD:(m + 1) * HD]
                        else:
                            c = slice(t // 8 * HD, t // 8 * HD + HD)
                            v = vah[:, k0 + j, c], val[:, k0 + j, c]
                            dst = ps[b][:, m * HD:(m + 1) * HD]
                        last = three(dst, hi[:, u, m, a], lo[:, u, m, a], v[0], v[1], j == 0, j == n - 1)
                last.then_inc(full[b], 1)

            def attend(kind, it, t0):
                for t in range(t0, t0 + STEPS):
                    if exists(kind, it, t - 2):
                        values(kind, it, t - 2)
                    if exists(kind, it, t + 2):
                        scores(kind, it, t + 2)
                    turn(kind, it, t)

            def attention(kind):
                scores(kind, 0, 0)
                scores(kind, 0, 1)
                attend_all(pe, kind, attend)
                values(kind, 0, TOTAL[kind] - 2)
                values(kind, 0, TOTAL[kind] - 1)

            pe.wait_ge(in_c, 16 * 2)
            norm(0)
            ht_ready("qa")
            for c in range(4):
                gemm_f("qa", c, c)
            gemm_f("kva", 0, 0)
            gemm_n("kva", 1, 1)
            pe.wait_ge(in_c2, 16 * 10)
            pe.wait_ge(boot, 2)
            if on("rope_r"):
                rope("rope_r", 2, qkr, 0)
            if on("vg"):
                gemm_t("vg")
            if on("ret"):
                ret = "ret"
                pe.wait_ge(roped, 8)

                def ret_scores(h):
                    for c in range(4):
                        bank_free(ret, c, h)
                        tensor.matmul(ps[c][:, 0:SEQ - c * P], qkr[:, 4 + h, c * P:(c + 1) * P], qkr[:, h, c * P:],
                                      start=True, stop=True).then_inc(full[c], 1)

                def ret_values(h):
                    u = h % 2
                    bank_free(ret, 4 + u, h // 2)
                    for i in range(4):
                        for c in range(i + 1):
                            if i == c:
                                pe.wait_ge(free[c], FREED[ret][c] + h + 1)
                            o = [0, 512, 896, 1152][c]
                            last = tensor.matmul(ps[4 + u][:, i * P:(i + 1) * P], STs[u][:, o + (i - c) * P:o + (i - c + 1) * P],
                                                 vr[:, c, h * P:(h + 1) * P], start=c == 0, stop=c == i)
                    last.then_inc(full[4 + u], 1)

                for b in range(8):
                    pe.wait_ge(free[b], FREED[ret][b])
                ret_scores(0)
                for h in range(4):
                    if h < 3:
                        ret_scores(h + 1)
                    ret_values(h)
            if on("local"):
                attention("local")
            if on("cat"):
                def cat_ready(tt):
                    if tt == 0:
                        pe.wait_ge(cat_ret, 1)
                        for b in (6, 7):
                            pe.wait_ge(free[b], FREED["cat"][b])
                to_ht("cat", CAT, cat_ready)
            if on("out1"):
                ht_ready("out1")
                gemm_t("out1")
            if on("norm1"):
                norm(1)
                ht_ready("up1")
            if on("up1"):
                up("up1")
            if on("down1"):
                down("down1")
            if on("norm2"):
                norm(2)
                ht_ready("up2")
            if on("up2"):
                up("up2")
            if on("down2"):
                down("down2")
            if on("norm3"):
                norm(3)
                ht_ready("rope_dq")
            if on("rope_dq"):
                pe.wait_ge(in_rope, 48)
                rope("rope_dq", 2, qkd, 0)
                rope("rope_dk", 2, qkd, 8)
            if on("vda"):
                gemm_t("vda")
            if on("da"):
                for b in range(8):
                    pe.wait_ge(free[b], FREED["da"][b])
                pe.wait_ge(st_zero, 1)
                attention("da")
            if on("nsf"):
                for c in range(4):
                    gemm_f("nsf", c, c)
                pe.wait_ge(in_rope, 80)
                for c in (2, 3):
                    pe.wait_ge(free[c], FREED["nsf"][c] + 1)
                    rotate("nsf", c, kraw[:, c - 2, :], 0, 1, 2 + c, (0, 0))
            if on("nst"):
                for c in range(3):
                    gemm_n("nst", c, c)
            if on("cmp"):
                pe.wait_ge(in_cw, 80)
                for kv in range(2):
                    pe.wait_ge(cm_a, kv + 1)
                    bank_free("cmp", 4 + kv)
                    cw = (cw1k, cw1v)[kv]
                    for ht in range(2):
                        for j in range(16):
                            last = tensor.matmul(ps[4 + kv][:, ht * 64:ht * 64 + 62], cw[:, j, ht * P:(ht + 1) * P], cA[:, kv, j, :],
                                                 start=j == 0, stop=j == 15)
                    last.then_inc(full[4 + kv], 1)
                pe.wait_ge(free[4], FREED["cmp"][4] + 1)
                bank_free("cmp", 6)
                for ht in range(2):
                    last = tensor.matmul(ps[6][:, 0:62], w2k[:, ht, :, :].rearrange("p a d -> p (a d)"), hid[:, 0, ht, :],
                                         start=ht == 0, stop=ht == 1)
                last.then_inc(full[6], 1)
                pe.wait_ge(hid_v, 1)
                bank_free("cmp", 7)
                for g in range(2):
                    for ht in range(2):
                        last = tensor.matmul(ps[7][:, g * HD:(g + 1) * HD], hid4[:, ht, g, :, :].rearrange("p a n -> p (a n)"), w2v[:, ht, :],
                                             start=ht == 0, stop=ht == 1)
                last.then_inc(full[7], 1)
            if on("rope_q"):
                rope("rope_q", 2, qn, 0)
            if on("cmpa"):
                st = "cmpa"
                for b in range(8):
                    pe.wait_ge(free[b], FREED[st][b])
                pe.wait_ge(vb, 1)

                def cmp_scores(n):
                    g, i = n // 4, n % 4
                    for u in range(2):
                        b = 2 * u + n % 2
                        bank_free(st, b, n // 2)
                        h = slice(HD * u, HD * u + HD)
                        for j in range(4):
                            last = tensor.matmul(ps[b][:, j * 32:j * 32 + N_CMP], qn[h, 4 * g + j, i * P:(i + 1) * P],
                                                 kcT[h, g * N_CMP:(g + 1) * N_CMP], start=True, stop=True)
                        last.then_inc(full[b], 1)

                def cmp_turn(n):
                    pe.wait_ge(cm_p, n + 1)
                    b = 4 + n % 2
                    bank_free(st, b, n // 2)
                    for f in range(2):
                        last = tensor.transpose(ps[b][:, f * P:(f + 1) * P], CP[:, n % 2, 4 * f:4 * f + 4, :].rearrange("p h n -> p (h n)"), ident[:])
                    last.then_inc(full[b], 1)

                def cmp_values(n):
                    pe.wait_ge(free[4 + n % 2], FREED[st][4 + n % 2] + n // 2 + 1)
                    b = 6 + n % 2
                    bank_free(st, b, n // 2)
                    for f in range(2):
                        last = tensor.matmul(ps[b][:, f * 256:(f + 1) * 256], CA[:, n % 2, f, :], vblk[:, n // 4, :], start=True, stop=True)
                    last.then_inc(full[b], 1)

                cmp_scores(0)
                for n in range(8):
                    if n < 7:
                        cmp_scores(n + 1)
                    if n:
                        cmp_values(n - 1)
                    cmp_turn(n)
                cmp_values(7)
            if on("nsa"):
                for b in range(6):
                    pe.wait_ge(free[b], FREED["nsa"][b])
                attention("nsa")
            if on("ydat"):
                to_ht("ydat", YD, lambda tt: pe.wait_ge(da_fin, tt + 1))
            if on("ga"):
                gemm_t("ga")
            if on("gb"):
                gemm_t("gb")
            if on("ynst"):
                for b in (6, 7):
                    pe.wait_ge(free[b], FREED["ydat"][b])
                to_ht("ynst", YN)
            if on("pda"):
                gemm_t("pda", HT2h, HT2l)
            if on("pns"):
                ht_ready("pda")
                gemm_t("pns")
            if on("mt"):
                to_ht("mt", GA, lambda tt: pe.wait_ge(merged, tt + 1))
            if on("out2"):
                ht_ready("out2")
                gemm_t("out2")
            if on("norm4"):
                norm(4)
                ht_ready("up3")
            if on("up3"):
                up("up3")
            if on("down3"):
                down("down3")

        @block.scalar
        def _(ac):
            def split(k, it=0):
                if isinstance(it, int) and k + 4 * it >= n_chunks:
                    return
                s = k % SLOTS
                ac.wait_ge(w_raw[s], it * 16 + 16 * (k // SLOTS + 1))
                at_least(ac, w_used, it * 4 + (k - SLOTS + 1))
                scalar.copy(Wh[:, s, :], raw[:, s, :]).then_inc(w_hi, 1)

            def chunk_done(stage, c, it=0):
                ac.wait_ge(w_used, it * 4 + (CHUNK0[stage] + c + 1))

            def filled(stage, b, k=0):
                ac.wait_ge(full[b], k + (FILLED[stage][b] + 1))

            def bank_done(stage, tt, half, n=KT):
                b = bank_t(tt, half)
                if b < 7:
                    ac.wait_ge(t_done, 7 * T_STAGES.index(stage) + b + 1)
                else:
                    chunk_done(stage, n - 1)

            def splits_t(stage, n=KT):
                for c in range(n):
                    split(CHUNK0[stage] + c + LEAD)

            def to_ht(stage, dst, gain=None):
                for k in range(KT):
                    filled(stage, k)
                    if gain is None:
                        scalar.copy(dst[:, k, :], ps[k][:]).then_inc(ht_hi, 1)
                    else:
                        scalar.activation(dst[:, k, :], ps[k][:], ACT.Copy, scale=gain(k)).then_inc(ht_hi, 1)

            def norm(i):
                for tt in range(TT):
                    if i == 0:
                        ac.wait_ge(in_x[tt], 16)
                    else:
                        ac.wait_ge(x_ready, 4 * (i - 1) + tt + 1)
                    scalar.activation(XN[:, tt, :], X[:, tt, :], ACT.Square, accum_out=sst[:, tt:tt + 1])
                scalar.drain()
                scalar.activation(std[:], sst[:], ACT.Sqrt, scale=1.0 / D, bias=eps[:]).then_inc(n_std, 1)
                to_ht(NORMS[i], HTh, lambda k: gains[:, i, k:k + 1])

            def rope(stage, rounds, dst, tile0, factor=1.0):
                with ac.Fori(0, rounds) as it:
                    for c in range(4):
                        split(CHUNK0[stage] + c + LEAD, it)
                        chunk_done(stage, c, it)
                        scalar.activation(dst[:, bass.ds(it * 4 + (tile0 + c), 1), :].rearrange("p a n -> p (a n)"), ps[c][:], ACT.Copy,
                                          scale=factor).then_inc(free[c], 1)

            def residual_squares(stage, n):
                for tt in range(TT):
                    for half in range(2):
                        bank_done(stage, tt, half, n)
                        b = bank_t(tt, half)
                        scalar.activation(XN[:, tt, half * 512:(half + 1) * 512], ps[b][:], ACT.Square,
                                          accum_out=ss[:, b:b + 1]).then_inc(r_sq, 1)
                ac.wait_ge(r_sum, {"out1": 1, "down1": 2}[stage])
                scalar.activation(std[:], sst[:], ACT.Sqrt, scale=1.0 / D, bias=eps[:]).then_inc(r_std, 1)

            def up_conv(stage):
                with ac.Fori(0, FT // 2) as it:
                    for c in range(4):
                        split(CHUNK0[stage] + c + LEAD, it)
                        tile = it * 2 + (c // 2) if c % 2 == 0 else it * 2 + (FT + c // 2)
                        if c % 2 == 0:
                            ac.wait_ge(y_ready, it * 2 + (c // 2 + 1))
                        chunk_done(stage, c, it)
                        cw = conv[:, bass.ds(tile, 1), :].rearrange("p a n -> p (a n)")
                        scalar.activation(U[:, c, :], ps[c][:], ACT.Identity, scale=cw[:, 2:3], bias=cw[:, 3:4]).then_inc(u_ready, 1)
                        if c % 2:
                            ac.wait_ge(free[c - 1], it + (FREED[stage][c - 1] + 1))
                            scalar.activation(GU[:, c // 2, :], U[:, c - 1, :], ACT.Gelu_apprx_tanh).then_inc(g_ready, 1)

            def up_swiglu(stage):
                with ac.Fori(0, FT // 2) as it:
                    for c in range(4):
                        split(CHUNK0[stage] + c + LEAD, it)
                        if c % 2 == 0:
                            at_least(ac, free[c + 1], it + FREED[stage][c + 1])
                            chunk_done(stage, c, it)
                            scalar.activation(GU[:, c // 2, :], ps[c][:], ACT.Silu).then_inc(free[c], 1)

            def down(stage, i):
                for k in range(LEAD):
                    if k == 0:
                        if stage == "down1":
                            ac.wait_ge(y_ready, FT + 2)
                        else:
                            for b in (1, 3):
                                ac.wait_ge(free[b], FREED[stage][b])
                    last = scalar.copy(Yh[:, k, :], Y[:, k, :])
                last.then_inc(y_pre_hi, 1)

                def step(c, it=0):
                    k = c + LEAD
                    if not (isinstance(it, int) and k >= FT):
                        at_least(ac, w_used, it * 4 + (CHUNK0[stage] + k - SLOTS + 1))
                        scalar.copy(Yh[:, k % SLOTS, :], Y[:, bass.ds(it * 4 + k, 1), :].rearrange("p a n -> p (a n)")
                                    if not isinstance(it, int) else Y[:, k, :])
                        if isinstance(it, int) and CHUNK0[stage] + k >= n_chunks:
                            assert False
                    split(CHUNK0[stage] + k, it)

                step(0)
                with ac.Fori(0, 4) as it:
                    for c in range(4):
                        step(1 + c, it)
                for c in range(17, FT):
                    step(c)

            def exps(kind, it, t):
                w = width(kind, t)
                u = t % 2
                if kind == "local":
                    ac.wait_ge(mx_done, MX0[kind] + 2 * t + 2)
                    scalar.activation(esk[:, u, :], sk[:, u, :], ACT.Exp)
                for m in range(2):
                    b = 2 * u + m
                    if kind != "local":
                        ac.wait_ge(mx_done, it * (2 * STEPS) + (MX0[kind] + 2 * t + m + 1))
                    scalar.activation(PROB[kind][:, u, m, 0:w], ps[b][:, 0:w], ACT.Exp, bias=nmx[:, u, m:m + 1],
                                      accum_out=rs[:, u, m:m + 1]).then_inc(free[b], 1)

            def high(kind, it, t):
                hi = TURNED[kind][0]
                w = width(kind, t)
                u = t % 2
                for m in range(1 if kind == "da" else 2):
                    b = turn_bank(kind, t, m)
                    filled(kind, b, turn_uses(kind, it, t))
                    if m == 0:
                        at_least(ac, full[6 + u], pair_uses(it, t) + FILLED[kind][6 + u])
                    scalar.copy(hi[:, u, m, 0:w], ps[b][:, 0:w]).then_inc(at_hi, 1)

            def da_out(it, t):
                u = t % 2
                if isinstance(it, int) and t >= TOTAL["da"] - 2:
                    filled("da", 6 + u, pair_uses(it, t))
                scalar.activation(YD[:, t % 4, span(it, 2 * P, t // 4 * P, P)], ps[6 + u][:, 0:P], ACT.Copy,
                                  scale=rr[:, t % 4, 0:1]).then_inc(free[6 + u], 1)

            def attend(kind, it, t0):
                for t in range(t0, t0 + STEPS):
                    if kind == "da" and exists(kind, it, t - 3):
                        da_out(it, t - 3)
                    if exists(kind, it, t + 1):
                        exps(kind, it, t + 1)
                    high(kind, it, t)
                    if kind == "da":
                        if t % 4 < 2 and exists(kind, it, t + 4):
                            high_parts(it, t // 4 + 1, t % 4)

            def attention(kind):
                exps(kind, 0, 0)
                attend_all(ac, kind, attend)
                if kind == "da":
                    for t in range(TOTAL[kind] - 3, TOTAL[kind]):
                        da_out(0, t)

            def high_parts(it, head, which):
                u = head % 2
                if which == 0:
                    q = qkd[:, span(it, 2, head, 1), :].rearrange("p a n -> p (a n)")
                    for m in range(2):
                        own = slice(HD * m, HD * m + HD)
                        scalar.copy(Qst[own, u, m, 0, :], q[own, :]).then_inc(st_hi, 1)
                    k = qkd[:, span(it, 2, 8 + head, 1), :].rearrange("p a n -> p (a n)")
                    scalar.copy(Kst[:, u, 0, :], k).then_inc(st_hi, 1)
                else:
                    scalar.copy(Vst[:, u, 0, :].rearrange("p (t n) -> p t n", t=TT), vd[:, :, span(it, 2 * P, head * P, P)]).then_inc(st_hi, 1)

            ac.wait_ge(boot, 1)
            for n in range(LEAD):
                split(n)
            ac.wait_ge(in_c, 16 * 2)
            norm(0)
            for c in range(4):
                split(CHUNK0["qa"] + c + LEAD)
                chunk_done("qa", c)
                for m in range(2):
                    own = slice(HD * m, HD * m + HD)
                    last = scalar.activation(qa[c // 2][own, 2 * (c % 2) + m, :], ps[c][own, :], ACT.Copy, scale=HD ** -0.5)
                last.then_inc(qk_hi, 1)
            split(CHUNK0["kva"] + LEAD)
            chunk_done("kva", 0)
            for kv in range(2):
                for half in range(2):
                    last = scalar.copy(kah[64 * half:64 * half + 64, kv, :], ps[0][64 * kv:64 * kv + 64, :])
            last.then_inc(qk_hi, 1)
            split(CHUNK0["kva"] + 1 + LEAD)
            chunk_done("kva", 1)
            scalar.copy(vah[:].rearrange("p a n -> p (a n)"), ps[1][:]).then_inc(qk_hi, 1)
            ac.wait_ge(boot2, 1)
            scalar.activation(lam_e[:], lam_s[:], ACT.Exp).then_inc(boot3, 1)
            if on("rope_r"):
                rope("rope_r", 2, qkr, 0)
            if on("vg"):
                splits_t("vg")
                for tt in range(TT):
                    bank_done("vg", tt, 1)
                    scalar.activation(sg[:, tt, :], ps[bank_t(tt, 1)][:], ACT.Silu).then_inc(free[bank_t(tt, 1)], 1)
            if on("ret"):
                for h in range(4):
                    filled("ret", 4 + h % 2, h // 2)
                    scalar.copy(CAT[:, :, 512 + h * P:512 + (h + 1) * P], ps[4 + h % 2][:].rearrange("p (i n) -> p i n", i=4)).then_inc(free[4 + h % 2], 1)
                ac.wait_ge(gn_mv, 1)
                scalar.activation(gsd[:], mv[:, :, 1], ACT.Sqrt, bias=eps[:]).then_inc(gn_sd, 1)
            if on("local"):
                attention("local")
            if on("cat"):
                to_ht("cat", HTh)
            if on("out1"):
                splits_t("out1")
                residual_squares("out1", KT)
            if on("norm1"):
                norm(1)
            if on("up1"):
                up_conv("up1")
            if on("down1"):
                down("down1", 1)
                residual_squares("down1", FT)
            if on("norm2"):
                norm(2)
            if on("up2"):
                up_swiglu("up2")
            if on("down2"):
                down("down2", 2)
            if on("norm3"):
                norm(3)
            if on("rope_dq"):
                rope("rope_dq", 2, qkd, 0, HD ** -0.5)
                rope("rope_dk", 2, qkd, 8)
            if on("vda"):
                splits_t("vda")
                for tt in range(TT):
                    bank_done("vda", tt, 1)
                    scalar.copy(vd[:, tt, 512:], ps[bank_t(tt, 1)][:]).then_inc(free[bank_t(tt, 1)], 1)
            if on("da"):
                ac.wait_ge(roped, 24)
                ac.wait_ge(free[6], FREED["da"][6])
                high_parts(0, 0, 0)
                high_parts(0, 0, 1)
                attention("da")
            if on("nsf"):
                scalar.drain()
                scalar.activation(DSQ[:], YD[:], ACT.Square).then_inc(da_sq, 1)
                ac.wait_ge(da_ss, 1)
                scalar.activation(hsd[:], hss[:], ACT.Sqrt, scale=1.0 / P, bias=eps[:]).then_inc(da_sd, 1)
                for c in range(4):
                    split(CHUNK0["nsf"] + c + LEAD)
                    chunk_done("nsf", c)
                    dst = kcv[:, c, :] if c < 2 else kraw[:, c - 2, :]
                    scalar.copy(dst, ps[c][:]).then_inc(free[c], 1)
                ac.wait_ge(ks_f, 1)
                scalar.copy(ksh[:].rearrange("p a g n -> p (a g n)"), ksw[:].rearrange("p a g n -> p (a g n)")).then_inc(ks_hi, 1)
            if on("nst"):
                for c in range(3):
                    split(CHUNK0["nst"] + c + LEAD)
                    chunk_done("nst", c)
                    if c < 2:
                        scalar.copy(vsh[:, c, :, :].rearrange("p a n -> p (a n)"), ps[c][:]).then_inc(vs_hi, 1)
                    else:
                        scalar.activation(gates[:], ps[2][:].rearrange("p (i n) -> p i n", i=4)[:, :, 0:48], ACT.Sigmoid).then_inc(free[2], 1)
            if on("cmp"):
                for kv in range(2):
                    filled("cmp", 4 + kv)
                    scalar.activation(hid[:, kv, :, :], ps[4 + kv][:, 0:128].rearrange("p (a n) -> p a n", a=2)[:, :, 0:62],
                                      ACT.Gelu_apprx_tanh).then_inc(free[4 + kv], 1)
                filled("cmp", 6)
                scalar.copy(kcT[:], ps[6][:, 0:62]).then_inc(free[6], 1)
            if on("rope_q"):
                rope("rope_q", 2, qn, 0, HD ** -0.5)
            if on("cmpa"):
                st = "cmpa"

                def cmp_exp(n):
                    ac.wait_ge(cm_s, n + 1)
                    scalar.activation(CS[:, n % 2, :, 0:N_CMP], CS[:, n % 2, :, 0:N_CMP], ACT.Exp).then_inc(cm_e, 1)

                def cmp_out(n):
                    filled(st, 6 + n % 2, n // 2)
                    g = n // 4
                    scalar.copy(YN[:, n % 4, 512 * g:512 * g + 512], ps[6 + n % 2][:]).then_inc(free[6 + n % 2], 1)

                cmp_exp(0)
                for n in range(8):
                    if n < 7:
                        cmp_exp(n + 1)
                    filled(st, 4 + n % 2, n // 2)
                    scalar.copy(CA[:, n % 2, :, :].rearrange("p f n -> p (f n)"), ps[4 + n % 2][:, 0:2 * P]).then_inc(free[4 + n % 2], 1)
                    if n:
                        cmp_out(n - 1)
                cmp_out(7)
            if on("nsa"):
                attention("nsa")
            if on("ydat"):
                to_ht("ydat", HT2h, lambda k: gains[:, 5, k:k + 1])
            if on("ga"):
                splits_t("ga")
                for tt in range(TT):
                    for half in range(2):
                        bank_done("ga", tt, half)
                        scalar.activation(GA[:, tt, half * 512:(half + 1) * 512], ps[bank_t(tt, half)][:], ACT.Sigmoid).then_inc(free[bank_t(tt, half)], 1)
            if on("gb"):
                splits_t("gb")
                for tt in range(TT):
                    for half in range(2):
                        bank_done("gb", tt, half)
                        scalar.activation(GB[:, tt, half * 512:(half + 1) * 512], ps[bank_t(tt, half)][:], ACT.Sigmoid).then_inc(free[bank_t(tt, half)], 1)
            if on("ynst"):
                to_ht("ynst", HTh)
            if on("pda"):
                splits_t("pda")
            if on("pns"):
                splits_t("pns")
            if on("mt"):
                to_ht("mt", HTh)
            if on("out2"):
                splits_t("out2")
            if on("norm4"):
                norm(4)
            if on("up3"):
                up_swiglu("up3")
            if on("down3"):
                down("down3", 3)
                for tt in range(TT):
                    ac.wait_ge(x_ready, 16 + tt + 1)
                    scalar.activation(XN[:, tt, :], X[:, tt, :], ACT.Square, accum_out=sst[:, tt:tt + 1])
                scalar.drain()
                scalar.activation(std[:], sst[:], ACT.Sqrt, scale=1.0 / D, bias=eps[:]).then_inc(n_std, 1)

        @block.vector
        def _(ve):
            def split(k, it=0):
                if isinstance(it, int) and k + 4 * it >= n_chunks:
                    return
                s = k % SLOTS
                ve.wait_ge(w_hi, it * 4 + (k + 1))
                vector.tensor_tensor(Wl[:, s, :], raw[:, s, :], Wh[:, s, :], ALU.subtract).then_inc(w_lo, 1)

            def chunk_done(stage, c, it=0):
                ve.wait_ge(w_used, it * 4 + (CHUNK0[stage] + c + 1))

            def filled(stage, b, k=0):
                ve.wait_ge(full[b], k + (FILLED[stage][b] + 1))

            def bank_done(stage, tt, half, n=KT):
                b = bank_t(tt, half)
                if b < 7:
                    ve.wait_ge(t_done, 7 * T_STAGES.index(stage) + b + 1)
                else:
                    chunk_done(stage, n - 1)

            def splits_t(stage, n=KT):
                for c in range(n):
                    split(CHUNK0[stage] + c + LEAD)

            def to_ht(stage, hi, lo, gain=None):
                for k in range(KT):
                    ve.wait_ge(ht_hi, 8 * HT_STAGES.index(stage) + k + 1)
                    if gain is None:
                        vector.tensor_tensor(lo[:, k, :], ps[k][:], hi[:, k, :], ALU.subtract).then_inc(free[k], 1)
                    else:
                        vector.scalar_tensor_tensor(out=lo[:, k, :], in0=ps[k][:], scalar=gain(k), in1=hi[:, k, :],
                                                    op0=ALU.mult, op1=ALU.subtract).then_inc(free[k], 1)

            def norm(i):
                ve.wait_ge(n_std, i + 1)
                vector.reciprocal(rstd[:], std[:])
                vector.drain()
                for tt in range(TT):
                    vector.tensor_scalar(XN[:, tt, :], X[:, tt, :], rstd[:, tt:tt + 1], None, ALU.mult).then_inc(xn_ready, 1)
                to_ht(NORMS[i], HTh, HTl, lambda k: gains[:, i, k:k + 1])

            def turn_rope(stage, src, dst, bank, use, tmp):
                vector.drain()
                filled(stage, bank, use)
                vector.tensor_tensor(tmp, ps[bank][:], sin[:], ALU.mult).then_inc(free[bank], 1)
                vector.tensor_tensor(dst, src, cos[:], ALU.mult)
                vector.drain()
                vector.tensor_tensor(dst, dst, tmp, ALU.add).then_inc(roped, 1)

            def rope(stage, rounds, src, dst, tmp, tile0=0):
                with ve.Fori(0, rounds) as it:
                    for c in range(4):
                        split(CHUNK0[stage] + c + LEAD, it)
                        tile = bass.ds(it * 4 + (tile0 + c), 1)
                        turn_rope(stage, src[:, tile, :].rearrange("p a n -> p (a n)"), dst[:, tile, :].rearrange("p a n -> p (a n)"),
                                  4 + c % 2, it * 2 + c // 2, tmp[:])

            def residual(stage, i, n):
                for tt in range(TT):
                    for half in range(2):
                        b = bank_t(tt, half)
                        ve.wait_ge(r_sq, 8 * i + b + 1)
                        if b == 0:
                            ve.wait_ge(in_post, 16 * (i + 1))
                        h = slice(half * 512, (half + 1) * 512)
                        vector.tensor_tensor(XN[:, tt, h], ps[b][:], gpost[:, h], ALU.mult).then_inc(free[b], 1)
                vector.tensor_tensor(sst[:], ss[:].rearrange("p (t a) -> p t a", a=2)[:, :, 0], ss[:].rearrange("p (t a) -> p t a", a=2)[:, :, 1],
                                     ALU.add).then_inc(r_sum, 1)
                vector.drain().then_inc(post_used, 1)
                ve.wait_ge(r_std, i + 1)
                vector.reciprocal(rstd[:], std[:])
                vector.drain()
                for tt in range(TT):
                    vector.scalar_tensor_tensor(out=X[:, tt, :], in0=XN[:, tt, :], scalar=rstd[:, tt:tt + 1], in1=X[:, tt, :],
                                                op0=ALU.mult, op1=ALU.add).then_inc(x_ready, 1)

            def residual_plain(stage, factor, n):
                for tt in range(TT):
                    for half in range(2):
                        bank_done(stage, tt, half, n)
                        h = slice(half * 512, (half + 1) * 512)
                        vector.scalar_tensor_tensor(out=X[:, tt, h], in0=ps[bank_t(tt, half)][:], scalar=factor, in1=X[:, tt, h],
                                                    op0=ALU.mult, op1=ALU.add).then_inc(free[bank_t(tt, half)], 1)
                    vector.drain().then_inc(x_ready, 1)

            def up_conv(stage):
                with ve.Fori(0, FT // 2) as it:
                    for c in range(4):
                        split(CHUNK0[stage] + c + LEAD, it)
                        tile = it * 2 + (c // 2) if c % 2 == 0 else it * 2 + (FT + c // 2)
                        cw = conv[:, bass.ds(tile, 1), :].rearrange("p a n -> p (a n)")
                        ve.wait_ge(u_ready, it * 4 + (c + 1))
                        vector.scalar_tensor_tensor(out=U[:, c, 1:], in0=ps[c][:, 0:SEQ - 1], scalar=cw[:, 1:2], in1=U[:, c, 1:],
                                                    op0=ALU.mult, op1=ALU.add)
                        vector.drain()
                        vector.scalar_tensor_tensor(out=U[:, c, 2:], in0=ps[c][:, 0:SEQ - 2], scalar=cw[:, 0:1], in1=U[:, c, 2:],
                                                    op0=ALU.mult, op1=ALU.add).then_inc(free[c], 1)
                        if c % 2:
                            vector.drain()
                            ve.wait_ge(g_ready, it * 2 + (c // 2 + 1))
                            vector.tensor_tensor(Y[:, bass.ds(it * 2 + c // 2, 1), :].rearrange("p a n -> p (a n)"), GU[:, c // 2, :], U[:, c, :],
                                                 ALU.mult).then_inc(y_ready, 1)

            def up_swiglu(stage):
                with ve.Fori(0, FT // 2) as it:
                    for c in range(4):
                        split(CHUNK0[stage] + c + LEAD, it)
                        if c % 2:
                            ve.wait_ge(free[c - 1], it + (FREED[stage][c - 1] + 1))
                            chunk_done(stage, c, it)
                            vector.tensor_tensor(Y[:, bass.ds(it * 2 + c // 2, 1), :].rearrange("p a n -> p (a n)"), ps[c][:], GU[:, c // 2, :],
                                                 ALU.mult).then_inc(free[c], 1)

            def down(stage, i):
                ve.wait_ge(y_pre_hi, i)
                for k in range(LEAD):
                    last = vector.tensor_tensor(Yl[:, k, :], Y[:, k, :], Yh[:, k, :], ALU.subtract)
                last.then_inc(y_pre, 1)

                def step(c, it=0):
                    k = c + LEAD
                    if not (isinstance(it, int) and k >= FT):
                        ve.wait_ge(w_hi, it * 4 + (CHUNK0[stage] + k + 1))
                        src = Y[:, k, :] if isinstance(it, int) else Y[:, bass.ds(it * 4 + k, 1), :].rearrange("p a n -> p (a n)")
                        vector.tensor_tensor(Yl[:, k % SLOTS, :], src, Yh[:, k % SLOTS, :], ALU.subtract)
                    split(CHUNK0[stage] + k, it)

                step(0)
                with ve.Fori(0, 4) as it:
                    for c in range(4):
                        step(1 + c, it)
                for c in range(17, FT):
                    step(c)

            def maxima(kind, it, t):
                w = width(kind, t)
                u = t % 2
                for m in range(2):
                    filled(kind, 2 * u + m, pair_uses(it, t))
                    last = vector.tensor_reduce(nmx[:, u, m:m + 1], ps[2 * u + m][:, 0:w], AX.X, ALU.max, negate=True)
                    if kind != "local":
                        last.then_inc(mx_done, 1)
                if kind == "local":
                    vector.drain()
                    hd = 2 * (t // 4)
                    vector.tensor_tensor(nmx[:, u, :], nmx[:, u, :], nsinks[:, hd:hd + 2], ALU.min)
                    vector.drain()
                    vector.tensor_tensor(sk[:, u, :], nmx[:, u, :], sinks[:, hd:hd + 2], ALU.add).then_inc(mx_done, 2)

            def exps_done(kind, it, t):
                for m in range(2):
                    b = 2 * (t % 2) + m
                    ve.wait_ge(free[b], pair_uses(it, t) + (FREED[kind][b] + 1))

            def combine(it, t):
                w = width("da", t)
                u, v = t % 2, t % 4
                exps_done("da", it, t)
                vector.reciprocal(rr[:, v, :], rs[:, u, :])
                vector.drain()
                vector.scalar_tensor_tensor(out=gg[:, v, 0:1], in0=rs[:, u, 0:1], scalar=nlam[:], in1=rr[:, v, 1:2],
                                            op0=ALU.mult, op1=ALU.mult)
                vector.drain()
                vector.scalar_tensor_tensor(out=Pb2[:, u, 0, 0:w], in0=Pb2[:, u, 1, 0:w], scalar=gg[:, v, 0:1], in1=Pb2[:, u, 0, 0:w],
                                            op0=ALU.mult, op1=ALU.add).then_inc(a_ready, 1)

            def factors(kind, it, t):
                u, v = t % 2, t % 4
                exps_done(kind, it, t)
                if kind == "local":
                    vector.tensor_tensor(rs[:, u, :], rs[:, u, :], esk[:, u, :], ALU.add)
                    vector.drain()
                    vector.reciprocal(gg[:, v, :], rs[:, u, :])
                else:
                    vector.reciprocal(rr[:, v, :], rs[:, u, :])
                    vector.drain()
                    vector.tensor_tensor(gg[:, v, :], rr[:, v, :], gates[:, v, span(it, 6, 3 * (t // 4) + 1, 2)], ALU.mult)

            def low(kind, it, t):
                hi, lo = TURNED[kind]
                w = width(kind, t)
                u = t % 2
                ms = 1 if kind == "da" else 2
                for m in range(ms):
                    b = turn_bank(kind, t, m)
                    ve.wait_ge(at_hi, it * (ms * STEPS) + (AH0[kind] + ms * t + m + 1))
                    vector.tensor_tensor(lo[:, u, m, 0:w], ps[b][:, 0:w], hi[:, u, m, 0:w], ALU.subtract).then_inc(free[b], 1)

            def take_out(kind, it, t, m):
                u, v = t % 2, t % 4
                if m == 0:
                    filled(kind, 6 + u, pair_uses(it, t))
                src = ps[6 + u][:, m * HD:(m + 1) * HD]
                if kind == "local":
                    hd = 2 * (t // 4) + m
                    last = vector.tensor_scalar(CAT[:, v, hd * HD:(hd + 1) * HD], src, gg[:, v, m:m + 1], None, ALU.mult)
                else:
                    dst = YN[:, v, span(it, P, HD * (t // 4), HD)]
                    last = vector.scalar_tensor_tensor(out=dst, in0=src, scalar=gg[:, v, m:m + 1], in1=dst, op0=ALU.mult, op1=ALU.add)
                if m == 1:
                    last.then_inc(free[6 + u], 1)

            def attend(kind, it, t0):
                for t in range(t0, t0 + STEPS):
                    if kind == "da":
                        combine(it, t)
                        if exists(kind, it, t + 1):
                            maxima(kind, it, t + 1)
                        if exists(kind, it, t - 1):
                            low(kind, it, t - 1)
                    else:
                        out = exists(kind, it, t - 3)
                        if exists(kind, it, t + 1):
                            maxima(kind, it, t + 1)
                        if exists(kind, it, t - 1):
                            low(kind, it, t - 1)
                        if out:
                            take_out(kind, it, t - 3, 0)
                        factors(kind, it, t)
                        if out:
                            take_out(kind, it, t - 3, 1)

            def attention(kind, then=None):
                maxima(kind, 0, 0)
                if then is not None:
                    then()
                attend_all(ve, kind, attend)
                low(kind, 0, TOTAL[kind] - 1)
                if kind != "da":
                    for t in range(TOTAL[kind] - 3, TOTAL[kind]):
                        for m in range(2):
                            vector.drain()
                            take_out(kind, 0, t, m)

            vector.memset(eps[:], EPS)
            vector.drain().then_inc(y_ready, 1)
            vector.drain().then_inc(y_ready, 1)
            vector.drain().then_inc(boot, 1)
            ve.wait_ge(in_c, 16 * 2)
            for n in range(LEAD):
                split(n)
            norm(0)
            for c in range(4):
                split(CHUNK0["qa"] + c + LEAD)
                ve.wait_ge(qk_hi, c + 1)
                for m in range(2):
                    own, other = slice(HD * m, HD * m + HD), slice(HD * (1 - m), HD * (1 - m) + HD)
                    head = qa[c // 2][:, 2 * (c % 2) + m, :]
                    last = vector.scalar_tensor_tensor(out=head[other, :], in0=ps[c][own, :], scalar=HD ** -0.5, in1=head[own, :],
                                                       op0=ALU.mult, op1=ALU.subtract)
                last.then_inc(free[c], 1)
            split(CHUNK0["kva"] + LEAD)
            ve.wait_ge(qk_hi, 5)
            for kv in range(2):
                for half in range(2):
                    last = vector.tensor_tensor(kal[64 * half:64 * half + 64, kv, :], ps[0][64 * kv:64 * kv + 64, :],
                                                kah[64 * kv:64 * kv + 64, kv, :], ALU.subtract)
            last.then_inc(free[0], 1)
            split(CHUNK0["kva"] + 1 + LEAD)
            ve.wait_ge(qk_hi, 6)
            vector.tensor_tensor(val[:].rearrange("p a n -> p (a n)"), ps[1][:], vah[:].rearrange("p a n -> p (a n)"),
                                 ALU.subtract).then_inc(free[1], 1)
            ve.wait_ge(in_c2, 16 * 10)
            vector.tensor_copy(identb[:], masks_f[:, 2, :])
            vector.tensor_copy(causal[:], masks_f[:, 0, :])
            vector.tensor_copy(outside[:], masks_f[:, 1, :])
            vector.tensor_scalar(nsinks[:], sinks[:], -1.0, None, ALU.mult)
            vector.tensor_tensor(lam_pr[:], lam_in[:, :, 0, :], lam_in[:, :, 1, :], ALU.mult)
            vector.tensor_scalar(gains[:, 5, :], gains[:, 5, :], 1.0 - LAM_INIT, None, ALU.mult)
            vector.drain().then_inc(boot, 1)
            vector.tensor_reduce(lam_s[:], lam_pr[:], AX.X, ALU.add).then_inc(boot2, 1)
            ve.wait_ge(boot3, 1)
            vector.tensor_tensor(nlam[:], lam_e[:, 1:2], lam_e[:, 0:1], ALU.subtract)
            vector.drain()
            vector.tensor_scalar(nlam[:], nlam[:], LAM_INIT, None, ALU.subtract)
            if on("rope_r"):
                rope("rope_r", 2, qkr, qkr, rtmp)
            if on("vg"):
                splits_t("vg")
                for tt in range(TT):
                    bank_done("vg", tt, 0)
                    vector.tensor_copy(vr[:, tt, :], ps[bank_t(tt, 0)][:]).then_inc(free[bank_t(tt, 0)], 1)
            if on("ret"):
                def decayed(h):
                    if h >= 2:
                        filled("ret", 4 + h % 2, h // 2 - 1)
                    for c in range(4):
                        filled("ret", c, h)
                        w = SEQ - c * P
                        o = [0, 512, 896, 1152][c]
                        vector.tensor_tensor(STs[h % 2][:, o:o + w], ps[c][:, 0:w], decay[:, h, 0:w], ALU.mult).then_inc(free[c], 1)

                def stats(h):
                    ve.wait_ge(free[4 + h % 2], FREED["ret"][4 + h % 2] + h // 2 + 1)
                    for i in range(4):
                        vector.bn_stats(bn[:, 4 * h + i, :], CAT[:, i, 512 + h * P:512 + (h + 1) * P])
                    vector.drain()
                    for i in range(4):
                        vector.bn_aggr(mv[:, 4 * h + i, :], bn[:, 4 * h + i, :])

                decayed(0)
                for h in range(4):
                    if h < 3:
                        decayed(h + 1)
                    stats(h)
                vector.drain().then_inc(gn_mv, 1)
            if on("local"):
                def gn_scale():
                    ve.wait_ge(gn_sd, 1)
                    vector.reciprocal(grs[:], gsd[:]).then_inc(gn_rs, 1)
                attention("local", gn_scale)
            if on("cat"):
                to_ht("cat", HTh, HTl)
            if on("out1"):
                splits_t("out1")
                residual("out1", 0, KT)
            if on("norm1"):
                norm(1)
            if on("up1"):
                up_conv("up1")
            if on("down1"):
                down("down1", 1)
                residual("down1", 1, FT)
            if on("norm2"):
                norm(2)
            if on("up2"):
                up_swiglu("up2")
            if on("down2"):
                down("down2", 2)
                residual_plain("down2", 0.5, FT)
            if on("norm3"):
                norm(3)
            if on("rope_dq"):
                ve.wait_ge(in_rope, 48)
                rope("rope_dq", 2, qkd, qkd, rtmp2)
                rope("rope_dk", 2, qkd, qkd, rtmp2, 8)
            if on("vda"):
                splits_t("vda")
                for tt in range(TT):
                    bank_done("vda", tt, 0)
                    vector.tensor_copy(vd[:, tt, 0:512], ps[bank_t(tt, 0)][:]).then_inc(free[bank_t(tt, 0)], 1)
            if on("da"):
                attention("da")
            if on("nsf"):
                ve.wait_ge(da_sq, 1)
                vector.tensor_reduce(hss[:], DSQ[:].rearrange("p i (h d) -> p (i h) d", d=P), AX.X, ALU.add).then_inc(da_ss, 1)
                ve.wait_ge(da_sd, 1)
                vector.reciprocal(hrs[:], hsd[:])
                vector.drain()
                for i in range(TT):
                    r = hrs[:, i * 8:(i + 1) * 8].rearrange("p (h a) -> p h a", a=1).broadcast_to((P, 8, P))
                    blk = YD[:, i, :].rearrange("p (h d) -> p h d", d=P)
                    vector.tensor_tensor(blk, blk, r, ALU.mult).then_inc(da_fin, 1)
                for c in range(4):
                    split(CHUNK0["nsf"] + c + LEAD)
                ve.wait_ge(in_rope, 80)
                for kind in range(2):
                    vector.drain()
                    filled("nsf", 4 + kind)
                    vector.tensor_tensor(rtmp3[:], ps[4 + kind][:], sin[:], ALU.mult).then_inc(free[4 + kind], 1)
                    vector.tensor_tensor(kraw[:, kind, :], kraw[:, kind, :], cos[:], ALU.mult)
                    vector.drain()
                    for g in range(2):
                        for half in range(2):
                            last = vector.tensor_tensor(ksw[64 * half:64 * half + 64, kind, g, :], kraw[64 * g:64 * g + 64, kind, :],
                                                        rtmp3[64 * g:64 * g + 64, :], ALU.add)
                    last.then_inc(roped, 1)
                vector.drain().then_inc(ks_f, 1)
            if on("nst"):
                ve.wait_ge(ks_hi, 1)
                vector.tensor_tensor(ksl[:].rearrange("p a g n -> p (a g n)"), ksw[:].rearrange("p a g n -> p (a g n)"),
                                     ksh[:].rearrange("p a g n -> p (a g n)"), ALU.subtract)
                for c in range(3):
                    split(CHUNK0["nst"] + c + LEAD)
                    if c < 2:
                        ve.wait_ge(vs_hi, c + 1)
                        vector.tensor_tensor(vsl[:, c, :, :].rearrange("p a n -> p (a n)"), ps[c][:], vsh[:, c, :, :].rearrange("p a n -> p (a n)"),
                                             ALU.subtract).then_inc(free[c], 1)
            if on("cmp"):
                ve.wait_ge(in_cw, 80)
                vector.drain()
                vector.memset(hid4[:], 0.0)
                for kv in range(2):
                    ve.wait_ge(free[kv], FREED["nst"][kv])
                    for jp in range(2):
                        for g in range(2):
                            h = slice(64 * g, 64 * g + 64)
                            src = kcv[h, kv, :].rearrange("p (n r a) -> p r n a", r=8, a=2)
                            for part in range(2):
                                x = src[:, :, part:part + N_CMP, jp]
                                pz = posT[h, kv, 16 * part:16 * part + 16].rearrange("p (j a) -> p j a", a=2)[:, :, jp:jp + 1].broadcast_to((64, 8, N_CMP))
                                last = vector.tensor_tensor(cA[64 * jp:64 * jp + 64, kv, 8 * part:8 * part + 8, g * 31:(g + 1) * 31], x, pz, ALU.add)
                    last.then_inc(cm_a, 1)
                ve.wait_ge(free[5], FREED["cmp"][5] + 1)
                for ht in range(2):
                    src = hid[:, 1, ht, :].rearrange("p (g a n) -> p g a n", g=2, a=1).broadcast_to((P, 2, 4, N_CMP))
                    last = vector.tensor_copy(hid4[:, ht, :, :, 0:N_CMP], src)
                last.then_inc(hid_v, 1)
                vector.memset(vblk[:], 0.0)
                vector.memset(CP[:], 0.0)
                vector.drain()
                filled("cmp", 7)
                for a in range(4):
                    q = slice(32 * a, 32 * a + 32)
                    last = vector.tensor_copy(vblk[q, :, a * HD:(a + 1) * HD], ps[7][q, 0:2 * HD].rearrange("p (g d) -> p g d", g=2))
                last.then_inc(free[7], 1)
                vector.drain().then_inc(vb, 1)
            if on("rope_q"):
                rope("rope_q", 2, qn, qnr, rtmp3)
            if on("cmpa"):
                st = "cmpa"

                def wide(a):
                    return a.rearrange("p (n a) -> p n a", a=1).broadcast_to((P, 8, N_CMP))

                def cmp_shift(n):
                    u = n % 2
                    s_ = CS[:, u, :, 0:N_CMP]
                    s2 = CS[:, u, :, :].rearrange("p (j h) n -> p h j n", h=2)
                    mask = cmask[:, n % 4:n % 4 + 1, :].broadcast_to((P, 4, N_CMP))
                    for h in range(2):
                        b = 2 * h + u
                        filled(st, b, n // 2)
                        vector.tensor_tensor(s2[:, h, :, 0:N_CMP], ps[b][:, 0:P].rearrange("p (j n) -> p j n", n=32)[:, :, 0:N_CMP],
                                             mask, ALU.add).then_inc(free[b], 1)
                    vector.drain()
                    vector.tensor_reduce(cst[:, u, 0, :], s_, AX.X, ALU.max)
                    vector.drain()
                    vector.tensor_tensor(s_, s_, wide(cst[:, u, 0, :]), ALU.subtract).then_inc(cm_s, 1)

                def cmp_weigh(n):
                    u, g, i = n % 2, n // 4, n % 4
                    s_ = CS[:, u, :, 0:N_CMP]
                    ve.wait_ge(cm_e, n + 1)
                    vector.tensor_reduce(cst[:, u, 1, :], s_, AX.X, ALU.add)
                    vector.drain()
                    vector.reciprocal(cst[:, u, 1, :], cst[:, u, 1, :])
                    vector.drain()
                    gate = gates[:, i, 24 * g:24 * g + 24].rearrange("p (h c) -> p h c", c=3)[:, :, 0]
                    vector.scalar_tensor_tensor(out=cst[:, u, 2, :], in0=gate, scalar=cvalid[:, i:i + 1], in1=cst[:, u, 1, :],
                                                op0=ALU.mult, op1=ALU.mult)
                    vector.drain()
                    if n >= 2:
                        filled(st, 4 + u, n // 2 - 1)
                    vector.tensor_tensor(CP[:, u, :, 0:N_CMP], s_, wide(cst[:, u, 2, :]), ALU.mult).then_inc(cm_p, 1)

                cmp_shift(0)
                for n in range(8):
                    if n < 7:
                        cmp_shift(n + 1)
                    cmp_weigh(n)
                vector.drain()
            if on("nsa"):
                attention("nsa")
            if on("ydat"):
                to_ht("ydat", HT2h, HT2l, lambda k: gains[:, 5, k:k + 1])
            if on("ga"):
                splits_t("ga")
            if on("gb"):
                splits_t("gb")
            if on("ynst"):
                to_ht("ynst", HTh, HTl)
            if on("pda"):
                splits_t("pda")
                for tt in range(TT):
                    for half in range(2):
                        bank_done("pda", tt, half)
                        h = slice(half * 512, (half + 1) * 512)
                        vector.tensor_tensor(GA[:, tt, h], ps[bank_t(tt, half)][:], GA[:, tt, h], ALU.mult).then_inc(free[bank_t(tt, half)], 1)
            if on("pns"):
                splits_t("pns")
                for tt in range(TT):
                    for half in range(2):
                        bank_done("pns", tt, half)
                        h = slice(half * 512, (half + 1) * 512)
                        vector.tensor_tensor(GB[:, tt, h], ps[bank_t(tt, half)][:], GB[:, tt, h], ALU.mult).then_inc(free[bank_t(tt, half)], 1)
                    vector.drain()
                    vector.tensor_tensor(GA[:, tt, :], GA[:, tt, :], GB[:, tt, :], ALU.add).then_inc(merged, 1)
            if on("mt"):
                to_ht("mt", HTh, HTl)
            if on("out2"):
                splits_t("out2")
                residual_plain("out2", 1.0, KT)
            if on("norm4"):
                norm(4)
            if on("up3"):
                up_swiglu("up3")
            if on("down3"):
                down("down3", 3)
                residual_plain("down3", 0.5, FT)
                ve.wait_ge(n_std, 6)
                ve.wait_ge(in_post, 48)
                vector.reciprocal(rstd[:], std[:])
                vector.drain()
                for tt in range(TT):
                    vector.scalar_tensor_tensor(out=XN[:, tt, :], in0=X[:, tt, :], scalar=rstd[:, tt:tt + 1], in1=gpost[:],
                                                op0=ALU.mult, op1=ALU.mult).then_inc(f_out, 1)


def constants():
    pos = np.arange(SEQ, dtype=np.float32)
    c = {}
    c["c_ident"] = np.eye(P, dtype=np.float32)
    q, k = np.arange(P)[:, None], np.arange(P)[None, :]
    masks = np.zeros((P, 3, P), np.float32)
    masks[:, 0] = np.where(k > q, NEG, 0)
    masks[:, 1] = np.where(k <= q, NEG, 0)
    masks[:, 2] = np.eye(P)
    c["c_masks"] = masks
    pr = np.zeros((P, P), np.float32)
    i = np.arange(0, P, 2)
    pr[i + 1, i] = -1
    pr[i, i + 1] = 1
    c["c_perm_r"] = pr
    pn = np.zeros((P, P), np.float32)
    for b in (0, 64):
        i = b + np.arange(32)
        pn[i + 32, i] = -1
        pn[i, i + 32] = 1
    c["c_perm_n"] = pn
    ang = (np.float32(1) / np.power(np.float32(10000), np.linspace(0, 1, 64, dtype=np.float32))).astype(np.float32)
    a = (pos[:, None] * np.repeat(ang, 2)[None]).astype(np.float32).astype(np.float64).T
    c["c_cos_r"], c["c_sin_r"] = np.cos(a).astype(np.float32), np.sin(a).astype(np.float32)
    inv = (np.float32(1) / np.power(np.float32(10000), np.arange(0, 64, 2, dtype=np.float32) / np.float32(64))).astype(np.float32)
    a = (pos[:, None] * np.tile(inv, 4)[None]).astype(np.float32).astype(np.float64).T
    c["c_cos_n"], c["c_sin_n"] = np.cos(a).astype(np.float32), np.sin(a).astype(np.float32)
    dec = np.zeros((P, 4, SEQ), np.float64)
    for h in range(4):
        lg = np.log(1 - 2.0 ** (-5 - h))
        rel = np.arange(SEQ)[None, :] - np.arange(P)[:, None]
        dec[:, h] = np.where(rel >= 0, np.exp(lg * np.maximum(rel, 0)), 0) * P ** -0.5
    c["c_decay"] = dec.astype(np.float32)
    tok = (np.arange(TT)[None, :, None] * P + np.arange(P)[:, None, None])
    end = np.arange(N_CMP)[None, None, :] * 16 + 31
    c["c_cmask"] = np.where(end <= tok, 0, NEG).astype(np.float32)
    c["c_cvalid"] = (tok[:, :, 0] >= 31).astype(np.float32)
    return c


def weight_order(inp):
    def f(w, c0, n):
        for j in range(n):
            part = w[:, c0 + j * P:min(c0 + (j + 1) * P, w.shape[1])]
            yield part

    chunks = []

    def add_f(w, c0, width=P):
        part = w[:, c0:c0 + width]
        if width < P:
            part = np.pad(part, ((0, 0), (0, P - width)))
        chunks.append(part.reshape(KT, P, P).transpose(1, 0, 2).reshape(P, CHUNK))

    def add_t(w, c0=0):
        for k in range(w.shape[0] // P):
            chunks.append(w[k * P:(k + 1) * P, c0:c0 + CHUNK])

    w = inp["w_in"][0]
    for c in (0, 128, 256, 384, 512, 640):
        add_f(w, c)
    for c in range(768, 1792, P):
        add_f(w, c)
    add_t(w, 1792)
    add_t(inp["w_out"][0])
    for j in range(FT):
        add_f(inp["w_up"][0], j * P)
        add_f(inp["w_up"][0], D_FF + j * P)
    add_t(inp["w_down"][0])
    for j in range(FT):
        add_f(inp["ffn1_w1_2"][0], j * P)
        add_f(inp["ffn1_w3_2"][0], j * P)
    add_t(inp["ffn1_w2_2"][0])
    w = inp["w_in_2"][0]
    for c in range(0, 2048, P):
        add_f(w, c)
    add_t(w, 2048)
    for c in (4096, 4224, 4352, 4608, 4480, 4736):
        add_f(w, c)
    add_f(w, 4864, 48)
    for c in range(3072, 4096, P):
        add_f(w, c)
    add_t(w, 4912)
    add_t(w, 5936)
    add_t(inp["w_proj_da_2"][0])
    add_t(inp["w_proj_nsa_2"][0])
    add_t(inp["w_out_2"][0])
    for j in range(FT):
        add_f(inp["ffn2_w1_2"][0], j * P)
        add_f(inp["ffn2_w3_2"][0], j * P)
    add_t(inp["ffn2_w2_2"][0])
    assert len(chunks) == N_CHUNKS
    return np.stack(chunks)


def laid_out(inp):
    a = dict(constants())
    a["x"] = inp["x"][0]
    a["w_all"] = weight_order(inp)

    def cols(v):
        return v.reshape(-1, P).T

    g = [inp["mix_pre_norm"][0], inp["ffn_pre_norm"][0], inp["ffn1_norm_2"][0], inp["mix_norm_2"][0], inp["ffn2_norm_2"][0],
         inp["da_head_norm_2"][0].reshape(-1)]
    a["gains"] = np.stack([cols(v) for v in g], axis=1)
    a["conv"] = np.stack([cols(inp["conv_w"][0][j]) for j in range(3)] + [cols(inp["conv_b"][0])], axis=2)
    a["attn_sinks"] = inp["attn_sinks"][0]
    a["da_lambda"] = inp["da_lambda_2"][0].reshape(-1)
    a["mix_post"], a["ffn_post"], a["final"] = inp["mix_post_norm"][0], inp["ffn_post_norm"][0], inp["final_norm_2"]
    pt = inp["cmp_pos_2"][0].transpose(2, 0, 1)
    a["posT"] = np.concatenate([pt, pt], axis=0)
    a["cw1"] = inp["cmp_w1_2"][0]
    w2 = inp["cmp_w2_2"][0].reshape(2, 2, P, HD).transpose(2, 0, 1, 3)
    a["w2k"] = np.repeat(w2[:, 0][:, :, None, :], 2, axis=2)
    a["w2v"] = w2[:, 1]
    return {k: np.ascontiguousarray(v) for k, v in a.items()}


STOP = None


def kernel(**inputs):
    import concourse.bacc as bacc
    from concourse.bass_utils import run_bass_kernel_spmd

    nc = bacc.Bacc("TRN2", target_bir_lowering=False, num_devices=1)
    arrays = laid_out({k: np.asarray(v) for k, v in inputs.items()})
    t = {k: nc.dram_tensor("in_" + k, v.shape, mybir.dt.from_np(v.dtype), kind="ExternalInput").ap() for k, v in arrays.items()}
    out = nc.dram_tensor("out", (SEQ, D), F32, kind="ExternalOutput").ap()
    program(nc, t, out, STOP)
    r = run_bass_kernel_spmd(nc, [{"in_" + k: v for k, v in arrays.items()}], core_ids=[0])
    return r.results[0]["out"].reshape(1, SEQ, D)
```

```python
from contextlib import ExitStack

import numpy as np

import concourse.bass as bass
from concourse import mybir

F32 = mybir.dt.float32
F32R = mybir.dt.float32r
BF16 = mybir.dt.bfloat16
ACT = mybir.ActivationFunctionType
ALU = mybir.AluOpType
AX = mybir.AxisListType

P = 128
SEQ = 512
D = 1024
TT = SEQ // P
KT = D // P
D_FF = 2816
FT = D_FF // P
CHUNK = 1024
SLOTS = 4
LEAD = 3
EPS = 1e-6
NEG = -1e30
HD = 64
N_CMP = 31
NSA_HEADS = 16
LAM_INIT = 0.2
VG_W = 2 * P + 3 * NSA_HEADS
VG_K = CHUNK // VG_W

STAGES = [
    ("norm0", 0, [0] * 8, [1] * 8),
    ("qa", 4, [1, 1, 1, 1, 0, 0, 0, 0], [0] * 8),
    ("kva", 2, [1, 1, 0, 0, 0, 0, 0, 0], [0] * 8),
    ("rope_r", 8, [2, 2, 2, 2, 0, 0, 0, 0], [0, 0, 0, 0, 4, 4, 0, 0]),
    ("vg", 8, [1] * 8, [0] * 8),
    ("ret", 0, [0] * 8, [4, 4, 4, 4, 2, 2, 0, 0]),
    ("local", 0, [0] * 8, [8, 8, 8, 8, 16, 16, 8, 8]),
    ("cat", 0, [0] * 8, [1] * 8),
    ("out1", 8, [1] * 8, [0] * 8),
    ("norm1", 0, [0] * 8, [1] * 8),
    ("up1", 2 * FT, [FT // 2] * 4 + [0] * 4, [0] * 8),
    ("down1", FT, [1] * 8, [0] * 8),
    ("norm2", 0, [0] * 8, [1] * 8),
    ("up2", 2 * FT, [FT // 2] * 4 + [0] * 4, [0] * 8),
    ("down2", FT, [1] * 8, [0] * 8),
    ("norm3", 0, [0] * 8, [1] * 8),
    ("rope_dq", 8, [2, 2, 2, 2, 0, 0, 0, 0], [0, 0, 0, 0, 4, 4, 0, 0]),
    ("rope_dk", 8, [2, 2, 2, 2, 0, 0, 0, 0], [0, 0, 0, 0, 4, 4, 0, 0]),
    ("vda", 8, [1] * 8, [0] * 8),
    ("da", 0, [0] * 8, [16, 16, 16, 16, 16, 16, 16, 16]),
    ("nsf", 4, [1, 1, 1, 1, 0, 0, 0, 0], [0, 0, 0, 0, 1, 1, 0, 0]),
    ("nst", 3, [1, 1, 1, 1, 0, 0, 0, 0], [0] * 8),
    ("cmp", 0, [0] * 8, [0, 0, 0, 0, 1, 1, 1, 1]),
    ("rope_q", 8, [2, 2, 2, 2, 0, 0, 0, 0], [0, 0, 0, 0, 4, 4, 0, 0]),
    ("cmpa", 0, [0] * 8, [4, 4, 0, 0, 4, 4, 4, 4]),
    ("nsa", 0, [0] * 8, [32, 32, 32, 32, 64, 64, 32, 32]),
    ("ydat", 0, [0] * 8, [1] * 8),
    ("ga", 8, [1] * 8, [0] * 8),
    ("gb", 8, [1] * 8, [0] * 8),
    ("ynst", 0, [0] * 8, [1] * 8),
    ("pda", 8, [1] * 8, [0] * 8),
    ("pns", 8, [1] * 8, [0] * 8),
    ("mt", 0, [0] * 8, [1] * 8),
    ("out2", 8, [1] * 8, [0] * 8),
    ("norm4", 0, [0] * 8, [1] * 8),
    ("up3", 2 * FT, [FT // 2] * 4 + [0] * 4, [0] * 8),
    ("down3", FT, [1] * 8, [0] * 8),
]
T_STAGES = ["vg", "out1", "down1", "down2", "vda", "ga", "gb", "pda", "pns", "out2", "down3"]
NORMS = ["norm0", "norm1", "norm2", "norm3", "norm4"]
HT_STAGES = ["norm0", "cat", "norm1", "norm2", "norm3", "ydat", "ynst", "mt", "norm4"]


def counts():
    chunk, freed, filled = {}, {}, {}
    c, fr, fi = 0, [0] * 8, [0] * 8
    for name, n, streamed, other in STAGES:
        chunk[name], freed[name], filled[name] = c, list(fr), list(fi)
        c += n
        fr = [a + b + d for a, b, d in zip(fr, streamed, other)]
        fi = [a + b for a, b in zip(fi, other)]
    return chunk, freed, filled, c


CHUNK0, FREED, FILLED, N_CHUNKS = counts()


def at_least(eng, sem, value):
    if isinstance(value, int) and value <= 0:
        return
    eng.wait_ge(sem, value)


def program(nc, t, out, stop=None):
    scalar, vector, tensor, pool = nc.scalar, nc.vector, nc.tensor, nc.gpsimd
    names = [s[0] for s in STAGES]
    last_stage = len(names) if stop is None else names.index(stop)

    def on(name):
        return names.index(name) < last_stage

    n_chunks = N_CHUNKS if stop is None else CHUNK0[stop]

    with ExitStack() as ctx:
        def sb(name, shape, dt=F32):
            return ctx.enter_context(nc.sbuf_tensor(name, shape, dt))

        def sem(name):
            return ctx.enter_context(nc.semaphore(name))

        STEPS = 8
        X = sb("X", [P, TT, D])
        HTh = sb("HTh", [P, KT, SEQ], F32R)
        HTl = sb("HTl", [P, KT, SEQ], F32R)
        raw = sb("raw", [P, SLOTS, CHUNK])
        Wh = sb("Wh", [P, SLOTS, CHUNK], F32R)
        Wl = sb("Wl", [P, SLOTS, CHUNK], F32R)
        ident = sb("ident", [P, P])
        identb = sb("identb", [P, P], BF16)
        causal = sb("causal", [P, P], BF16)
        outside = sb("outside", [P, P], BF16)
        perm = sb("perm", [P, P])
        gains = sb("gains", [P, 6, KT])
        conv = sb("conv", [P, 2 * FT, 4])
        sinks = sb("sinks", [P, 8])
        nsinks = sb("nsinks", [P, 8])
        cst = sb("cst", [P, 2, 3, 8])
        lam_pr = sb("lam_pr", [P, 2, HD])
        lam_s = sb("lam_s", [P, 2])
        lam_e = sb("lam_e", [P, 2])
        nlam = sb("nlam", [P, 1])
        cmask = sb("cmask", [P, TT, N_CMP])
        cvalid = sb("cvalid", [P, TT])
        eps = sb("eps", [P, 1])
        ss = sb("ss", [P, 8])
        sst = sb("sst", [P, TT])
        std = sb("std", [P, TT])
        rstd = sb("rstd", [P, TT])
        pstd = sb("pstd", [P, TT])
        prs = sb("prs", [P, TT])
        nmx = sb("nmx", [P, 2, 2])
        rs = sb("rs", [P, 2, 2])
        esk = sb("esk", [P, 2, 2])
        rr = sb("rr", [P, STEPS, 2])
        gg = sb("gg", [P, 4, 2])
        bn = sb("bn", [P, 16, 6])
        mv = sb("mv", [P, 16, 2])
        gsd = sb("gsd", [P, 16])
        grs = sb("grs", [P, 16])
        hss = sb("hss", [P, 32])
        hsd = sb("hsd", [P, 32])
        hrs = sb("hrs", [P, 32])

        K = 1024
        spare = (nc.sbuf_base + 31) // 32 * 32
        region = spare + 8 * K
        limit = nc.sbuf_usable_end

        def at(name, kib, shape, dt=F32):
            off = region + int(kib * K)
            size = int(np.prod(shape[1:])) * 4
            assert off + size <= limit, (name, off + size, limit)
            return nc.alloc_sbuf_tensor_at(name, shape, dt, offset=off)

        gpost = at("gpost", -8, [P, D])
        cos = at("cos", -4, [P, SEQ])
        sin = at("sin", -2, [P, SEQ])
        kal = at("kal", -8, [P, 2, SEQ], F32R)
        Vst = at("Vst", -8, [P, 2, 2, SEQ], F32R)
        vsl = at("vsl", -8, [P, 2, TT, P], F32R)
        XN = at("XN", 0, [P, TT, D])
        Y = at("Y", 0, [P, FT, SEQ])
        Yh = at("Yh", 44, [P, SLOTS, SEQ], F32R)
        Yl = at("Yl", 52, [P, SLOTS, SEQ], F32R)
        U = at("U", 60, [P, 4, SEQ])
        GU = at("GU", 68, [P, 2, SEQ])
        masks_f = at("masks_f", 58, [P, 3, P])
        lam_in = at("lam_in", 60, [P, 2, 2, HD])
        qa = [at("qa0", 0, [P, 4, SEQ], F32R), at("qa1", 78, [P, 4, SEQ], F32R)]
        kah = at("kah", 8, [P, 2, SEQ], F32R)
        vah = at("vah", 12, [P, TT, P], F32R)
        val = at("val", 74, [P, TT, P], F32R)
        qkr = at("qkr", 14, [P, 8, SEQ])
        vr = at("vr", 30, [P, TT, SEQ])
        sg = at("sg", 38, [P, TT, SEQ])
        CAT = at("CAT", 46, [P, TT, D])
        Pb = at("Pb", 62, [P, 2, 2, 2 * P])
        ATh = at("ATh", 66, [P, 2, 2, 2 * P], F32R)
        ATl = at("ATl", 70, [P, 2, 2, 2 * P], F32R)
        rtmp = at("rtmp", 86, [P, SEQ])
        decay = at("decay", 88, [P, 4, SEQ])
        STs = [at(f"STs{u}", 62 + 5 * u, [P, 1280]) for u in range(2)]
        qkd = at("qkd", 0, [P, 16, SEQ])
        vd = at("vd", 48, [P, TT, D])
        YD = at("YD", 48, [P, TT, D])
        Pb2 = at("Pb2", 64, [P, 2, 2, SEQ])
        ATdh = at("ATdh", 72, [P, 2, 1, SEQ], F32R)
        ATdl = at("ATdl", 76, [P, 2, 1, SEQ], F32R)
        Qst = at("Qst", 32, [P, 2, 2, 2, SEQ], F32R)
        Kst = at("Kst", 80, [P, 2, 2, SEQ], F32R)
        rtmp2 = at("rtmp2", 78, [P, SEQ])
        DSQ = at("DSQ", 64, [P, TT, D])
        cw1k = at("cw1k", 0, [P, 16, 256])
        cw1v = at("cw1v", 16, [P, 16, 256])
        w2k = at("w2k", 32, [P, 2, 2, HD])
        w2v = at("w2v", 33, [P, 2, HD])
        posT = at("posT", 34, [P, 2, 32])
        YN = at("YN", 32, [P, TT, D])
        qn = at("qn", 0, [P, 8, SEQ])
        qnr = at("qnr", 16, [P, 8, SEQ])
        kcv = at("kcv", 64, [P, 2, SEQ])
        cA = at("cA", 68, [P, 2, 16, 62])
        hid = at("hid", 35, [P, 2, 2, 62])
        hid4 = at("hid4", 36, [P, 2, 2, 4, 32])
        kraw = at("kraw", 44, [P, 2, SEQ])
        ksw = at("ksw", 36, [P, 2, 2, SEQ])
        rtmp3 = at("rtmp3", 74, [P, SEQ])
        ksl = at("ksl", 76, [P, 2, 2, SEQ], F32R)
        ksh = at("ksh", 84, [P, 2, 2, SEQ], F32R)
        vsh = at("vsh", 92, [P, 2, TT, P], F32R)
        ATnh = at("ATnh", 0, [P, 2, 2, SEQ], F32R)
        ATnl = at("ATnl", 8, [P, 2, 2, SEQ], F32R)
        gates = at("gates", 96, [P, TT, 48])
        kcb = at("kcb", 96.75, [P, 2, 2, 32])
        QSn = at("QSn", 72, [P, 2, SEQ], F32R)
        CS = at("CS", 64, [P, 2, 8, 32])
        CP = at("CP", 66, [P, 2, 8, 32])
        CA = at("CA", 68, [P, 2, 2, P])
        vblk = at("vblk", 70, [P, 2, 4 * HD])
        HT2h = at("HT2h", 0, [P, KT, SEQ], F32R)
        HT2l = at("HT2l", 16, [P, KT, SEQ], F32R)
        GA = at("GA", 64, [P, TT, D])
        GB = at("GB", 80, [P, TT, D])

        ps = [ctx.enter_context(nc.psum_tensor(f"ps{b}", [P, 512], F32)) for b in range(8)]

        in_x = [sem(f"in_x{tt}") for tt in range(TT)]
        in_c = sem("in_c")
        in_rope = sem("in_rope")
        in_post = sem("in_post")
        in_pos = sem("in_pos")
        in_cw = sem("in_cw")
        w_raw = [sem(f"w_raw{s}") for s in range(SLOTS)]
        w_hi = sem("w_hi")
        w_lo = sem("w_lo")
        w_used = sem("w_used")
        t_done = sem("t_done")
        free = [sem(f"free{b}") for b in range(8)]
        full = [sem(f"full{b}") for b in range(8)]
        boot = sem("boot")
        boot2 = sem("boot2")
        boot3 = sem("boot3")
        x_ready = sem("x_ready")
        n_sq = sem("n_sq")
        n_rs = sem("n_rs")
        r_sum = sem("r_sum")
        r_std = sem("r_std")
        xn_ready = sem("xn_ready")
        ht_hi = sem("ht_hi")
        roped = sem("roped")
        post_used = sem("post_used")
        r_sq = sem("r_sq")
        gb_ready = sem("gb_ready")
        merged_3 = sem("merged_3")
        gn_mv = sem("gn_mv")
        gn_sd = sem("gn_sd")
        gn_rs = sem("gn_rs")
        cat_ret = sem("cat_ret")
        staged = sem("staged")
        st_hi = sem("st_hi")
        st_zero = sem("st_zero")
        st_lo = sem("st_lo")
        mx_done = sem("mx_done")
        a_ready = sem("a_ready")
        at_hi = sem("at_hi")
        qk_hi = sem("qk_hi")
        ks_f = sem("ks_f")
        ks_hi = sem("ks_hi")
        vs_hi = sem("vs_hi")
        in_c2 = sem("in_c2")
        hid_v = sem("hid_v")
        kcb_zero = sem("kcb_zero")
        vb = sem("vb")
        u_ready = sem("u_ready")
        g_ready = sem("g_ready")
        y_ready = sem("y_ready")
        y_pre_hi = sem("y_pre_hi")
        y_pre = sem("y_pre")
        da_sq = sem("da_sq")
        da_ss = sem("da_ss")
        da_sd = sem("da_sd")
        da_fin = sem("da_fin")
        cm_a = sem("cm_a")
        cm_s = sem("cm_s")
        cm_e = sem("cm_e")
        cm_p = sem("cm_p")
        merged = sem("merged")
        f_out = sem("f_out")
        s_out = sem("s_out")

        lam_stage_x = {"norm1": 0, "norm2": 1, "norm3": 2, "norm4": 3}

        MX0 = {"local": 0, "da": 32, "nsa": 96}
        AH0 = {"local": 0, "da": 32, "nsa": 64}
        PROB = {"local": Pb, "da": Pb2, "nsa": Pb2}
        TURNED = {"local": (ATh, ATl), "da": (ATdh, ATdl), "nsa": (ATnh, ATnl)}
        TOTAL = {"local": 16, "da": 32, "nsa": 64}
        BODIES = {"local": [(0, 0), (1, 0)], "da": [(0, 0), (1, 2), (3, 0)],
                  "nsa": [(0, 0), (1, 2), (3, 0), (4, 0), (5, 2), (7, 0)]}

        def exists(kind, it, t):
            return not isinstance(it, int) or 0 <= t < TOTAL[kind]

        def keys(kind, t):
            i = t % 4
            return (max(i - 1, 0), i + 1) if kind == "local" else (0, i + 1)

        def width(kind, t):
            k0, k1 = keys(kind, t)
            return (k1 - k0) * P

        def pair_uses(it, t):
            return it * (STEPS // 2) + t // 2

        def turn_uses(kind, it, t):
            return pair_uses(it, t) if kind == "da" else it * STEPS + t

        def turn_bank(kind, t, m):
            return 4 + t % 2 if kind == "da" else 4 + m

        def attend_all(eng, kind, body):
            for c, n in BODIES[kind]:
                if n:
                    with eng.Fori(0, n) as it:
                        body(kind, it, c * STEPS)
                else:
                    body(kind, 0, c * STEPS)

        def span(it, scale, const, size):
            return slice(const, const + size) if isinstance(it, int) else bass.ds(it * scale + const, size)

        def bank_t(tt, half):
            return 2 * tt + half

        block = ctx.enter_context(nc.Block())

        @block.sync
        def _(sp):
            for tt in range(TT):
                sp.dma_start(X[:, tt, :], t["x"][tt * P:(tt + 1) * P, :]).then_inc(in_x[tt], 16)
            w = t["w_all"]
            for n in range(SLOTS):
                sp.dma_start(raw[:, n, :], w[n]).then_inc(w_raw[n], 16)
            rounds = (n_chunks - SLOTS) // SLOTS
            with sp.Fori(0, rounds) as i:
                for s in range(SLOTS):
                    sp.wait_ge(w_lo, i * SLOTS + s + 1)
                    sp.dma_start(raw[:, s, :], w[bass.ds(i * SLOTS + (SLOTS + s), 1)].rearrange("a p n -> p (a n)")).then_inc(w_raw[s], 16)
            for n in range(SLOTS + rounds * SLOTS, n_chunks):
                sp.wait_ge(w_lo, n - SLOTS + 1)
                sp.dma_start(raw[:, n % SLOTS, :], w[n]).then_inc(w_raw[n % SLOTS], 16)
            if stop is None:
                for tt in range(TT):
                    sp.wait_ge(f_out, tt + 1)
                    sp.dma_start(out[tt * P:(tt + 1) * P, :], XN[:, tt, :]).then_inc(s_out, 16)
                sp.wait_ge(s_out, TT * 16)
            else:
                k = sum(4 for s in ("out1", "down1", "down2", "out2") if on(s))
                sp.wait_ge(x_ready, k)
                sp.dma_start(out.rearrange("(t p) d -> p t d", p=P), X[:]).then_inc(s_out, 16)
                sp.wait_ge(s_out, 16)

        @block.gpsimd
        def _(pl):
            def everywhere(v):
                return v.rearrange("(a n) -> a n", a=1).broadcast_to((P, v.shape[0]))

            def load(dst, src, s):
                pl.dma_start(dst, src).then_inc(s, 16)

            load(gains[:], t["gains"], in_c)
            load(ident[:], t["c_ident"], in_c)
            load(perm[:], t["c_perm_r"], in_c2)
            load(cos[:], t["c_cos_r"], in_c2)
            load(sin[:], t["c_sin_r"], in_c2)
            load(masks_f[:], t["c_masks"], in_c2)
            load(sinks[:], everywhere(t["attn_sinks"]), in_c2)
            load(lam_in[:].rearrange("p a b d -> p (a b d)"), everywhere(t["da_lambda"]), in_c2)
            load(decay[:], t["c_decay"], in_c2)
            load(conv[:], t["conv"], in_c2)
            load(cmask[:], t["c_cmask"], in_c2)
            load(cvalid[:], t["c_cvalid"], in_c2)
            if on("ret"):
                ret_out = CAT[:, :, 512:].rearrange("p i (h d) -> p i h d", d=P)
                by_tile = lambda a: a.rearrange("p (h i a) -> p i h a", i=TT, a=1).broadcast_to((P, TT, 4, P))
                pl.wait_ge(gn_rs, 1)
                pool.tensor_tensor(ret_out, ret_out, by_tile(mv[:, :, 0]), ALU.subtract)
                pool.drain()
                pool.tensor_tensor(ret_out, ret_out, by_tile(grs[:]), ALU.mult)
                pool.drain()
                for b in (1, 3, 5, 7):
                    pl.wait_ge(free[b], FREED["ret"][b])
                pool.tensor_tensor(CAT[:, :, 512:], CAT[:, :, 512:], sg[:], ALU.mult).then_inc(cat_ret, 1)
            if on("local"):
                for b in (6, 7):
                    pl.wait_ge(full[b], FILLED["cat"][b])
                load(gpost[:], everywhere(t["mix_post"]), in_post)
            if on("out1"):
                pl.wait_ge(post_used, 1)
                load(gpost[:], everywhere(t["ffn_post"]), in_post)
            if on("rope_r"):
                pl.wait_ge(roped, 8)
                load(perm[:], t["c_perm_n"], in_rope)
                load(cos[:], t["c_cos_n"], in_rope)
                load(sin[:], t["c_sin_n"], in_rope)
            if on("da"):
                def qk_low(it, head):
                    u = head % 2
                    q = qkd[:, span(it, 2, head, 1), :].rearrange("p a n -> p (a n)")
                    for m in range(2):
                        own = slice(HD * m, HD * m + HD)
                        pool.drain()
                        pl.wait_ge(st_hi, it * 8 + (4 * head + m + 1))
                        pool.tensor_tensor(Qst[own, u, m, 1, :], q[own, :], Qst[own, u, m, 0, :], ALU.subtract).then_inc(st_lo, 1)
                    pool.drain()
                    pl.wait_ge(st_hi, it * 8 + (4 * head + 3))
                    k = qkd[:, span(it, 2, 8 + head, 1), :].rearrange("p a n -> p (a n)")
                    pool.tensor_tensor(Kst[:, u, 1, :], k, Kst[:, u, 0, :], ALU.subtract).then_inc(st_lo, 1)

                def v_low(it, head):
                    u = head % 2
                    pl.wait_ge(st_hi, it * 8 + (4 * head + 4))
                    by_tile = lambda a: a.rearrange("p (t n) -> p t n", t=TT)
                    pool.tensor_tensor(by_tile(Vst[:, u, 1, :]), vd[:, :, span(it, 2 * P, head * P, P)],
                                       by_tile(Vst[:, u, 0, :]), ALU.subtract).then_inc(st_lo, 1)

                pl.wait_ge(roped, 8 + 16)
                for m in range(2):
                    other = slice(HD * (1 - m), HD * (1 - m) + HD)
                    for u in range(2):
                        last = pool.memset(Qst[other, u, m, :, :].bitcast(F32), 0.0)
                last.then_inc(st_zero, 1)
                qk_low(0, 0)
                v_low(0, 0)
                qk_low(0, 1)
                with pl.Fori(0, 3) as it:
                    for head in (1, 2):
                        v_low(it, head)
                        qk_low(it, head + 1)
                v_low(0, 7)
                for b in (6, 7):
                    pl.wait_ge(full[b], FILLED["nsf"][b])
                load(cos[:], t["c_cos_n"], in_rope)
                load(sin[:], t["c_sin_n"], in_rope)
            if on("cmp"):
                pl.wait_ge(full[7], FILLED["nsf"][7])
                load(posT[:], t["posT"], in_pos)
                load(cw1k[:], t["cw1"][0].rearrange("(j p) n -> p j n", p=P), in_cw)
                load(cw1v[:], t["cw1"][1].rearrange("(j p) n -> p j n", p=P), in_cw)
                load(w2k[:], t["w2k"], in_cw)
                load(w2v[:], t["w2v"], in_cw)
            if on("nsa"):
                pl.wait_ge(roped, 34)
                def queries(u, tile):
                    own, other = slice(HD * u, HD * u + HD), slice(HD * (1 - u), HD * (1 - u) + HD)
                    x = qnr[own, tile, :].rearrange("p a n -> p (a n)")
                    pool.tensor_copy(QSn[own, u, :], x)
                    pool.drain()
                    pool.tensor_tensor(QSn[other, u, :], x, QSn[own, u, :], ALU.subtract).then_inc(staged, 1)

                for b in (6, 7):
                    pl.wait_ge(full[b], FILLED["nsa"][b])
                for u in range(2):
                    queries(u, slice(0, 1))
                with pl.Fori(0, 7) as it:
                    for u in range(2):
                        pl.wait_ge(full[3], it * 4 + (FILLED["nsa"][3] + 2 * u + 2))
                        queries(u, bass.ds(it + 1, 1))
                for b in (6, 7):
                    pl.wait_ge(full[b], FILLED["ydat"][b])
                load(gpost[:], everywhere(t["final"]), in_post)
            if on("pns"):
                for tt in range(TT - 1):
                    pl.wait_ge(gb_ready, tt + 1)
                    pool.tensor_tensor(GA[:, tt, :], GA[:, tt, :], GB[:, tt, :], ALU.add).then_inc(merged, 1)

        @block.tensor
        def _(pe):
            def weights(k, it=0):
                pe.wait_ge(w_lo, it * 4 + (k + 1))
                return k % SLOTS

            def three(dst, a_hi, a_lo, b_hi, b_lo, start, stop):
                tensor.matmul(dst, a_hi, b_hi, start=start, stop=False)
                tensor.matmul(dst, a_hi, b_lo, start=False, stop=False)
                return tensor.matmul(dst, a_lo, b_hi, start=False, stop=stop)

            def bank_free(stage, b, k=0):
                at_least(pe, free[b], k + FREED[stage][b])

            def gemm_f(stage, c, bank, it=0, per=1, k0=0, fresh=False):
                s = weights(CHUNK0[stage] + c, it)
                bank_free(stage, bank, it * per + k0)
                for k in range(KT):
                    if fresh:
                        pe.wait_ge(free[k], FREED[stage][k])
                    a = slice(k * P, (k + 1) * P)
                    last = three(ps[bank][:], Wh[:, s, a], Wl[:, s, a], HTh[:, k, :], HTl[:, k, :], k == 0, k == KT - 1)
                last.then_inc(w_used, 1)

            def gemm_n(stage, c, bank, it=0):
                s = weights(CHUNK0[stage] + c, it)
                bank_free(stage, bank)
                for tt in range(TT):
                    q = slice(tt * P, (tt + 1) * P)
                    for k in range(KT):
                        a = slice(k * P, (k + 1) * P)
                        last = three(ps[bank][:, q], HTh[:, k, q], HTl[:, k, q], Wh[:, s, a], Wl[:, s, a], k == 0, k == KT - 1)
                last.then_inc(w_used, 1)

            def chunk_t(stage, c, lh, ll, first, final, it=0, tiles=range(TT)):
                s = weights(CHUNK0[stage] + c, it)
                for tt in tiles:
                    q = slice(tt * P, (tt + 1) * P)
                    for half in range(2):
                        b = bank_t(tt, half)
                        if first:
                            bank_free(stage, b)
                        n = slice(half * 512, (half + 1) * 512)
                        last = three(ps[b][:], lh[:, q], ll[:, q], Wh[:, s, n], Wl[:, s, n], first, final)
                        if final and b < 7:
                            last.then_inc(t_done, 1)
                last.then_inc(w_used, 1)

            def gemm_t(stage, hh=HTh, hl=HTl):
                for k in range(KT):
                    chunk_t(stage, k, hh[:, k, :], hl[:, k, :], k == 0, k == KT - 1)

            def to_ht(stage, src, ready=None):
                for tt in range(TT):
                    if ready is not None:
                        ready(tt)
                    for k in range(KT):
                        if tt == 0:
                            bank_free(stage, k)
                        last = tensor.transpose(ps[k][:, tt * P:(tt + 1) * P], src[:, tt, k * P:(k + 1) * P], ident[:])
                        if tt == TT - 1:
                            last.then_inc(full[k], 1)

            def norm(i):
                to_ht(NORMS[i], XN, lambda tt: pe.wait_ge(xn_ready, 4 * i + tt + 1))

            def rotate(stage, c, src, it, per, dst_bank, uses):
                bank_free(stage, dst_bank, it * uses[0] + uses[1])
                tensor.matmul(ps[dst_bank][:], perm[:], src, start=True, stop=True).then_inc(full[dst_bank], 1)

            def rope(stage, rounds, src, tile0):
                with pe.Fori(0, rounds) as it:
                    for c in range(4):
                        gemm_f(stage, c, c, it, 1, fresh=stage == "rope_dq" and c == 0)
                        if c:
                            pe.wait_ge(free[c - 1], it + (FREED[stage][c - 1] + 1))
                            rotate(stage, c - 1, src[:, bass.ds(it * 4 + (tile0 + c - 1), 1), :].rearrange("p a n -> p (a n)"), it, 1,
                                   4 + (c - 1) % 2, (2, (c - 1) // 2))
                    pe.wait_ge(free[3], it + (FREED[stage][3] + 1))
                    rotate(stage, 3, src[:, bass.ds(it * 4 + (tile0 + 3), 1), :].rearrange("p a n -> p (a n)"), it, 1, 5, (2, 1))

            def up(stage, rounds=FT // 2):
                with pe.Fori(0, rounds) as it:
                    for c in range(4):
                        gemm_f(stage, c, c, it, 1, fresh=c == 0)

            def down(stage):
                pe.wait_ge(y_pre, LEAD * int(stage[-1]))
                chunk_t(stage, 0, Yh[:, 0, :], Yl[:, 0, :], True, False, tiles=(2, 3, 0, 1))
                with pe.Fori(0, 4) as it:
                    for c in range(4):
                        s = (1 + c) % SLOTS
                        chunk_t(stage, 1 + c, Yh[:, s, :], Yl[:, s, :], False, False, it)
                for c in range(17, FT):
                    chunk_t(stage, c, Yh[:, c % SLOTS, :], Yl[:, c % SLOTS, :], False, c == FT - 1)

            def scores(kind, it, t):
                i, u, b2 = t % 4, t // 4 % 2, 2 * (t % 2)
                k0, k1 = keys(kind, t)
                w = width(kind, t)
                q, k = slice(i * P, (i + 1) * P), slice(k0 * P, k1 * P)
                if kind == "nsa" and i == 0:
                    pe.wait_ge(staged, it * 2 + (t // 4 + 1))
                if kind == "da" and i == 0:
                    pe.wait_ge(st_lo, it * 8 + (4 * (t // 4) + 3))
                for m in range(2):
                    b = b2 + m
                    bank_free(kind, b, pair_uses(it, t))
                    dst = ps[b][:, 0:w]
                    if kind == "nsa":
                        g = t // 32
                        tensor.matmul(dst, QSn[:, u, q], ksh[:, m, g, k], start=True, stop=False)
                        tensor.matmul(dst, QSn[:, u, q], ksl[:, m, g, k], start=False, stop=False)
                    elif kind == "da":
                        three(dst, Qst[:, u, m, 0, q], Qst[:, u, m, 1, q], Kst[:, u, 0, k], Kst[:, u, 1, k], True, False)
                    else:
                        tile = t // 4
                        two = qa[tile // 2][:, 2 * (tile % 2) + m, q]
                        tensor.matmul(dst, two, kah[:, tile // 2, k], start=True, stop=False)
                        tensor.matmul(dst, two, kal[:, tile // 2, k], start=False, stop=False)
                    if kind == "local" and i > 0:
                        tensor.matmul(ps[b][:, 0:P], identb[:], outside[:], start=False, stop=False)
                    tensor.matmul(ps[b][:, w - P:w], identb[:], causal[:], start=False, stop=True).then_inc(full[b], 1)

            def turn(kind, it, t):
                if kind == "da":
                    pe.wait_ge(a_ready, it * STEPS + (t + 1))
                for m in range(1 if kind == "da" else 2):
                    b = turn_bank(kind, t, m)
                    if kind != "da":
                        bank_free(kind, 2 * (t % 2) + m, pair_uses(it, t) + 1)
                    bank_free(kind, b, turn_uses(kind, it, t))
                    for j in range(width(kind, t) // P):
                        last = tensor.transpose(ps[b][:, j * P:(j + 1) * P], PROB[kind][:, t % 2, m, j * P:(j + 1) * P], ident[:])
                    last.then_inc(full[b], 1)

            def values(kind, it, t):
                hi, lo = TURNED[kind]
                k0, k1 = keys(kind, t)
                u = t % 2
                b = 6 + u
                n = k1 - k0
                bank_free(kind, b, pair_uses(it, t))
                if kind == "da" and t % 4 == 0:
                    pe.wait_ge(st_lo, it * 8 + (4 * (t // 4) + 4))
                for m in range(1 if kind == "da" else 2):
                    bank_free(kind, turn_bank(kind, t, m), turn_uses(kind, it, t) + 1)
                    for j in range(n):
                        a = slice(j * P, (j + 1) * P)
                        if kind == "da":
                            v = Vst[:, t // 4 % 2, 0, a], Vst[:, t // 4 % 2, 1, a]
                            dst = ps[b][:, 0:P]
                        elif kind == "nsa":
                            c = slice(t // 32 * HD, t // 32 * HD + HD)
                            v = vsh[:, m, j, c], vsl[:, m, j, c]
                            dst = ps[b][:, m * HD:(m + 1) * HD]
                        else:
                            c = slice(t // 8 * HD, t // 8 * HD + HD)
                            v = vah[:, k0 + j, c], val[:, k0 + j, c]
                            dst = ps[b][:, m * HD:(m + 1) * HD]
                        last = three(dst, hi[:, u, m, a], lo[:, u, m, a], v[0], v[1], j == 0, j == n - 1)
                last.then_inc(full[b], 1)

            def attend(kind, it, t0):
                for t in range(t0, t0 + STEPS):
                    if exists(kind, it, t - 2):
                        values(kind, it, t - 2)
                    if exists(kind, it, t + 2):
                        scores(kind, it, t + 2)
                    turn(kind, it, t)

            def attention(kind):
                if kind != "local":
                    scores(kind, 0, 0)
                    scores(kind, 0, 1)
                attend_all(pe, kind, attend)
                values(kind, 0, TOTAL[kind] - 2)
                values(kind, 0, TOTAL[kind] - 1)

            pe.wait_ge(in_c, 16 * 2)
            norm(0)
            for c in range(4):
                gemm_f("qa", c, c, fresh=c == 0)
            gemm_f("kva", 0, 0)
            gemm_n("kva", 1, 1)
            pe.wait_ge(in_c2, 16 * 10)
            pe.wait_ge(boot, 2)
            if on("rope_r"):
                rope("rope_r", 2, qkr, 0)
            if on("vg"):
                gemm_t("vg")
            if on("ret"):
                ret = "ret"
                pe.wait_ge(roped, 8)

                def ret_scores(h):
                    for c in range(4):
                        bank_free(ret, c, h)
                        tensor.matmul(ps[c][:, 0:SEQ - c * P], qkr[:, 4 + h, c * P:(c + 1) * P], qkr[:, h, c * P:],
                                      start=True, stop=True).then_inc(full[c], 1)

                def ret_values(h):
                    u = h % 2
                    bank_free(ret, 4 + u, h // 2)
                    for i in range(4):
                        for c in range(i + 1):
                            if i == c:
                                pe.wait_ge(free[c], FREED[ret][c] + h + 1)
                            o = [0, 512, 896, 1152][c]
                            last = tensor.matmul(ps[4 + u][:, i * P:(i + 1) * P], STs[u][:, o + (i - c) * P:o + (i - c + 1) * P],
                                                 vr[:, c, h * P:(h + 1) * P], start=c == 0, stop=c == i)
                    last.then_inc(full[4 + u], 1)

                for b in range(8):
                    pe.wait_ge(free[b], FREED[ret][b])
                ret_scores(0)
                for h in range(4):
                    if h < 3:
                        ret_scores(h + 1)
                    elif on("local"):
                        scores("local", 0, 0)
                        scores("local", 0, 1)
                    ret_values(h)
            if on("local"):
                attention("local")
            if on("cat"):
                def cat_ready(tt):
                    if tt == 0:
                        pe.wait_ge(cat_ret, 1)
                        for b in (6, 7):
                            pe.wait_ge(free[b], FREED["cat"][b])
                to_ht("cat", CAT, cat_ready)
            if on("out1"):
                gemm_t("out1")
            if on("norm1"):
                norm(1)
            if on("up1"):
                up("up1")
            if on("down1"):
                down("down1")
            if on("norm2"):
                norm(2)
            if on("up2"):
                up("up2")
            if on("down2"):
                down("down2")
            if on("norm3"):
                norm(3)
            if on("rope_dq"):
                pe.wait_ge(in_rope, 48)
                rope("rope_dq", 2, qkd, 0)
                rope("rope_dk", 2, qkd, 8)
            if on("vda"):
                gemm_t("vda")
            if on("da"):
                for b in range(8):
                    pe.wait_ge(free[b], FREED["da"][b])
                pe.wait_ge(st_zero, 1)
                attention("da")
            if on("nsf"):
                for c in range(4):
                    gemm_f("nsf", c, c)
                pe.wait_ge(in_rope, 80)
                for c in (2, 3):
                    pe.wait_ge(free[c], FREED["nsf"][c] + 1)
                    rotate("nsf", c, kraw[:, c - 2, :], 0, 1, 2 + c, (0, 0))
            if on("nst"):
                for c in range(3):
                    s = weights(CHUNK0["nst"] + c)
                    for tt in range(TT):
                        q = slice(tt * P, (tt + 1) * P)
                        if c == 0:
                            bank_free("nst", tt)
                        for j, k in enumerate(range(c * VG_K, min(c * VG_K + VG_K, KT))):
                            n = slice(j * VG_W, (j + 1) * VG_W)
                            last = three(ps[tt][:, 0:VG_W], HTh[:, k, q], HTl[:, k, q], Wh[:, s, n], Wl[:, s, n], k == 0, k == KT - 1)
                    last.then_inc(w_used, 1)
            if on("cmp"):
                pe.wait_ge(in_cw, 64)
                for kv in range(2):
                    pe.wait_ge(cm_a, kv + 1)
                    bank_free("cmp", 4 + kv)
                    cw = (cw1k, cw1v)[kv]
                    for ht in range(2):
                        for j in range(16):
                            last = tensor.matmul(ps[4 + kv][:, ht * 64:ht * 64 + 62], cw[:, j, ht * P:(ht + 1) * P], cA[:, kv, j, :],
                                                 start=j == 0, stop=j == 15)
                    last.then_inc(full[4 + kv], 1)
                pe.wait_ge(free[4], FREED["cmp"][4] + 1)
                bank_free("cmp", 6)
                for ht in range(2):
                    last = tensor.matmul(ps[6][:, 0:62], w2k[:, ht, :, :].rearrange("p a d -> p (a d)"), hid[:, 0, ht, :],
                                         start=ht == 0, stop=ht == 1)
                last.then_inc(full[6], 1)
                pe.wait_ge(hid_v, 1)
                bank_free("cmp", 7)
                for g in range(2):
                    for ht in range(2):
                        last = tensor.matmul(ps[7][:, g * HD:(g + 1) * HD], hid4[:, ht, g, :, :].rearrange("p a n -> p (a n)"), w2v[:, ht, :],
                                             start=ht == 0, stop=ht == 1)
                last.then_inc(full[7], 1)
            if on("rope_q"):
                rope("rope_q", 2, qn, 0)
            if on("cmpa"):
                st = "cmpa"
                for b in range(8):
                    pe.wait_ge(free[b], FREED[st][b])
                pe.wait_ge(vb, 1)

                def cmp_scores(n):
                    g, i = n // 4, n % 4
                    b = n % 2
                    bank_free(st, b, n // 2)
                    for j in range(4):
                        last = tensor.matmul(ps[b][:, j * 64:(j + 1) * 64], qn[:, 4 * g + j, i * P:(i + 1) * P],
                                             kcb[:, g, :, :].rearrange("p h n -> p (h n)"), start=True, stop=True)
                    last.then_inc(full[b], 1)

                def cmp_turn(n):
                    pe.wait_ge(cm_p, n + 1)
                    b = 4 + n % 2
                    bank_free(st, b, n // 2)
                    for f in range(2):
                        last = tensor.transpose(ps[b][:, f * P:(f + 1) * P], CP[:, n % 2, 4 * f:4 * f + 4, :].rearrange("p h n -> p (h n)"), ident[:])
                    last.then_inc(full[b], 1)

                def cmp_values(n):
                    pe.wait_ge(free[4 + n % 2], FREED[st][4 + n % 2] + n // 2 + 1)
                    b = 6 + n % 2
                    bank_free(st, b, n // 2)
                    for f in range(2):
                        last = tensor.matmul(ps[b][:, f * 256:(f + 1) * 256], CA[:, n % 2, f, :], vblk[:, n // 4, :], start=True, stop=True)
                    last.then_inc(full[b], 1)

                cmp_scores(0)
                cmp_scores(1)
                for n in range(8):
                    if n < 6:
                        cmp_scores(n + 2)
                    if n:
                        cmp_values(n - 1)
                    cmp_turn(n)
                cmp_values(7)
            if on("nsa"):
                for b in range(6):
                    pe.wait_ge(free[b], FREED["nsa"][b])
                attention("nsa")
            if on("ydat"):
                to_ht("ydat", YD, lambda tt: pe.wait_ge(da_fin, tt + 1))
            if on("ga"):
                gemm_t("ga")
            if on("gb"):
                gemm_t("gb")
            if on("ynst"):
                for b in (6, 7):
                    pe.wait_ge(free[b], FREED["ydat"][b])
                to_ht("ynst", YN)
            if on("pda"):
                gemm_t("pda", HT2h, HT2l)
            if on("pns"):
                gemm_t("pns")
            if on("mt"):
                to_ht("mt", GA, lambda tt: pe.wait_ge(merged, tt + 1) if tt < 3 else pe.wait_ge(merged_3, 1))
            if on("out2"):
                gemm_t("out2")
            if on("norm4"):
                norm(4)
            if on("up3"):
                up("up3")
            if on("down3"):
                down("down3")

        @block.scalar
        def _(ac):
            def split(k, it=0):
                if isinstance(it, int) and k + 4 * it >= n_chunks:
                    return
                s = k % SLOTS
                ac.wait_ge(w_raw[s], it * 16 + 16 * (k // SLOTS + 1))
                at_least(ac, w_used, it * 4 + (k - SLOTS + 1))
                scalar.copy(Wh[:, s, :], raw[:, s, :]).then_inc(w_hi, 1)

            def chunk_done(stage, c, it=0):
                ac.wait_ge(w_used, it * 4 + (CHUNK0[stage] + c + 1))

            def filled(stage, b, k=0):
                ac.wait_ge(full[b], k + (FILLED[stage][b] + 1))

            def bank_done(stage, tt, half, n=KT):
                b = bank_t(tt, half)
                if b < 7:
                    ac.wait_ge(t_done, 7 * T_STAGES.index(stage) + b + 1)
                else:
                    chunk_done(stage, n - 1)

            def splits_t(stage, n=KT):
                for c in range(n):
                    split(CHUNK0[stage] + c + LEAD)

            def to_ht(stage, dst, gain=None):
                for k in range(KT):
                    filled(stage, k)
                    if gain is None:
                        scalar.copy(dst[:, k, :], ps[k][:]).then_inc(ht_hi, 1)
                    else:
                        scalar.activation(dst[:, k, :], ps[k][:], ACT.Copy, scale=gain(k)).then_inc(ht_hi, 1)

            def squares(i, tt):
                if i == 0:
                    ac.wait_ge(in_x[tt], 16)
                else:
                    ac.wait_ge(x_ready, 4 * (i - 1) + tt + 1)
                one = slice(tt, tt + 1)
                scalar.activation(XN[:, tt, :], X[:, tt, :], ACT.Square, accum_out=sst[:, one])
                scalar.drain()
                scalar.activation(std[:, one], sst[:, one], ACT.Sqrt, scale=1.0 / D, bias=eps[:]).then_inc(n_sq, 1)

            def scale(i, tt):
                ac.wait_ge(n_rs, 4 * i + tt + 1)
                scalar.activation(XN[:, tt, :], X[:, tt, :], ACT.Copy, scale=rstd[:, tt:tt + 1]).then_inc(xn_ready, 1)

            def norm(i, *before):
                parts = (*before, squares, scale)
                for step in range(TT + len(parts) - 1):
                    for lag, f in enumerate(parts):
                        if 0 <= step - lag < TT:
                            f(i, step - lag)
                if i == 0:
                    split(0)
                to_ht(NORMS[i], HTh, lambda k: gains[:, i, k:k + 1])

            def rope(stage, rounds, dst, tile0, factor=1.0):
                with ac.Fori(0, rounds) as it:
                    for c in range(4):
                        split(CHUNK0[stage] + c + LEAD, it)
                        chunk_done(stage, c, it)
                        scalar.activation(dst[:, bass.ds(it * 4 + (tile0 + c), 1), :].rearrange("p a n -> p (a n)"), ps[c][:], ACT.Copy,
                                          scale=factor).then_inc(free[c], 1)

            def product_squares(i, tt):
                stage, n = ("out1", KT) if i == 1 else ("down1", FT)
                for half in range(2):
                    bank_done(stage, tt, half, n)
                    b = bank_t(tt, half)
                    scalar.activation(XN[:, tt, half * 512:(half + 1) * 512], ps[b][:], ACT.Square,
                                      accum_out=ss[:, b:b + 1]).then_inc(r_sq, 1)

            def product_root(i, tt):
                ac.wait_ge(r_sum, 4 * (i - 1) + tt + 1)
                scalar.activation(pstd[:, tt:tt + 1], pstd[:, tt:tt + 1], ACT.Sqrt, scale=1.0 / D, bias=eps[:]).then_inc(r_std, 1)

            def up_conv(stage, i):
                def body(it):
                    for c in range(4):
                        split(CHUNK0[stage] + c + LEAD, it)
                        tile = it * 2 + (c // 2) if c % 2 == 0 else it * 2 + (FT + c // 2)
                        if c % 2 == 0:
                            ac.wait_ge(y_ready, it * 2 + (c // 2 + 1))
                        chunk_done(stage, c, it)
                        cw = conv[:, bass.ds(tile, 1), :].rearrange("p a n -> p (a n)")
                        scalar.activation(U[:, c, :], ps[c][:], ACT.Identity, scale=cw[:, 2:3], bias=cw[:, 3:4]).then_inc(u_ready, 1)
                        if c % 2:
                            ac.wait_ge(free[c - 1], it + (FREED[stage][c - 1] + 1))
                            scalar.activation(GU[:, c // 2, :], U[:, c - 1, :], ACT.Gelu_apprx_tanh).then_inc(g_ready, 1)

                with ac.Fori(0, FT // 2 - 1) as it:
                    body(it)
                first_high(stage, i)
                body(FT // 2 - 1)

            def up_swiglu(stage, i):
                def body(it):
                    for c in range(4):
                        split(CHUNK0[stage] + c + LEAD, it)
                        if c % 2 == 0:
                            at_least(ac, free[c + 1], it + FREED[stage][c + 1])
                            chunk_done(stage, c, it)
                            scalar.activation(GU[:, c // 2, :], ps[c][:], ACT.Silu).then_inc(free[c], 1)

                with ac.Fori(0, FT // 2 - 1) as it:
                    body(it)
                first_high(stage, i)
                body(FT // 2 - 1)

            def first_high(stage, i):
                if i == 1:
                    ac.wait_ge(y_ready, LEAD + 2)
                else:
                    ac.wait_ge(free[1], FREED[stage][1] + 2)
                    ac.wait_ge(free[3], FREED[stage][3] + 1)
                for k in range(LEAD):
                    last = scalar.copy(Yh[:, k, :], Y[:, k, :])
                last.then_inc(y_pre_hi, 1)

            def down(stage, i):
                if i == 1:
                    ac.wait_ge(y_ready, FT + 2)
                else:
                    for b in (1, 3):
                        ac.wait_ge(free[b], FREED[stage][b])

                def step(c, it=0):
                    k = c + LEAD
                    if not (isinstance(it, int) and k >= FT):
                        at_least(ac, w_used, it * 4 + (CHUNK0[stage] + k - SLOTS + 1))
                        scalar.copy(Yh[:, k % SLOTS, :], Y[:, bass.ds(it * 4 + k, 1), :].rearrange("p a n -> p (a n)")
                                    if not isinstance(it, int) else Y[:, k, :])
                        if isinstance(it, int) and CHUNK0[stage] + k >= n_chunks:
                            assert False
                    split(CHUNK0[stage] + k, it)

                step(0)
                with ac.Fori(0, 4) as it:
                    for c in range(4):
                        step(1 + c, it)
                for c in range(17, FT):
                    step(c)

            def exps(kind, it, t):
                w = width(kind, t)
                u = t % 2
                if kind == "local":
                    ac.wait_ge(mx_done, MX0[kind] + 2 * t + 2)
                    for m in range(2):
                        hd = 2 * (t // 4) + m
                        scalar.activation(esk[:, u, m:m + 1], sinks[:, hd:hd + 1], ACT.Exp, bias=nmx[:, u, m:m + 1])
                for m in range(2):
                    b = 2 * u + m
                    if kind != "local":
                        ac.wait_ge(mx_done, it * (2 * STEPS) + (MX0[kind] + 2 * t + m + 1))
                    scalar.activation(PROB[kind][:, u, m, 0:w], ps[b][:, 0:w], ACT.Exp, bias=nmx[:, u, m:m + 1],
                                      accum_out=rs[:, u, m:m + 1]).then_inc(free[b], 1)

            def high(kind, it, t):
                hi = TURNED[kind][0]
                w = width(kind, t)
                u = t % 2
                for m in range(1 if kind == "da" else 2):
                    b = turn_bank(kind, t, m)
                    filled(kind, b, turn_uses(kind, it, t))
                    if m == 0:
                        at_least(ac, full[6 + u], pair_uses(it, t) + FILLED[kind][6 + u])
                    scalar.copy(hi[:, u, m, 0:w], ps[b][:, 0:w]).then_inc(at_hi, 1)

            def da_out(it, t):
                u = t % 2
                if isinstance(it, int) and t >= TOTAL["da"] - 2:
                    filled("da", 6 + u, pair_uses(it, t))
                scalar.activation(YD[:, t % 4, span(it, 2 * P, t // 4 * P, P)], ps[6 + u][:, 0:P], ACT.Copy,
                                  scale=rr[:, t % STEPS, 0:1]).then_inc(free[6 + u], 1)

            def attend(kind, it, t0):
                for t in range(t0, t0 + STEPS):
                    if kind == "local" and t == 6:
                        ac.wait_ge(gn_mv, 1)
                        scalar.activation(gsd[:], mv[:, :, 1], ACT.Sqrt, bias=eps[:]).then_inc(gn_sd, 1)
                    if kind == "da" and exists(kind, it, t - 3):
                        da_out(it, t - 3)
                    high(kind, it, t)
                    if kind == "da":
                        if t % 4 == 1 and exists(kind, it, t + 4):
                            high_parts(it, t // 4 + 1, 1)
                        if t % 4 == 3 and exists(kind, it, t + 5):
                            high_parts(it, t // 4 + 2, 0)
                    if exists(kind, it, t + 2):
                        exps(kind, it, t + 2)

            def attention(kind):
                if kind != "local":
                    exps(kind, 0, 0)
                exps(kind, 0, 1)
                attend_all(ac, kind, attend)
                if kind == "da":
                    for t in range(TOTAL[kind] - 3, TOTAL[kind]):
                        da_out(0, t)

            def high_parts(it, head, which):
                u = head % 2
                if which == 0:
                    q = qkd[:, span(it, 2, head, 1), :].rearrange("p a n -> p (a n)")
                    for m in range(2):
                        own = slice(HD * m, HD * m + HD)
                        scalar.copy(Qst[own, u, m, 0, :], q[own, :]).then_inc(st_hi, 1)
                    k = qkd[:, span(it, 2, 8 + head, 1), :].rearrange("p a n -> p (a n)")
                    scalar.copy(Kst[:, u, 0, :], k).then_inc(st_hi, 1)
                else:
                    scalar.copy(Vst[:, u, 0, :].rearrange("p (t n) -> p t n", t=TT), vd[:, :, span(it, 2 * P, head * P, P)]).then_inc(st_hi, 1)

            ac.wait_ge(boot, 1)
            ac.wait_ge(in_c, 16 * 2)
            norm(0)
            for n in range(1, LEAD):
                split(n)
            for c in range(4):
                split(CHUNK0["qa"] + c + LEAD)
                chunk_done("qa", c)
                for m in range(2):
                    own = slice(HD * m, HD * m + HD)
                    last = scalar.activation(qa[c // 2][own, 2 * (c % 2) + m, :], ps[c][own, :], ACT.Copy, scale=HD ** -0.5)
                last.then_inc(qk_hi, 1)
            split(CHUNK0["kva"] + LEAD)
            chunk_done("kva", 0)
            for kv in range(2):
                for half in range(2):
                    last = scalar.copy(kah[64 * half:64 * half + 64, kv, :], ps[0][64 * kv:64 * kv + 64, :])
            last.then_inc(qk_hi, 1)
            split(CHUNK0["kva"] + 1 + LEAD)
            chunk_done("kva", 1)
            scalar.copy(vah[:].rearrange("p a n -> p (a n)"), ps[1][:]).then_inc(qk_hi, 1)
            ac.wait_ge(boot2, 1)
            scalar.activation(lam_e[:], lam_s[:], ACT.Exp).then_inc(boot3, 1)
            if on("rope_r"):
                rope("rope_r", 2, qkr, 0)
            if on("vg"):
                splits_t("vg")
                for tt in range(TT):
                    bank_done("vg", tt, 1)
                    scalar.activation(sg[:, tt, :], ps[bank_t(tt, 1)][:], ACT.Silu).then_inc(free[bank_t(tt, 1)], 1)
            if on("ret"):
                for h in range(4):
                    if h == 3 and on("local"):
                        exps("local", 0, 0)
                    filled("ret", 4 + h % 2, h // 2)
                    scalar.copy(CAT[:, :, 512 + h * P:512 + (h + 1) * P], ps[4 + h % 2][:].rearrange("p (i n) -> p i n", i=4)).then_inc(free[4 + h % 2], 1)
            if on("local"):
                attention("local")
            if on("cat"):
                to_ht("cat", HTh)
            if on("out1"):
                splits_t("out1")
                if not on("norm1"):
                    for tt in range(TT):
                        product_squares(1, tt)
                        product_root(1, tt)
            if on("norm1"):
                norm(1, product_squares, product_root)
            if on("up1"):
                up_conv("up1", 1)
            if on("down1"):
                down("down1", 1)
            if on("norm2"):
                norm(2, product_squares, product_root)
            if on("up2"):
                up_swiglu("up2", 2)
            if on("down2"):
                down("down2", 2)
            if on("norm3"):
                norm(3)
            if on("rope_dq"):
                rope("rope_dq", 2, qkd, 0, HD ** -0.5)
                rope("rope_dk", 2, qkd, 8)
            if on("vda"):
                for c in range(KT):
                    split(CHUNK0["vda"] + c + LEAD)
                    if c == 3 and on("da"):
                        ac.wait_ge(roped, 24)
                        high_parts(0, 0, 0)
                for tt in range(TT):
                    bank_done("vda", tt, 1)
                    scalar.copy(vd[:, tt, 512:], ps[bank_t(tt, 1)][:]).then_inc(free[bank_t(tt, 1)], 1)
            if on("da"):
                ac.wait_ge(free[6], FREED["da"][6])
                high_parts(0, 0, 1)
                high_parts(0, 1, 0)
                attention("da")
            if on("nsf"):
                scalar.drain()
                scalar.activation(DSQ[:], YD[:], ACT.Square).then_inc(da_sq, 1)
                ac.wait_ge(da_ss, 1)
                scalar.activation(hsd[:], hss[:], ACT.Sqrt, scale=1.0 / P, bias=eps[:]).then_inc(da_sd, 1)
                for c in range(4):
                    split(CHUNK0["nsf"] + c + LEAD)
                    chunk_done("nsf", c)
                    dst = kcv[:, c, :] if c < 2 else kraw[:, c - 2, :]
                    scalar.copy(dst, ps[c][:]).then_inc(free[c], 1)
                ac.wait_ge(ks_f, 1)
                scalar.copy(ksh[:].rearrange("p a g n -> p (a g n)"), ksw[:].rearrange("p a g n -> p (a g n)")).then_inc(ks_hi, 1)
            if on("nst"):
                for c in range(3):
                    split(CHUNK0["nst"] + c + LEAD)
                chunk_done("nst", 2)
                for tt in range(TT):
                    scalar.copy(vsh[:, :, tt, :], ps[tt][:, 0:2 * P].rearrange("p (a n) -> p a n", a=2))
                for tt in range(TT):
                    scalar.activation(gates[:, tt, :], ps[tt][:, 2 * P:VG_W], ACT.Sigmoid).then_inc(vs_hi, 1)
            if on("cmp"):
                for kv in range(2):
                    filled("cmp", 4 + kv)
                    scalar.activation(hid[:, kv, :, :], ps[4 + kv][:, 0:128].rearrange("p (a n) -> p a n", a=2)[:, :, 0:62],
                                      ACT.Gelu_apprx_tanh).then_inc(free[4 + kv], 1)
                filled("cmp", 6)
                ac.wait_ge(kcb_zero, 1)
                for u in range(2):
                    h = slice(HD * u, HD * u + HD)
                    last = scalar.copy(kcb[h, :, u, 0:N_CMP], ps[6][h, 0:2 * N_CMP].rearrange("p (g n) -> p g n", g=2))
                last.then_inc(free[6], 1)
            if on("rope_q"):
                rope("rope_q", 2, qn, 0, HD ** -0.5)
            if on("cmpa"):
                st = "cmpa"

                def cmp_exp(n):
                    ac.wait_ge(cm_s, n + 1)
                    scalar.activation(CS[:, n % 2, :, 0:N_CMP], CS[:, n % 2, :, 0:N_CMP], ACT.Exp).then_inc(cm_e, 1)

                def cmp_out(n):
                    filled(st, 6 + n % 2, n // 2)
                    g = n // 4
                    scalar.copy(YN[:, n % 4, 512 * g:512 * g + 512], ps[6 + n % 2][:]).then_inc(free[6 + n % 2], 1)

                cmp_exp(0)
                for n in range(8):
                    if n < 7:
                        cmp_exp(n + 1)
                    filled(st, 4 + n % 2, n // 2)
                    scalar.copy(CA[:, n % 2, :, :].rearrange("p f n -> p (f n)"), ps[4 + n % 2][:, 0:2 * P]).then_inc(free[4 + n % 2], 1)
                    if n:
                        cmp_out(n - 1)
                cmp_out(7)
            if on("nsa"):
                attention("nsa")
            if on("ydat"):
                to_ht("ydat", HT2h, lambda k: gains[:, 5, k:k + 1])
            if on("ga"):
                splits_t("ga")
                for tt in range(TT):
                    for half in range(2):
                        bank_done("ga", tt, half)
                        scalar.activation(GA[:, tt, half * 512:(half + 1) * 512], ps[bank_t(tt, half)][:], ACT.Sigmoid).then_inc(free[bank_t(tt, half)], 1)
            if on("gb"):
                splits_t("gb")
                for tt in range(TT):
                    for half in range(2):
                        bank_done("gb", tt, half)
                        scalar.activation(GB[:, tt, half * 512:(half + 1) * 512], ps[bank_t(tt, half)][:], ACT.Sigmoid).then_inc(free[bank_t(tt, half)], 1)
            if on("ynst"):
                to_ht("ynst", HTh)
            if on("pda"):
                splits_t("pda")
            if on("pns"):
                splits_t("pns")
            if on("mt"):
                to_ht("mt", HTh)
            if on("out2"):
                splits_t("out2")
            if on("norm4"):
                norm(4)
            if on("up3"):
                up_swiglu("up3", 3)
            if on("down3"):
                down("down3", 3)
                for tt in range(TT):
                    squares(5, tt)

        @block.vector
        def _(ve):
            def split(k, it=0):
                if isinstance(it, int) and k + 4 * it >= n_chunks:
                    return
                s = k % SLOTS
                ve.wait_ge(w_hi, it * 4 + (k + 1))
                vector.tensor_tensor(Wl[:, s, :], raw[:, s, :], Wh[:, s, :], ALU.subtract).then_inc(w_lo, 1)

            def chunk_done(stage, c, it=0):
                ve.wait_ge(w_used, it * 4 + (CHUNK0[stage] + c + 1))

            def filled(stage, b, k=0):
                ve.wait_ge(full[b], k + (FILLED[stage][b] + 1))

            def bank_done(stage, tt, half, n=KT):
                b = bank_t(tt, half)
                if b < 7:
                    ve.wait_ge(t_done, 7 * T_STAGES.index(stage) + b + 1)
                else:
                    chunk_done(stage, n - 1)

            def splits_t(stage, n=KT):
                for c in range(n):
                    split(CHUNK0[stage] + c + LEAD)

            def to_ht(stage, hi, lo, gain=None):
                for k in range(KT):
                    ve.wait_ge(ht_hi, 8 * HT_STAGES.index(stage) + k + 1)
                    if gain is None:
                        vector.tensor_tensor(lo[:, k, :], ps[k][:], hi[:, k, :], ALU.subtract).then_inc(free[k], 1)
                    else:
                        vector.scalar_tensor_tensor(out=lo[:, k, :], in0=ps[k][:], scalar=gain(k), in1=hi[:, k, :],
                                                    op0=ALU.mult, op1=ALU.subtract).then_inc(free[k], 1)

            def root(i, tt):
                ve.wait_ge(n_sq, 4 * i + tt + 1)
                one = slice(tt, tt + 1)
                return vector.reciprocal(rstd[:, one], std[:, one])

            def norm(i, *before):
                n = len(before)
                for step in range(TT + n):
                    for lag, f in enumerate((*before, lambda tt: root(i, tt).then_inc(n_rs, 1))):
                        if 0 <= step - lag < TT:
                            f(step - lag)
                if i == 0:
                    split(0)
                to_ht(NORMS[i], HTh, HTl, lambda k: gains[:, i, k:k + 1])

            def turn_rope(stage, src, dst, bank, use, tmp):
                vector.drain()
                filled(stage, bank, use)
                vector.tensor_tensor(tmp, ps[bank][:], sin[:], ALU.mult).then_inc(free[bank], 1)
                vector.tensor_tensor(dst, src, cos[:], ALU.mult)
                vector.drain()
                vector.tensor_tensor(dst, dst, tmp, ALU.add).then_inc(roped, 1)

            def rope(stage, rounds, src, dst, tmp, tile0=0):
                with ve.Fori(0, rounds) as it:
                    for c in range(4):
                        split(CHUNK0[stage] + c + LEAD, it)
                        tile = bass.ds(it * 4 + (tile0 + c), 1)
                        turn_rope(stage, src[:, tile, :].rearrange("p a n -> p (a n)"), dst[:, tile, :].rearrange("p a n -> p (a n)"),
                                  4 + c % 2, it * 2 + c // 2, tmp[:])

            def post_gain(i, tt):
                one = slice(tt, tt + 1)
                for half in range(2):
                    b = bank_t(tt, half)
                    ve.wait_ge(r_sq, 8 * i + b + 1)
                    if b == 0:
                        ve.wait_ge(in_post, 16 * (i + 1))
                    h = slice(half * 512, (half + 1) * 512)
                    vector.tensor_tensor(XN[:, tt, h], ps[b][:], gpost[:, h], ALU.mult).then_inc(free[b], 1)
                vector.tensor_tensor(pstd[:, one], ss[:, 2 * tt:2 * tt + 1], ss[:, 2 * tt + 1:2 * tt + 2], ALU.add).then_inc(r_sum, 1)

            def post_add(i, tt):
                one = slice(tt, tt + 1)
                ve.wait_ge(r_std, 4 * i + tt + 1)
                vector.reciprocal(prs[:, one], pstd[:, one])
                last = vector.drain()
                if tt == TT - 1:
                    last.then_inc(post_used, 1)
                vector.scalar_tensor_tensor(out=X[:, tt, :], in0=XN[:, tt, :], scalar=prs[:, one], in1=X[:, tt, :],
                                            op0=ALU.mult, op1=ALU.add).then_inc(x_ready, 1)

            def residual_plain(stage, factor, n, tt):
                for half in range(2):
                    bank_done(stage, tt, half, n)
                    h = slice(half * 512, (half + 1) * 512)
                    vector.scalar_tensor_tensor(out=X[:, tt, h], in0=ps[bank_t(tt, half)][:], scalar=factor, in1=X[:, tt, h],
                                                op0=ALU.mult, op1=ALU.add).then_inc(free[bank_t(tt, half)], 1)
                vector.drain().then_inc(x_ready, 1)

            def up_conv(stage, i):
                def body(it):
                    for c in range(4):
                        split(CHUNK0[stage] + c + LEAD, it)
                        tile = it * 2 + (c // 2) if c % 2 == 0 else it * 2 + (FT + c // 2)
                        cw = conv[:, bass.ds(tile, 1), :].rearrange("p a n -> p (a n)")
                        ve.wait_ge(u_ready, it * 4 + (c + 1))
                        vector.scalar_tensor_tensor(out=U[:, c, 1:], in0=ps[c][:, 0:SEQ - 1], scalar=cw[:, 1:2], in1=U[:, c, 1:],
                                                    op0=ALU.mult, op1=ALU.add)
                        vector.drain()
                        vector.scalar_tensor_tensor(out=U[:, c, 2:], in0=ps[c][:, 0:SEQ - 2], scalar=cw[:, 0:1], in1=U[:, c, 2:],
                                                    op0=ALU.mult, op1=ALU.add).then_inc(free[c], 1)
                        if c % 2:
                            vector.drain()
                            ve.wait_ge(g_ready, it * 2 + (c // 2 + 1))
                            vector.tensor_tensor(Y[:, bass.ds(it * 2 + c // 2, 1), :].rearrange("p a n -> p (a n)"), GU[:, c // 2, :], U[:, c, :],
                                                 ALU.mult).then_inc(y_ready, 1)

                with ve.Fori(0, FT // 2 - 1) as it:
                    body(it)
                first_low(i)
                body(FT // 2 - 1)

            def up_swiglu(stage, i):
                def body(it):
                    for c in range(4):
                        split(CHUNK0[stage] + c + LEAD, it)
                        if c % 2:
                            ve.wait_ge(free[c - 1], it + (FREED[stage][c - 1] + 1))
                            chunk_done(stage, c, it)
                            vector.tensor_tensor(Y[:, bass.ds(it * 2 + c // 2, 1), :].rearrange("p a n -> p (a n)"), ps[c][:], GU[:, c // 2, :],
                                                 ALU.mult).then_inc(free[c], 1)

                with ve.Fori(0, FT // 2 - 1) as it:
                    body(it)
                first_low(i)
                body(FT // 2 - 1)

            def first_low(i):
                ve.wait_ge(y_pre_hi, i)
                for k in range(LEAD):
                    vector.tensor_tensor(Yl[:, k, :], Y[:, k, :], Yh[:, k, :], ALU.subtract).then_inc(y_pre, 1)

            def down(stage, i):
                vector.drain()

                def step(c, it=0):
                    k = c + LEAD
                    if not (isinstance(it, int) and k >= FT):
                        ve.wait_ge(w_hi, it * 4 + (CHUNK0[stage] + k + 1))
                        src = Y[:, k, :] if isinstance(it, int) else Y[:, bass.ds(it * 4 + k, 1), :].rearrange("p a n -> p (a n)")
                        vector.tensor_tensor(Yl[:, k % SLOTS, :], src, Yh[:, k % SLOTS, :], ALU.subtract)
                    split(CHUNK0[stage] + k, it)

                step(0)
                with ve.Fori(0, 4) as it:
                    for c in range(4):
                        step(1 + c, it)
                for c in range(17, FT):
                    step(c)

            def maxima(kind, it, t):
                w = width(kind, t)
                u = t % 2
                for m in range(2):
                    filled(kind, 2 * u + m, pair_uses(it, t))
                    last = vector.tensor_reduce(nmx[:, u, m:m + 1], ps[2 * u + m][:, 0:w], AX.X, ALU.max, negate=True)
                    if kind != "local":
                        last.then_inc(mx_done, 1)
                if kind == "local":
                    vector.drain()
                    hd = 2 * (t // 4)
                    vector.tensor_tensor(nmx[:, u, :], nmx[:, u, :], nsinks[:, hd:hd + 2], ALU.min).then_inc(mx_done, 2)

            def exps_done(kind, it, t):
                for m in range(2):
                    b = 2 * (t % 2) + m
                    ve.wait_ge(free[b], pair_uses(it, t) + (FREED[kind][b] + 1))

            def combine(it, t):
                w = width("da", t)
                u, v = t % 2, t % 4
                exps_done("da", it, t)
                vector.reciprocal(rr[:, t % STEPS, :], rs[:, u, :])
                vector.drain()
                vector.scalar_tensor_tensor(out=gg[:, v, 0:1], in0=rs[:, u, 0:1], scalar=nlam[:], in1=rr[:, t % STEPS, 1:2],
                                            op0=ALU.mult, op1=ALU.mult)
                vector.drain()
                vector.scalar_tensor_tensor(out=Pb2[:, u, 0, 0:w], in0=Pb2[:, u, 1, 0:w], scalar=gg[:, v, 0:1], in1=Pb2[:, u, 0, 0:w],
                                            op0=ALU.mult, op1=ALU.add).then_inc(a_ready, 1)

            def factors(kind, it, t):
                u, v = t % 2, t % 4
                exps_done(kind, it, t)
                if kind == "local":
                    vector.tensor_tensor(rs[:, u, :], rs[:, u, :], esk[:, u, :], ALU.add)
                    vector.drain()
                    vector.reciprocal(gg[:, v, :], rs[:, u, :])
                else:
                    vector.reciprocal(rr[:, v, :], rs[:, u, :])
                    vector.drain()
                    vector.tensor_tensor(gg[:, v, :], rr[:, v, :], gates[:, v, span(it, 6, 3 * (t // 4) + 1, 2)], ALU.mult)

            def low(kind, it, t):
                hi, lo = TURNED[kind]
                w = width(kind, t)
                u = t % 2
                ms = 1 if kind == "da" else 2
                for m in range(ms):
                    b = turn_bank(kind, t, m)
                    ve.wait_ge(at_hi, it * (ms * STEPS) + (AH0[kind] + ms * t + m + 1))
                    vector.tensor_tensor(lo[:, u, m, 0:w], ps[b][:, 0:w], hi[:, u, m, 0:w], ALU.subtract).then_inc(free[b], 1)

            def take_out(kind, it, t, m):
                u, v = t % 2, t % 4
                if m == 0:
                    filled(kind, 6 + u, pair_uses(it, t))
                src = ps[6 + u][:, m * HD:(m + 1) * HD]
                if kind == "local":
                    hd = 2 * (t // 4) + m
                    last = vector.tensor_scalar(CAT[:, v, hd * HD:(hd + 1) * HD], src, gg[:, v, m:m + 1], None, ALU.mult)
                else:
                    dst = YN[:, v, span(it, P, HD * (t // 4), HD)]
                    last = vector.scalar_tensor_tensor(out=dst, in0=src, scalar=gg[:, v, m:m + 1], in1=dst, op0=ALU.mult, op1=ALU.add)
                if m == 1:
                    last.then_inc(free[6 + u], 1)

            def ret_stats(h):
                ve.wait_ge(free[4 + h % 2], FREED["ret"][4 + h % 2] + h // 2 + 1)
                for i in range(4):
                    vector.bn_stats(bn[:, 4 * h + i, :], CAT[:, i, 512 + h * P:512 + (h + 1) * P])
                vector.drain()
                for i in range(4):
                    vector.bn_aggr(mv[:, 4 * h + i, :], bn[:, 4 * h + i, :])

            def attend(kind, it, t0):
                for t in range(t0, t0 + STEPS):
                    if kind == "local" and t == 4:
                        ret_stats(3)
                        vector.drain().then_inc(gn_mv, 1)
                    if kind == "local" and t == 10:
                        ve.wait_ge(gn_sd, 1)
                        vector.reciprocal(grs[:], gsd[:]).then_inc(gn_rs, 1)
                    if kind == "da":
                        combine(it, t)
                        if exists(kind, it, t - 1):
                            low(kind, it, t - 1)
                    else:
                        out = exists(kind, it, t - 3)
                        if exists(kind, it, t - 1):
                            low(kind, it, t - 1)
                        if out:
                            take_out(kind, it, t - 3, 0)
                        factors(kind, it, t)
                        if out:
                            take_out(kind, it, t - 3, 1)
                    if exists(kind, it, t + 2):
                        maxima(kind, it, t + 2)

            def attention(kind):
                if kind != "local":
                    maxima(kind, 0, 0)
                    maxima(kind, 0, 1)
                attend_all(ve, kind, attend)
                low(kind, 0, TOTAL[kind] - 1)
                if kind != "da":
                    for t in range(TOTAL[kind] - 3, TOTAL[kind]):
                        for m in range(2):
                            vector.drain()
                            take_out(kind, 0, t, m)

            vector.memset(eps[:], EPS)
            vector.drain().then_inc(y_ready, 1)
            vector.drain().then_inc(y_ready, 1)
            vector.drain().then_inc(boot, 1)
            ve.wait_ge(in_c, 16 * 2)
            norm(0)
            for n in range(1, LEAD):
                split(n)
            for c in range(4):
                split(CHUNK0["qa"] + c + LEAD)
                ve.wait_ge(qk_hi, c + 1)
                for m in range(2):
                    own, other = slice(HD * m, HD * m + HD), slice(HD * (1 - m), HD * (1 - m) + HD)
                    head = qa[c // 2][:, 2 * (c % 2) + m, :]
                    last = vector.scalar_tensor_tensor(out=head[other, :], in0=ps[c][own, :], scalar=HD ** -0.5, in1=head[own, :],
                                                       op0=ALU.mult, op1=ALU.subtract)
                last.then_inc(free[c], 1)
            split(CHUNK0["kva"] + LEAD)
            ve.wait_ge(qk_hi, 5)
            for kv in range(2):
                for half in range(2):
                    last = vector.tensor_tensor(kal[64 * half:64 * half + 64, kv, :], ps[0][64 * kv:64 * kv + 64, :],
                                                kah[64 * kv:64 * kv + 64, kv, :], ALU.subtract)
            last.then_inc(free[0], 1)
            split(CHUNK0["kva"] + 1 + LEAD)
            ve.wait_ge(qk_hi, 6)
            vector.tensor_tensor(val[:].rearrange("p a n -> p (a n)"), ps[1][:], vah[:].rearrange("p a n -> p (a n)"),
                                 ALU.subtract).then_inc(free[1], 1)
            ve.wait_ge(in_c2, 16 * 10)
            vector.tensor_copy(identb[:], masks_f[:, 2, :])
            vector.tensor_copy(causal[:], masks_f[:, 0, :])
            vector.tensor_copy(outside[:], masks_f[:, 1, :])
            vector.tensor_scalar(nsinks[:], sinks[:], -1.0, None, ALU.mult)
            vector.tensor_tensor(lam_pr[:], lam_in[:, :, 0, :], lam_in[:, :, 1, :], ALU.mult)
            vector.tensor_scalar(gains[:, 5, :], gains[:, 5, :], 1.0 - LAM_INIT, None, ALU.mult)
            vector.drain().then_inc(boot, 1)
            vector.tensor_reduce(lam_s[:], lam_pr[:], AX.X, ALU.add).then_inc(boot2, 1)
            ve.wait_ge(boot3, 1)
            vector.tensor_tensor(nlam[:], lam_e[:, 1:2], lam_e[:, 0:1], ALU.subtract)
            vector.drain()
            vector.tensor_scalar(nlam[:], nlam[:], LAM_INIT, None, ALU.subtract)
            if on("rope_r"):
                rope("rope_r", 2, qkr, qkr, rtmp)
            if on("vg"):
                splits_t("vg")
                for tt in range(TT):
                    bank_done("vg", tt, 0)
                    vector.tensor_copy(vr[:, tt, :], ps[bank_t(tt, 0)][:]).then_inc(free[bank_t(tt, 0)], 1)
            if on("ret"):
                def decayed(h):
                    if h >= 2:
                        filled("ret", 4 + h % 2, h // 2 - 1)
                    for c in range(4):
                        filled("ret", c, h)
                        w = SEQ - c * P
                        o = [0, 512, 896, 1152][c]
                        vector.tensor_tensor(STs[h % 2][:, o:o + w], ps[c][:, 0:w], decay[:, h, 0:w], ALU.mult).then_inc(free[c], 1)

                decayed(0)
                for h in range(4):
                    if h < 3:
                        decayed(h + 1)
                    elif on("local"):
                        maxima("local", 0, 0)
                        maxima("local", 0, 1)
                    if h < 3:
                        ret_stats(h)
            if on("local"):
                attention("local")
            if on("cat"):
                to_ht("cat", HTh, HTl)
            if on("out1"):
                splits_t("out1")
                if not on("norm1"):
                    for tt in range(TT):
                        post_gain(0, tt)
                        post_add(0, tt)
            if on("norm1"):
                norm(1, lambda tt: post_gain(0, tt), lambda tt: post_add(0, tt))
            if on("up1"):
                up_conv("up1", 1)
            if on("down1"):
                down("down1", 1)
            if on("norm2"):
                norm(2, lambda tt: post_gain(1, tt), lambda tt: post_add(1, tt))
            if on("up2"):
                up_swiglu("up2", 2)
            if on("down2"):
                down("down2", 2)
                if not on("norm3"):
                    for tt in range(TT):
                        residual_plain("down2", 0.5, FT, tt)
            if on("norm3"):
                norm(3, lambda tt: residual_plain("down2", 0.5, FT, tt))
            if on("rope_dq"):
                ve.wait_ge(in_rope, 48)
                rope("rope_dq", 2, qkd, qkd, rtmp2)
                rope("rope_dk", 2, qkd, qkd, rtmp2, 8)
            if on("vda"):
                splits_t("vda")
                for tt in range(TT):
                    bank_done("vda", tt, 0)
                    vector.tensor_copy(vd[:, tt, 0:512], ps[bank_t(tt, 0)][:]).then_inc(free[bank_t(tt, 0)], 1)
            if on("da"):
                attention("da")
            if on("nsf"):
                ve.wait_ge(da_sq, 1)
                vector.tensor_reduce(hss[:], DSQ[:].rearrange("p i (h d) -> p (i h) d", d=P), AX.X, ALU.add).then_inc(da_ss, 1)
                ve.wait_ge(da_sd, 1)
                vector.reciprocal(hrs[:], hsd[:])
                vector.drain()
                for i in range(TT):
                    r = hrs[:, i * 8:(i + 1) * 8].rearrange("p (h a) -> p h a", a=1).broadcast_to((P, 8, P))
                    blk = YD[:, i, :].rearrange("p (h d) -> p h d", d=P)
                    vector.tensor_tensor(blk, blk, r, ALU.mult).then_inc(da_fin, 1)
                for c in range(4):
                    split(CHUNK0["nsf"] + c + LEAD)
                ve.wait_ge(in_rope, 80)
                for kind in range(2):
                    vector.drain()
                    filled("nsf", 4 + kind)
                    vector.tensor_tensor(rtmp3[:], ps[4 + kind][:], sin[:], ALU.mult).then_inc(free[4 + kind], 1)
                    vector.tensor_tensor(kraw[:, kind, :], kraw[:, kind, :], cos[:], ALU.mult)
                    vector.drain()
                    for g in range(2):
                        for half in range(2):
                            last = vector.tensor_tensor(ksw[64 * half:64 * half + 64, kind, g, :], kraw[64 * g:64 * g + 64, kind, :],
                                                        rtmp3[64 * g:64 * g + 64, :], ALU.add)
                    last.then_inc(roped, 1)
                vector.drain().then_inc(ks_f, 1)
            if on("nst"):
                def compression_input(kv):
                    for jp in range(2):
                        for g in range(2):
                            h = slice(64 * g, 64 * g + 64)
                            src = kcv[h, kv, :].rearrange("p (n r a) -> p r n a", r=8, a=2)
                            for part in range(2):
                                x = src[:, :, part:part + N_CMP, jp]
                                pz = posT[h, kv, 16 * part:16 * part + 16].rearrange("p (j a) -> p j a", a=2)[:, :, jp:jp + 1].broadcast_to((64, 8, N_CMP))
                                last = vector.tensor_tensor(cA[64 * jp:64 * jp + 64, kv, 8 * part:8 * part + 8, g * 31:(g + 1) * 31], x, pz, ALU.add)
                    last.then_inc(cm_a, 1)

                ve.wait_ge(in_pos, 16)
                for kv in range(2):
                    ve.wait_ge(free[kv], FREED["nst"][kv])
                    compression_input(kv)
                for c in range(3):
                    split(CHUNK0["nst"] + c + LEAD)
                ve.wait_ge(ks_hi, 1)
                vector.tensor_tensor(ksl[:].rearrange("p a g n -> p (a g n)"), ksw[:].rearrange("p a g n -> p (a g n)"),
                                     ksh[:].rearrange("p a g n -> p (a g n)"), ALU.subtract)
                for tt in range(TT):
                    ve.wait_ge(vs_hi, tt + 1)
                    vector.tensor_tensor(vsl[:, :, tt, :], ps[tt][:, 0:2 * P].rearrange("p (a n) -> p a n", a=2), vsh[:, :, tt, :],
                                         ALU.subtract).then_inc(free[tt], 1)
            if on("cmp"):
                vector.drain()
                vector.memset(hid4[:], 0.0)
                vector.memset(kcb[:], 0.0)
                vector.drain().then_inc(kcb_zero, 1)
                ve.wait_ge(free[5], FREED["cmp"][5] + 1)
                for ht in range(2):
                    src = hid[:, 1, ht, :].rearrange("p (g a n) -> p g a n", g=2, a=1).broadcast_to((P, 2, 4, N_CMP))
                    last = vector.tensor_copy(hid4[:, ht, :, :, 0:N_CMP], src)
                last.then_inc(hid_v, 1)
                vector.memset(vblk[:], 0.0)
                vector.memset(CP[:], 0.0)
                vector.drain()
                filled("cmp", 7)
                for a in range(4):
                    q = slice(32 * a, 32 * a + 32)
                    last = vector.tensor_copy(vblk[q, :, a * HD:(a + 1) * HD], ps[7][q, 0:2 * HD].rearrange("p (g d) -> p g d", g=2))
                last.then_inc(free[7], 1)
                vector.drain().then_inc(vb, 1)
            if on("rope_q"):
                rope("rope_q", 2, qn, qnr, rtmp3)
            if on("cmpa"):
                st = "cmpa"

                def wide(a):
                    return a.rearrange("p (n a) -> p n a", a=1).broadcast_to((P, 8, N_CMP))

                def cmp_shift(n):
                    u = n % 2
                    s_ = CS[:, u, :, 0:N_CMP]
                    if n >= 2:
                        vector.drain()
                    filled(st, u, n // 2)
                    vector.tensor_tensor(s_, ps[u][:, 0:2 * P].rearrange("p (h n) -> p h n", n=32)[:, :, 0:N_CMP],
                                         cmask[:, n % 4:n % 4 + 1, :].broadcast_to((P, 8, N_CMP)), ALU.add).then_inc(free[u], 1)
                    vector.drain()
                    vector.tensor_reduce(cst[:, u, 0, :], s_, AX.X, ALU.max)
                    vector.drain()
                    vector.tensor_tensor(s_, s_, wide(cst[:, u, 0, :]), ALU.subtract).then_inc(cm_s, 1)

                def cmp_weigh(n):
                    u, g, i = n % 2, n // 4, n % 4
                    s_ = CS[:, u, :, 0:N_CMP]
                    ve.wait_ge(cm_e, n + 1)
                    vector.tensor_reduce(cst[:, u, 1, :], s_, AX.X, ALU.add)
                    vector.drain()
                    vector.reciprocal(cst[:, u, 1, :], cst[:, u, 1, :])
                    vector.drain()
                    gate = gates[:, i, 24 * g:24 * g + 24].rearrange("p (h c) -> p h c", c=3)[:, :, 0]
                    vector.scalar_tensor_tensor(out=cst[:, u, 2, :], in0=gate, scalar=cvalid[:, i:i + 1], in1=cst[:, u, 1, :],
                                                op0=ALU.mult, op1=ALU.mult)
                    vector.drain()
                    if n >= 2:
                        filled(st, 4 + u, n // 2 - 1)
                    vector.tensor_tensor(CP[:, u, :, 0:N_CMP], s_, wide(cst[:, u, 2, :]), ALU.mult).then_inc(cm_p, 1)

                cmp_shift(0)
                for n in range(8):
                    if n < 7:
                        cmp_shift(n + 1)
                    cmp_weigh(n)
                vector.drain()
            if on("nsa"):
                attention("nsa")
            if on("ydat"):
                to_ht("ydat", HT2h, HT2l, lambda k: gains[:, 5, k:k + 1])
            if on("ga"):
                splits_t("ga")
            if on("gb"):
                splits_t("gb")
            if on("ynst"):
                to_ht("ynst", HTh, HTl)
            if on("pda"):
                splits_t("pda")
                for tt in range(TT):
                    for half in range(2):
                        bank_done("pda", tt, half)
                        h = slice(half * 512, (half + 1) * 512)
                        vector.tensor_tensor(GA[:, tt, h], ps[bank_t(tt, half)][:], GA[:, tt, h], ALU.mult).then_inc(free[bank_t(tt, half)], 1)
            if on("pns"):
                splits_t("pns")
                for tt in range(TT):
                    for half in range(2):
                        bank_done("pns", tt, half)
                        h = slice(half * 512, (half + 1) * 512)
                        vector.tensor_tensor(GB[:, tt, h], ps[bank_t(tt, half)][:], GB[:, tt, h], ALU.mult).then_inc(free[bank_t(tt, half)], 1)
                    if tt < TT - 1:
                        vector.drain().then_inc(gb_ready, 1)
                    else:
                        vector.drain()
                        vector.tensor_tensor(GA[:, tt, :], GA[:, tt, :], GB[:, tt, :], ALU.add).then_inc(merged_3, 1)
            if on("mt"):
                to_ht("mt", HTh, HTl)
            if on("out2"):
                splits_t("out2")
                if not on("norm4"):
                    for tt in range(TT):
                        residual_plain("out2", 1.0, KT, tt)
            if on("norm4"):
                norm(4, lambda tt: residual_plain("out2", 1.0, KT, tt))
            if on("up3"):
                up_swiglu("up3", 3)
            if on("down3"):
                down("down3", 3)
                for tt in range(TT + 1):
                    if tt < TT:
                        residual_plain("down3", 0.5, FT, tt)
                    if tt:
                        root(5, tt - 1)
                        vector.drain()
                        if tt == 1:
                            ve.wait_ge(in_post, 48)
                        vector.scalar_tensor_tensor(out=XN[:, tt - 1, :], in0=X[:, tt - 1, :], scalar=rstd[:, tt - 1:tt], in1=gpost[:],
                                                    op0=ALU.mult, op1=ALU.mult).then_inc(f_out, 1)


def constants():
    pos = np.arange(SEQ, dtype=np.float32)
    c = {}
    c["c_ident"] = np.eye(P, dtype=np.float32)
    q, k = np.arange(P)[:, None], np.arange(P)[None, :]
    masks = np.zeros((P, 3, P), np.float32)
    masks[:, 0] = np.where(k > q, NEG, 0)
    masks[:, 1] = np.where(k <= q, NEG, 0)
    masks[:, 2] = np.eye(P)
    c["c_masks"] = masks
    pr = np.zeros((P, P), np.float32)
    i = np.arange(0, P, 2)
    pr[i + 1, i] = -1
    pr[i, i + 1] = 1
    c["c_perm_r"] = pr
    pn = np.zeros((P, P), np.float32)
    for b in (0, 64):
        i = b + np.arange(32)
        pn[i + 32, i] = -1
        pn[i, i + 32] = 1
    c["c_perm_n"] = pn
    ang = (np.float32(1) / np.power(np.float32(10000), np.linspace(0, 1, 64, dtype=np.float32))).astype(np.float32)
    a = (pos[:, None] * np.repeat(ang, 2)[None]).astype(np.float32).astype(np.float64).T
    c["c_cos_r"], c["c_sin_r"] = np.cos(a).astype(np.float32), np.sin(a).astype(np.float32)
    inv = (np.float32(1) / np.power(np.float32(10000), np.arange(0, 64, 2, dtype=np.float32) / np.float32(64))).astype(np.float32)
    a = (pos[:, None] * np.tile(inv, 4)[None]).astype(np.float32).astype(np.float64).T
    c["c_cos_n"], c["c_sin_n"] = np.cos(a).astype(np.float32), np.sin(a).astype(np.float32)
    dec = np.zeros((P, 4, SEQ), np.float64)
    for h in range(4):
        lg = np.log(1 - 2.0 ** (-5 - h))
        rel = np.arange(SEQ)[None, :] - np.arange(P)[:, None]
        dec[:, h] = np.where(rel >= 0, np.exp(lg * np.maximum(rel, 0)), 0) * P ** -0.5
    c["c_decay"] = dec.astype(np.float32)
    tok = (np.arange(TT)[None, :, None] * P + np.arange(P)[:, None, None])
    end = np.arange(N_CMP)[None, None, :] * 16 + 31
    c["c_cmask"] = np.where(end <= tok, 0, NEG).astype(np.float32)
    c["c_cvalid"] = (tok[:, :, 0] >= 31).astype(np.float32)
    return c


def weight_order(inp):
    def f(w, c0, n):
        for j in range(n):
            part = w[:, c0 + j * P:min(c0 + (j + 1) * P, w.shape[1])]
            yield part

    chunks = []

    def add_f(w, c0, width=P):
        part = w[:, c0:c0 + width]
        if width < P:
            part = np.pad(part, ((0, 0), (0, P - width)))
        chunks.append(part.reshape(KT, P, P).transpose(1, 0, 2).reshape(P, CHUNK))

    def add_t(w, c0=0):
        for k in range(w.shape[0] // P):
            chunks.append(w[k * P:(k + 1) * P, c0:c0 + CHUNK])

    w = inp["w_in"][0]
    for c in (0, 128, 256, 384, 512, 640):
        add_f(w, c)
    for c in range(768, 1792, P):
        add_f(w, c)
    add_t(w, 1792)
    add_t(inp["w_out"][0])
    for j in range(FT):
        add_f(inp["w_up"][0], j * P)
        add_f(inp["w_up"][0], D_FF + j * P)
    add_t(inp["w_down"][0])
    for j in range(FT):
        add_f(inp["ffn1_w1_2"][0], j * P)
        add_f(inp["ffn1_w3_2"][0], j * P)
    add_t(inp["ffn1_w2_2"][0])
    w = inp["w_in_2"][0]
    for c in range(0, 2048, P):
        add_f(w, c)
    add_t(w, 2048)
    for c in (4096, 4224, 4352, 4608):
        add_f(w, c)
    vg = np.concatenate([w[:, 4480:4608], w[:, 4736:4864], w[:, 4864:4912]], axis=1).reshape(KT, P, VG_W)
    for c in range(3):
        part = vg[c * VG_K:(c + 1) * VG_K].transpose(1, 0, 2).reshape(P, -1)
        chunks.append(np.pad(part, ((0, 0), (0, CHUNK - part.shape[1]))))
    for c in range(3072, 4096, P):
        add_f(w, c)
    add_t(w, 4912)
    add_t(w, 5936)
    add_t(inp["w_proj_da_2"][0])
    add_t(inp["w_proj_nsa_2"][0])
    add_t(inp["w_out_2"][0])
    for j in range(FT):
        add_f(inp["ffn2_w1_2"][0], j * P)
        add_f(inp["ffn2_w3_2"][0], j * P)
    add_t(inp["ffn2_w2_2"][0])
    assert len(chunks) == N_CHUNKS
    return np.stack(chunks)


def laid_out(inp):
    a = dict(constants())
    a["x"] = inp["x"][0]
    a["w_all"] = weight_order(inp)

    def cols(v):
        return v.reshape(-1, P).T

    g = [inp["mix_pre_norm"][0], inp["ffn_pre_norm"][0], inp["ffn1_norm_2"][0], inp["mix_norm_2"][0], inp["ffn2_norm_2"][0],
         inp["da_head_norm_2"][0].reshape(-1)]
    a["gains"] = np.stack([cols(v) for v in g], axis=1)
    a["conv"] = np.stack([cols(inp["conv_w"][0][j]) for j in range(3)] + [cols(inp["conv_b"][0])], axis=2)
    a["attn_sinks"] = inp["attn_sinks"][0]
    a["da_lambda"] = inp["da_lambda_2"][0].reshape(-1)
    a["mix_post"], a["ffn_post"], a["final"] = inp["mix_post_norm"][0], inp["ffn_post_norm"][0], inp["final_norm_2"]
    pt = inp["cmp_pos_2"][0].transpose(2, 0, 1)
    a["posT"] = np.concatenate([pt, pt], axis=0)
    a["cw1"] = inp["cmp_w1_2"][0]
    w2 = inp["cmp_w2_2"][0].reshape(2, 2, P, HD).transpose(2, 0, 1, 3)
    a["w2k"] = np.repeat(w2[:, 0][:, :, None, :], 2, axis=2)
    a["w2v"] = w2[:, 1]
    return {k: np.ascontiguousarray(v) for k, v in a.items()}


STOP = None


def kernel(**inputs):
    import concourse.bacc as bacc
    from concourse.bass_utils import run_bass_kernel_spmd

    nc = bacc.Bacc("TRN2", target_bir_lowering=False, num_devices=1)
    arrays = laid_out({k: np.asarray(v) for k, v in inputs.items()})
    t = {k: nc.dram_tensor("in_" + k, v.shape, mybir.dt.from_np(v.dtype), kind="ExternalInput").ap() for k, v in arrays.items()}
    out = nc.dram_tensor("out", (SEQ, D), F32, kind="ExternalOutput").ap()
    program(nc, t, out, STOP)
    r = run_bass_kernel_spmd(nc, [{"in_" + k: v for k, v in arrays.items()}], core_ids=[0])
    return r.results[0]["out"].reshape(1, SEQ, D)
```
